# Optimizing a Trainium2 kernel written in Bass

```python
import math
import jax, jax.numpy as jnp
from jax import lax
import numpy as np

D_MODEL = 1024
BATCH = 1
SEQ = 128
DEPTH = 2
DEC_BATCH = 1
DEC_SEQ = 512
PAST_LEN = 128

GRID_W = 64
N_EVEN = (DEPTH + 1) // 2
N_ODD = DEPTH // 2
EPS = 1e-6
MIX_W = D_MODEL
FNET_W = MIX_W // 2
FNET_GROUPS = 4
FNET_GW = FNET_W // FNET_GROUPS
CONV_W = MIX_W // 2
CONV_HEADS = 8
SHORT_CONV_K = 3
EVEN_IN = FNET_W + 3 * CONV_W
SSM_INNER = 2 * D_MODEL
SSM_HEADDIM = 64
SSM_HEADS = SSM_INNER // SSM_HEADDIM
SSM_GROUPS = 8
SSM_STATE = 128
SSM_CONV_K = 3
SSM_CHUNK = 128
SSM_CONV_DIM = SSM_INNER + 2 * SSM_GROUPS * SSM_STATE
SSM_IN = SSM_INNER + SSM_CONV_DIM + 2 * SSM_HEADS
PEER_HEADS = 8
PEER_NKEYS = 128
PEER_EXPERTS = PEER_NKEYS * PEER_NKEYS
PEER_TOPK = 16
PEER_DKEY = 256
PEER_BLOCK = 128

kernel_name = "hybrid_fnet_shortconv_ssd_peer_diffusion_step"

def rmsnorm(x, w):
    xf = x.astype(jnp.float32)
    y = xf * lax.rsqrt(jnp.mean(xf * xf, axis=-1, keepdims=True) + EPS)
    return (y * w.astype(jnp.float32)).astype(x.dtype)

def dwconv_centred(u, w, grid):
    b, t, ch = u.shape
    k = w.shape[0]
    if grid:
        rows = t // GRID_W
        u = u.reshape(b * rows, GRID_W, ch)
    y = lax.conv_general_dilated(u, w[:, None, :].astype(u.dtype), window_strides=(1,),
                                 padding=((k // 2, k // 2),),
                                 dimension_numbers=("NWC", "WIO", "NWC"),
                                 feature_group_count=ch)
    return y.reshape(b, t, ch)

def fourier_mix(a):
    b, t, _ = a.shape
    g = a.astype(jnp.float32).reshape(b, t, FNET_GROUPS, FNET_GW)
    f = jnp.fft.fftn(g, axes=(1, 3), norm="ortho").real
    return f.reshape(b, t, FNET_W).astype(a.dtype)

def even_mixer(h, w_in, conv_w, w_out, grid):
    p = h @ w_in
    a, bg, cg, v = jnp.split(p, [FNET_W, FNET_W + CONV_W, FNET_W + 2 * CONV_W], axis=-1)
    ya = fourier_mix(a)
    yb = bg * dwconv_centred(cg * v, conv_w, grid)
    return jnp.concatenate([ya, yb], axis=-1) @ w_out

def segsum(a):
    t = a.shape[-1]
    x = jnp.broadcast_to(a[..., None], a.shape + (t,))
    x = jnp.where(jnp.tril(jnp.ones((t, t), bool), -1), x, 0.0)
    s = jnp.cumsum(x, axis=-2)
    return jnp.where(jnp.tril(jnp.ones((t, t), bool)), s, -jnp.inf)

def ssd_scan(x, dt, A, B, C, init):
    b, t, h, p = x.shape
    g, n, L = SSM_GROUPS, SSM_STATE, SSM_CHUNK
    r = h // g
    nc = t // L
    f32 = jnp.float32
    xdt = (x.astype(f32) * dt[..., None]).reshape(b, nc, L, g, r, p)
    dA = (dt * A).reshape(b, nc, L, g, r).transpose(0, 3, 4, 1, 2)
    Bc = B.astype(f32).reshape(b, nc, L, g, n)
    Cc = C.astype(f32).reshape(b, nc, L, g, n)
    acum = jnp.cumsum(dA, axis=-1)
    cb = jnp.einsum("bclgn,bcsgn->bgcls", Cc, Bc)
    m = cb[:, :, None] * jnp.exp(segsum(dA))
    y_diag = jnp.einsum("bgrcls,bcsgrp->bclgrp", m, xdt)
    decay_s = jnp.exp(acum[..., -1:] - acum)
    st = jnp.einsum("bclgn,bgrcl,bclgrp->bcgrpn", Bc, decay_s, xdt)
    st = jnp.concatenate([init.astype(f32).reshape(b, 1, g, r, p, n), st], axis=1)
    chunk_decay = jnp.exp(segsum(jnp.pad(acum[..., -1], ((0, 0), (0, 0), (0, 0), (1, 0)))))
    st = jnp.einsum("bgrzc,bcgrpn->bzgrpn", chunk_decay, st)
    st_in, final = st[:, :-1], st[:, -1]
    y_off = jnp.einsum("bclgn,bcgrpn,bgrcl->bclgrp", Cc, st_in, jnp.exp(acum))
    y = (y_diag + y_off).reshape(b, t, h, p)
    return y, final.reshape(b, h, p, n)

def ssd_mixer(h, w_in, conv_w, conv_b, dt_bias, a_log, d_skip, norm_w, w_out, init_f, init_b, grid):
    b, t, _ = h.shape
    f32 = jnp.float32
    proj = h @ w_in
    z = proj[..., :SSM_INNER]
    xbc = proj[..., SSM_INNER:SSM_INNER + SSM_CONV_DIM]
    dt_raw = proj[..., SSM_INNER + SSM_CONV_DIM:]
    xbc = jax.nn.silu(dwconv_centred(xbc, conv_w, grid) + conv_b)
    xs, Bm, Cm = jnp.split(xbc, [SSM_INNER, SSM_INNER + SSM_GROUPS * SSM_STATE], axis=-1)
    xs = xs.reshape(b, t, SSM_HEADS, SSM_HEADDIM)
    Bm = Bm.reshape(b, t, SSM_GROUPS, SSM_STATE)
    Cm = Cm.reshape(b, t, SSM_GROUPS, SSM_STATE)
    dt = jax.nn.softplus(dt_raw.astype(f32).reshape(b, t, 2, SSM_HEADS) + dt_bias.astype(f32))
    A = -jnp.exp(a_log.astype(f32))
    flip = lambda v: jnp.flip(v, axis=1)
    y_f, s_f = ssd_scan(xs, dt[:, :, 0], A[0], Bm, Cm, init_f)
    y_b, s_b = ssd_scan(flip(xs), flip(dt[:, :, 1]), A[1], flip(Bm), flip(Cm), init_b)
    y = y_f + flip(y_b) + xs.astype(f32) * d_skip.astype(f32)[:, None]
    y = y.reshape(b, t, SSM_INNER) * jax.nn.silu(z.astype(f32))
    y = rmsnorm(y, norm_w).astype(h.dtype)
    return y @ w_out, s_f.astype(h.dtype), s_b.astype(h.dtype)

def peer(h, w_q, sub_keys, u_tab, v_tab):
    b, t, d = h.shape
    nt = b * t
    f32 = jnp.float32
    q = (h @ w_q).reshape(nt, PEER_HEADS, 2, PEER_DKEY // 2)
    s = jnp.einsum("thzd,hzkd->thzk", q.astype(f32), sub_keys.astype(f32))
    v1, i1 = lax.top_k(s[:, :, 0], PEER_TOPK)
    v2, i2 = lax.top_k(s[:, :, 1], PEER_TOPK)
    cand = (v1[..., :, None] + v2[..., None, :]).reshape(nt, PEER_HEADS, PEER_TOPK * PEER_TOPK)
    cand_ids = (i1[..., :, None] * PEER_NKEYS + i2[..., None, :]).reshape(nt, PEER_HEADS, PEER_TOPK * PEER_TOPK)
    top_v, top_i = lax.top_k(cand, PEER_TOPK)
    ids = jnp.take_along_axis(cand_ids, top_i, axis=-1)
    gates = jax.nn.softmax(top_v, axis=-1)
    nblk = nt // PEER_BLOCK
    xb = h.reshape(nblk, PEER_BLOCK, d)
    ids_b = ids.reshape(nblk, PEER_BLOCK, PEER_HEADS * PEER_TOPK)
    g_b = gates.reshape(nblk, PEER_BLOCK, PEER_HEADS * PEER_TOPK).astype(h.dtype)

    def block(args):
        xt, it, gt = args
        u = u_tab[it]
        v = v_tab[it]
        act = jax.nn.gelu(jnp.einsum("tkd,td->tk", u, xt), approximate=False)
        return jnp.einsum("tk,tkd->td", gt * act, v)

    out = lax.map(block, (xb, ids_b, g_b))
    return out.reshape(b, t, d)

def setup_inputs(seed: int = 0) -> dict:
    key = jax.random.key(seed)
    ks = jax.random.split(key, 32)
    nrm = lambda k, shape, s=1.0: jax.random.normal(k, shape, jnp.float32) * s
    H = SSM_HEADS
    dt0 = jnp.exp(jax.random.uniform(ks[20], (N_ODD, 2, H)) * (math.log(0.1) - math.log(0.001)) + math.log(0.001))
    return {
        "x_prompt": nrm(ks[0], (BATCH, SEQ, D_MODEL)),
        "x_sample": nrm(ks[1], (DEC_BATCH, DEC_SEQ, D_MODEL)),
        "c": nrm(ks[2], (DEC_BATCH, D_MODEL)),
        "state_ssd_fwd": nrm(ks[3], (DEC_BATCH, N_ODD, H, SSM_HEADDIM, SSM_STATE), 0.1),
        "state_ssd_bwd": nrm(ks[4], (DEC_BATCH, N_ODD, H, SSM_HEADDIM, SSM_STATE), 0.1),
        "c_ctx": nrm(ks[5], (D_MODEL,)),
        "adaln_w": nrm(ks[6], (DEPTH, D_MODEL, 6 * D_MODEL), 0.5 * D_MODEL ** -0.5),
        "adaln_b": nrm(ks[7], (DEPTH, 6 * D_MODEL), 0.01),
        "norm_mix": 1.0 + nrm(ks[8], (DEPTH, D_MODEL), 0.02),
        "norm_ffn": 1.0 + nrm(ks[9], (DEPTH, D_MODEL), 0.02),
        "norm_final": 1.0 + nrm(ks[10], (D_MODEL,), 0.02),
        "even_w_in": nrm(ks[11], (N_EVEN, D_MODEL, EVEN_IN), D_MODEL ** -0.5),
        "even_conv_w": nrm(ks[12], (N_EVEN, SHORT_CONV_K, CONV_W), SHORT_CONV_K ** -0.5),
        "even_w_out": nrm(ks[13], (N_EVEN, MIX_W, D_MODEL), MIX_W ** -0.5),
        "ssd_w_in": nrm(ks[14], (N_ODD, D_MODEL, SSM_IN), D_MODEL ** -0.5),
        "ssd_conv_w": nrm(ks[15], (N_ODD, SSM_CONV_K, SSM_CONV_DIM), SSM_CONV_K ** -0.5),
        "ssd_conv_b": nrm(ks[16], (N_ODD, SSM_CONV_DIM), 0.01),
        "ssd_dt_bias": dt0 + jnp.log(-jnp.expm1(-dt0)),
        "ssd_a_log": jnp.log(jax.random.uniform(ks[17], (N_ODD, 2, H), minval=1.0, maxval=16.0)),
        "ssd_d": 1.0 + nrm(ks[18], (N_ODD, H), 0.1),
        "ssd_norm_w": 1.0 + nrm(ks[19], (N_ODD, SSM_INNER), 0.02),
        "ssd_w_out": nrm(ks[21], (N_ODD, SSM_INNER, D_MODEL), SSM_INNER ** -0.5),
        "peer_w_q": nrm(ks[22], (DEPTH, D_MODEL, PEER_HEADS * PEER_DKEY), D_MODEL ** -0.5),
        "peer_keys": nrm(ks[23], (DEPTH, PEER_HEADS, 2, PEER_NKEYS, PEER_DKEY // 2), (PEER_DKEY // 2) ** -0.5),
        "peer_u": nrm(ks[24], (DEPTH, PEER_EXPERTS, D_MODEL), D_MODEL ** -0.5),
        "peer_v": nrm(ks[25], (DEPTH, PEER_EXPERTS, D_MODEL)),
    }

def reference(x_prompt, x_sample, c, state_ssd_fwd, state_ssd_bwd, c_ctx,
              adaln_w, adaln_b, norm_mix, norm_ffn, norm_final,
              even_w_in, even_conv_w, even_w_out,
              ssd_w_in, ssd_conv_w, ssd_conv_b, ssd_dt_bias, ssd_a_log, ssd_d, ssd_norm_w, ssd_w_out,
              peer_w_q, peer_keys, peer_u, peer_v):

    def stream(x, cond, init_f, init_b, grid):
        finals_f, finals_b = [], []
        for i in range(DEPTH):
            j = i // 2
            mod = (jax.nn.silu(cond) @ adaln_w[i] + adaln_b[i])[:, None, :]
            sh1, sc1, g1, sh2, sc2, g2 = jnp.split(mod, 6, axis=-1)
            hn = rmsnorm(x, norm_mix[i]) * (1 + sc1) + sh1
            if i % 2 == 0:
                m = even_mixer(hn, even_w_in[j], even_conv_w[j], even_w_out[j], grid)
            else:
                m, s_f, s_b = ssd_mixer(hn, ssd_w_in[j], ssd_conv_w[j], ssd_conv_b[j], ssd_dt_bias[j],
                                        ssd_a_log[j], ssd_d[j], ssd_norm_w[j], ssd_w_out[j],
                                        init_f[:, j], init_b[:, j], grid)
                finals_f.append(s_f)
                finals_b.append(s_b)
            x = x + g1 * m
            hn = rmsnorm(x, norm_ffn[i]) * (1 + sc2) + sh2
            x = x + g2 * peer(hn, peer_w_q[i], peer_keys[i], peer_u[i], peer_v[i])
        return rmsnorm(x, norm_final), finals_f, finals_b

    zero_state = jnp.zeros((x_prompt.shape[0], N_ODD, SSM_HEADS, SSM_HEADDIM, SSM_STATE), x_prompt.dtype)
    y_prompt, ctx_f, ctx_b = stream(x_prompt, c_ctx[None, :], zero_state, zero_state, False)
    new_state_ssd_fwd = jnp.stack(ctx_f, axis=1)
    new_state_ssd_bwd = jnp.stack(ctx_b, axis=1)
    y_sample, _, _ = stream(x_sample, c, state_ssd_fwd, state_ssd_bwd, True)
    return (y_prompt, y_sample, new_state_ssd_fwd, new_state_ssd_bwd)


_drawn_inputs = setup_inputs


def setup_inputs(seed=0):
    import zlib

    import numpy as np

    out = dict(_drawn_inputs(seed))
    spreads = {}
    factors = {'norm_final': 2.906, 'ssd_conv_b': 3.817, 'ssd_d': 2.673, 'ssd_norm_w': 4.387}
    for name, (base, spread) in spreads.items():
        noise = np.random.default_rng([zlib.crc32(name.encode()), seed]).standard_normal(out[name].shape)
        drawn = base * np.exp(spread * noise) if base else spread * noise
        out[name] = __import__('jax').numpy.asarray(drawn.astype(out[name].dtype))
    for name, factor in factors.items():
        out[name] = (out[name] * factor).astype(out[name].dtype)
    return out
```

```python
import concourse.bass as bass
from concourse import mybir
from contextlib import ExitStack, contextmanager

F32 = mybir.dt.float32
U32 = mybir.dt.uint32
ALU = mybir.AluOpType
ACT = mybir.ActivationFunctionType
AX = mybir.AxisListType

P = 128
D_MODEL = 1024
NCH = D_MODEL // P
SAMPLE, PROMPT = 512, 128
TOK = SAMPLE + PROMPT
TILES = TOK // P
SAMPLE_TILES = SAMPLE // P
DEPTH = 2
GRID_W = 64
EPS = 1e-6
MODS = 6
EVEN_IN = 2048
GROUPS = 4
SSM_INNER = 2048
HEADS = 32
SSM_GROUPS = 8
HPG = HEADS // SSM_GROUPS
HEADDIM = 64
GW = HPG * HEADDIM
PEER_HEADS = 8
TOPK = 16
ENTRIES = PEER_HEADS * TOPK
KEYS = 128
EXPERT_BLOCKS = 128
BLOCKS_PER_GROUP = 4
SLOTS = 8
NEG = -3.0e38
SH1, SC1, G1, SH2, SC2, G2 = range(MODS)

N_ADALN = MODS * NCH
N_EVEN_IN = EVEN_IN // P
N_EVEN_OUT = NCH
N_WQ = 2048 // P
N_PEER = 2 * EXPERT_BLOCKS
N_SSD = 4 * SSM_GROUPS
N_Z = 16
N_SSD_OUT = 2 * NCH

PAIRS_OF = [TOPK // (i + 1) for i in range(TOPK)]
PAIR_AT = [sum(PAIRS_OF[:i]) for i in range(TOPK)]
PAIRS = sum(PAIRS_OF)

COL_SIZES = [("cond", NCH * 2), ("adaln_b", DEPTH * N_ADALN), ("norm_mix", DEPTH * NCH),
             ("norm_ffn", DEPTH * NCH), ("norm_final", NCH), ("even_conv_w", 12), ("ssd_conv_w", 96),
             ("ssd_conv_b", 32), ("ssd_norm_w", 16)]
COL_AT, NCOLS = {}, 0
for _name, _n in COL_SIZES:
    COL_AT[_name] = (NCOLS, _n)
    NCOLS += _n
ROW_SIZES = [("dt_bias", 64), ("a_log", 64), ("d", 32), ("iota", 128), ("rank", TOPK), ("pair_at", TOPK),
             ("pairs_before", TOPK)]
ROW_AT, NROWS = {}, 0
for _name, _n in ROW_SIZES:
    ROW_AT[_name] = (NROWS, _n)
    NROWS += _n
LE, LT, GE, GT, ONES, IDENT = range(6)


class Steps:

    def __init__(self, sem):
        self.sem, self.base, self.k = sem, 0, 0

    def did(self, ins):
        self.k += 1
        return ins.then_inc(self.sem, 1)

    def settle(self, eng):
        eng.wait_ge(self.sem, self.base + self.k)

    @contextmanager
    def loop(self, eng, n, per):
        start = self.base + self.k
        with eng.Fori(0, n) as i:
            self.base, self.k = i * per + start, 0
            yield i
            assert self.k == per, (self.k, per)
        self.base, self.k = start + n * per, 0


def bcast(ap, axis, n):
    v = ap.unsqueeze(axis)
    shape = list(v.shape)
    shape[axis] = n
    return v.broadcast_to(shape)


def hybrid_trunk(nc, stream, keys, wdt, xin, cols_d, rows_d, masks_d, dft_d, state_in, y_out, state_out,
                 gates_dram):
    ctx = ExitStack()
    with ctx:
        def sb(name, shape, dt=F32, into=ctx):
            return into.enter_context(nc.sbuf_tensor(name, shape, dt))

        def pb(name, cols=512, into=ctx):
            return into.enter_context(nc.psum_tensor(name, [P, cols], F32))

        def sem(name, into=ctx):
            return ctx.enter_context(nc.semaphore(name))

        xT = sb("xT", [P, NCH, TOK])
        hT = sb("hT", [P, NCH, TOK])
        ring = sb("ring", [P, SLOTS, 1024])
        cols = sb("cols", [P, NCOLS])
        rows = sb("rows", [P, NROWS])
        masks = sb("masks", [P, 6, P])
        mods = sb("mods", [P, N_ADALN, 2])
        scale_mix = sb("scale_mix", [P, NCH, 2])
        scale_ffn = sb("scale_ffn", [P, NCH, 2])
        scond = sb("scond", [P, NCH, 2])
        eps = sb("eps", [P, 1])
        zero = sb("zero", [P, 1])

        def col(name, a=0, b=None):
            at, n = COL_AT[name]
            return cols[:, at + a:at + (n if b is None else b)]

        def row(name):
            at, n = ROW_AT[name]
            return rows[:, at:at + n]

        slot_loaded = [sem(f"slot_loaded{s}") for s in range(SLOTS)]
        blocks_used = sem("blocks_used")
        consts_loaded = sem("consts_loaded")
        x_loaded = sem("x_loaded")
        dve_steps = Steps(sem("dve_steps"))
        act_steps = Steps(sem("act_steps"))
        pool_steps = Steps(sem("pool_steps"))
        at = [0]

        def take(n):
            first = at[0]
            at[0] += n
            return first

        def feed(sp, first, n):
            last = min(first + n + SLOTS, N_BLOCKS) - SLOTS
            if last == first:
                return
            with sp.Fori(0, (last - first) // SLOTS) as i:
                for s in range(SLOTS):
                    sp.wait_ge(blocks_used, i * SLOTS + (first + s + 1))
                    sp.dma_start(ring[:, s, :], stream[i * SLOTS + (first + SLOTS + s)]).then_inc(slot_loaded[s], 16)

        def loaded(pe, s, round_):
            pe.wait_ge(slot_loaded[s], round_ * 16 + 16)

        N_BLOCKS = stream.shape[0]

        def pair_matmul(out_s, out_p, lhsT, rhs, c, start, stop):
            nc.tensor.matmul(out_s, lhsT=lhsT, rhs=rhs[:, c, 0:SAMPLE], start=start, stop=stop)
            return nc.tensor.matmul(out_p, lhsT=lhsT, rhs=rhs[:, c, SAMPLE:TOK], start=start, stop=stop)

        def norm_modulate(tag, dst, scale, shift):
            with ExitStack() as ph:
                sq = sb(f"sq{tag}", [P, 2, TOK], into=ph)
                rms = sb(f"rms{tag}", [P, TOK], into=ph)
                sum_s, sum_p = pb(f"sums{tag}", into=ph), pb(f"sump{tag}", into=ph)
                squared, summed, rooted, scaled = (sem(f"{n}_{tag}") for n in ("squared", "summed", "rooted", "scaled"))
                with nc.Block() as block:
                    @block.scalar
                    def _(act):
                        for c in range(NCH):
                            if c >= 2:
                                act.wait_ge(summed, c - 1)
                            nc.scalar.activation(sq[:, c % 2, :], xT[:, c, :], ACT.Square).then_inc(squared, 1)
                        act.wait_ge(summed, NCH)
                        nc.scalar.activation(rms[:, 0:SAMPLE], sum_s[:, :], ACT.Sqrt, bias=eps[:, :],
                                             scale=1.0 / D_MODEL).then_inc(rooted, 1)
                        nc.scalar.activation(rms[:, SAMPLE:TOK], sum_p[:, 0:PROMPT], ACT.Sqrt, bias=eps[:, :],
                                             scale=1.0 / D_MODEL).then_inc(rooted, 1)
                        for c in range(NCH):
                            act.wait_ge(scaled, c + 1)
                            for k, part in ((0, slice(0, SAMPLE)), (1, slice(SAMPLE, TOK))):
                                nc.scalar.activation(dst[:, c, part], dst[:, c, part], ACT.Identity,
                                                     scale=scale(c, k), bias=shift(c, k) if shift else 0.0)

                    @block.tensor
                    def _(pe):
                        for c in range(NCH):
                            pe.wait_ge(squared, c + 1)
                            nc.tensor.matmul(sum_s[:, :], lhsT=masks[:, ONES, :], rhs=sq[:, c % 2, 0:SAMPLE],
                                             start=c == 0, stop=c == NCH - 1)
                            nc.tensor.matmul(sum_p[:, 0:PROMPT], lhsT=masks[:, ONES, :], rhs=sq[:, c % 2, SAMPLE:TOK],
                                             start=c == 0, stop=c == NCH - 1).then_inc(summed, 1)

                    @block.vector
                    def _(dve):
                        dve.wait_ge(rooted, 2)
                        dve_steps.did(nc.vector.reciprocal(rms[:, :], rms[:, :]))
                        dve_steps.settle(dve)
                        for c in range(NCH):
                            nc.vector.tensor_tensor(dst[:, c, :], xT[:, c, :], rms[:, :], ALU.mult).then_inc(scaled, 1)

        def adaln(layer):
            tag = f"ada{layer}"
            first = take(N_ADALN)
            with ExitStack() as ph:
                ps = pb(f"ps{tag}", into=ph)
                silu_done = sem(f"silu_done{layer}")
                with nc.Block() as block:
                    @block.sync
                    def _(sp):
                        feed(sp, first, N_ADALN)

                    @block.scalar
                    def _(act):
                        nc.scalar.activation(scond[:, :, :], col("cond").rearrange("p (c k) -> p c k", k=2),
                                             ACT.Silu).then_inc(silu_done, 1)

                    @block.tensor
                    def _(pe):
                        pe.wait_ge(silu_done, 1)
                        with pe.Fori(0, N_ADALN // SLOTS) as i:
                            for s in range(SLOTS):
                                loaded(pe, s, i + first // SLOTS)
                                for c in range(NCH):
                                    last = nc.tensor.matmul(ps[:, bass.ds(i * 2 * SLOTS + 2 * s, 2)],
                                                            lhsT=ring[:, s, c * P:(c + 1) * P], rhs=scond[:, c, :],
                                                            start=c == 0, stop=c == NCH - 1)
                                last.then_inc(blocks_used, 1)

                    @block.vector
                    def _(dve):
                        dve.wait_ge(blocks_used, first + N_ADALN)
                        bias = col("adaln_b", layer * N_ADALN, (layer + 1) * N_ADALN)
                        dve_steps.did(nc.vector.tensor_tensor(
                            mods[:, :, :], ps[:, 0:2 * N_ADALN].rearrange("p (m k) -> p m k", k=2),
                            bcast(bias, 2, 2), ALU.add))
                        dve_steps.settle(dve)
                        for dst, comp, w in ((scale_mix, SC1, "norm_mix"), (scale_ffn, SC2, "norm_ffn")):
                            nc.vector.scalar_tensor_tensor(
                                dst[:, :, :], in0=mods[:, comp * NCH:(comp + 1) * NCH, :], scalar=1.0,
                                in1=bcast(col(w, layer * NCH, (layer + 1) * NCH), 2, 2), op0=ALU.add, op1=ALU.mult)

        def project(tag, n_blocks, rhs, evacuate, per_steps=0, dve_evac=False, chunks=NCH):
            first = take(n_blocks)
            each = chunks // NCH
            per_round = SLOTS // each
            with ExitStack() as ph:
                ps = [pb(f"ps{tag}{j}", into=ph) for j in range(2)]
                pp = [pb(f"pp{tag}{j}", into=ph) for j in range(2)]
                pair_free = sem(f"pair_free_{tag}")
                with nc.Block() as block:
                    @block.sync
                    def _(sp):
                        feed(sp, first, n_blocks)

                    @block.tensor
                    def _(pe):
                        with pe.Fori(0, n_blocks // SLOTS) as i:
                            for o in range(per_round):
                                pe.wait_ge(pair_free, i * per_round + (o + 1))
                                for s in range(o * each, (o + 1) * each):
                                    loaded(pe, s, i + first // SLOTS)
                                    for c in range(NCH):
                                        cc = (s - o * each) * NCH + c
                                        last = pair_matmul(ps[o % 2][:, :], pp[o % 2][:, 0:PROMPT],
                                                           ring[:, s, c * P:(c + 1) * P], rhs, cc,
                                                           cc == 0, cc == chunks - 1)
                                    last.then_inc(blocks_used, 1)

                    def evac(eng, steps):
                        eng.sem_inc(pair_free, 2)
                        with steps.loop(eng, n_blocks // SLOTS, per_steps) as i:
                            for o in range(per_round):
                                eng.wait_ge(blocks_used, i * SLOTS + (first + (o + 1) * each))
                                evacuate(eng, i * per_round + o, ps[o % 2][:, :], pp[o % 2][:, 0:PROMPT]).then_inc(pair_free, 1)

                    if dve_evac:
                        @block.vector
                        def _(dve):
                            evac(dve, dve_steps)
                    else:
                        @block.scalar
                        def _(act):
                            evac(act, act_steps)

        def copy_into(dst):
            def f(act, m, s, p):
                nc.scalar.activation(dst[:, bass.ds(m, 1), 0:SAMPLE].rearrange("p a t -> p (a t)"), s, ACT.Copy)
                return nc.scalar.activation(dst[:, bass.ds(m, 1), SAMPLE:TOK].rearrange("p a t -> p (a t)"), p, ACT.Copy)
            return f

        def add_gated(gate):
            def f(dve, m, s, p):
                for k, src, a, b in ((0, s, 0, SAMPLE), (1, p, SAMPLE, TOK)):
                    x = xT[:, bass.ds(m, 1), a:b].rearrange("p a t -> p (a t)")
                    last = nc.vector.scalar_tensor_tensor(
                        x, in0=src, scalar=mods[:, bass.ds(m + gate * NCH, 1), k:k + 1].rearrange("p a k -> p (a k)"),
                        in1=x, op0=ALU.mult, op1=ALU.add)
                return last
            return f

        with nc.Block() as block:
            @block.sync
            def _(sp):
                sp.dma_start(cols[:, :], cols_d).then_inc(consts_loaded, 16)
                sp.dma_start(rows[:, :], rows_d).then_inc(consts_loaded, 16)
                sp.dma_start(masks[:, :, :], masks_d).then_inc(consts_loaded, 16)
                for s in range(SLOTS):
                    sp.dma_start(ring[:, s, :], stream[s]).then_inc(slot_loaded[s], 16)
                sp.dma_start(xT[:, :, :], xin).then_inc(x_loaded, 16)
                sp.wait_ge(consts_loaded, 48)
                sp.wait_ge(x_loaded, 16)

            @block.vector
            def _(dve):
                nc.vector.memset(eps[:, :], EPS)

        def even_mixer():
            with ExitStack() as ph:
                pT = sb("pT", [P, N_EVEN_IN, TOK], into=ph)
                dft = sb("dft", [P, 2 * SAMPLE_TILES * SAMPLE + 4 * P], into=ph)
                dft_loaded = sem("dft_loaded")
                cos_t = dft[:, 0:2048].rearrange("p (t u) -> p t u", u=SAMPLE)
                sin_t = dft[:, 2048:4096].rearrange("p (t u) -> p t u", u=SAMPLE)
                both_c = dft[:, 4096:4096 + 256]
                cos_p, sin_p = dft[:, 4352:4480], dft[:, 4480:4608]
                project("even_in", N_EVEN_IN, hT, copy_into(pT))
                by_c = sb("by_c", [P, TILES, GROUPS, 2 * P], into=ph)
                PADDED = 8 * (GRID_W + 2) + PROMPT + 2
                upad = sb("upad", [P, 2, PADDED], into=ph)
                conv = sb("conv", [P, 2, PADDED], into=ph)
                banks = ExitStack()
                pc = [pb(f"pc{j}", into=banks) for j in range(2)]
                pf = [pb(f"pf{j}", into=banks) for j in range(2)]
                pfp = [pb(f"pfp{j}", into=banks) for j in range(2)]
                chan_done, chan_used, pos_done, pos_free = (sem(n) for n in ("chan_done", "chan_used", "pos_done", "pos_free"))
                with nc.Block() as block:
                    @block.sync
                    def _(sp):
                        sp.dma_start(dft[:, :], dft_d).then_inc(dft_loaded, 16)

                    @block.tensor
                    def _(pe):
                        pe.wait_ge(dft_loaded, 16)
                        n = 0
                        for t in range(TILES):
                            for g in range(0, GROUPS, 2):
                                if n >= 2:
                                    pe.wait_ge(chan_used, n - 1)
                                for k in range(2):
                                    last = nc.tensor.matmul(pc[n % 2][:, 256 * k:256 * k + 256],
                                                            lhsT=pT[:, g + k, t * P:(t + 1) * P], rhs=both_c,
                                                            start=True, stop=True)
                                last.then_inc(chan_done, 1)
                                n += 1
                        pe.wait_ge(chan_used, n)
                        for g in range(GROUPS):
                            if g >= 2:
                                pe.wait_ge(pos_free, g - 1)
                            for t in range(SAMPLE_TILES):
                                nc.tensor.matmul(pf[g % 2][:, :], lhsT=by_c[:, t, g, 0:P], rhs=cos_t[:, t, :],
                                                 start=t == 0, stop=False)
                                nc.tensor.matmul(pf[g % 2][:, :], lhsT=by_c[:, t, g, P:2 * P], rhs=sin_t[:, t, :],
                                                 start=False, stop=t == SAMPLE_TILES - 1)
                            nc.tensor.matmul(pfp[g % 2][:, 0:P], lhsT=by_c[:, SAMPLE_TILES, g, 0:P], rhs=cos_p,
                                             start=True, stop=False)
                            nc.tensor.matmul(pfp[g % 2][:, 0:P], lhsT=by_c[:, SAMPLE_TILES, g, P:2 * P], rhs=sin_p,
                                             start=False, stop=True).then_inc(pos_done, 1)

                    @block.scalar
                    def _(act):
                        n = 0
                        for t in range(TILES):
                            for g in range(0, GROUPS, 2):
                                act.wait_ge(chan_done, n + 1)
                                nc.scalar.activation(by_c[:, t, g:g + 2, :].rearrange("p g c -> p (g c)"), pc[n % 2][:, :],
                                                     ACT.Copy).then_inc(chan_used, 1)
                                n += 1
                        for g in range(GROUPS):
                            act.wait_ge(pos_done, g + 1)
                            nc.scalar.activation(pT[:, g, 0:SAMPLE], pf[g % 2][:, :], ACT.Copy)
                            nc.scalar.activation(pT[:, g, SAMPLE:TOK], pfp[g % 2][:, 0:P], ACT.Copy).then_inc(pos_free, 1)

                    @block.vector
                    def _(dve):
                        dve_steps.did(nc.vector.memset(upad[:, :, :], 0.0))
                        dve_steps.settle(dve)
                        for j in range(4):
                            u, v = upad[:, j % 2, :], conv[:, j % 2, :]
                            us = grid(u)
                            dve_steps.did(nc.vector.tensor_tensor(
                                us, pT[:, 8 + j, 0:SAMPLE].rearrange("p (r w) -> p r w", w=GRID_W),
                                pT[:, 12 + j, 0:SAMPLE].rearrange("p (r w) -> p r w", w=GRID_W), ALU.mult))
                            dve_steps.did(nc.vector.tensor_tensor(row_p(u), pT[:, 8 + j, SAMPLE:TOK],
                                                                  pT[:, 12 + j, SAMPLE:TOK], ALU.mult))
                            dve_steps.settle(dve)
                            conv3(dve, v, u, lambda k: col("even_conv_w", 3 * j + k, 3 * j + k + 1))
                            for dst, src in ((pT[:, 4 + j, 0:SAMPLE].rearrange("p (r w) -> p r w", w=GRID_W), grid(v)),
                                             (pT[:, 4 + j, SAMPLE:TOK], row_p(v))):
                                dve_steps.did(nc.vector.tensor_tensor(dst, dst, src, ALU.mult))
                banks.close()
                project("even_out", N_EVEN_OUT, pT, add_gated(G1), dve_evac=True)

        def grid(u):
            return u[:, 0:8 * (GRID_W + 2)].rearrange("p (r w) -> p r w", w=GRID_W + 2)[:, :, 1:GRID_W + 1]

        def row_p(u):
            return u[:, 8 * (GRID_W + 2) + 1:8 * (GRID_W + 2) + 1 + PROMPT]

        def conv3(dve, v, u, w):
            n = 8 * (GRID_W + 2) + PROMPT + 2
            dve_steps.did(nc.vector.tensor_scalar(v[:, 1:n - 1], u[:, 1:n - 1], w(1), None, ALU.mult))
            for k, shift in ((0, 0), (2, 2)):
                dve_steps.settle(dve)
                dve_steps.did(nc.vector.scalar_tensor_tensor(v[:, 1:n - 1], in0=u[:, shift:n - 2 + shift], scalar=w(k),
                                                             in1=v[:, 1:n - 1], op0=ALU.mult, op1=ALU.add))
            dve_steps.settle(dve)

        def peer(layer):
            tag = f"_p{layer}"
            with ExitStack() as ids_life:
                idT = sb(f"idT{tag}", [P, 3, TOK], into=ids_life)
                with ExitStack() as ph:
                    qT = sb(f"qT{tag}", [P, N_WQ, TOK], into=ph)
                    keysT = sb(f"keysT{tag}", [P, 2 * PEER_HEADS * KEYS], into=ph)
                    project(f"q{layer}", N_WQ, hT, copy_into(qT))
                    top_keys(layer, tag, ph, qT, keysT, idT)
                scatter_gates(layer, tag, idT)
            experts(layer, tag)

        def top_keys(layer, tag, ph, qT, keysT, idT):
            H2 = 2 * PEER_HEADS
            sc = sb(f"sc{tag}", [P, H2, KEYS], into=ph)
            best = sb(f"best{tag}", [P, H2, TOPK], into=ph)
            besti = sb(f"besti{tag}", [P, H2, TOPK], U32, into=ph)
            bestf = sb(f"bestf{tag}", [P, H2, TOPK], into=ph)
            idstep = sb(f"idstep{tag}", [P, H2, TOPK], into=ph)
            cand = sb(f"cand{tag}", [P, PEER_HEADS, PAIRS], into=ph)
            top = sb(f"top{tag}", [P, PEER_HEADS, TOPK], into=ph)
            posi = sb(f"posi{tag}", [P, PEER_HEADS, TOPK], U32, into=ph)
            posf = sb(f"posf{tag}", [P, ENTRIES], into=ph)
            start_of = sb(f"start_of{tag}", [P, ENTRIES], into=ph)
            passed = sb(f"passed{tag}", [P, ENTRIES, TOPK], into=ph)
            prod = sb(f"prod{tag}", [P, ENTRIES, TOPK], into=ph)
            found = sb(f"found{tag}", [P, 3, ENTRIES], into=ph)
            total = sb(f"total{tag}", [P, PEER_HEADS], into=ph)
            ps = [pb(f"pk{tag}{j}", into=ph) for j in range(4)]
            pt = pb(f"pt{tag}", into=ph)
            batches_begun = sem(f"batches_begun{tag}")
            (keys_loaded, scores_done, scores_copied, sc_free, exp_in, exp_out, found_ready, turned, turned_out) = (
                sem(f"{n}{tag}") for n in ("keys_loaded", "scores_done", "scores_copied", "sc_free", "exp_in",
                                           "exp_out", "found_ready", "turned", "turned_out"))
            with nc.Block() as block:
                @block.sync
                def _(sp):
                    sp.dma_start(keysT[:, :], keys[layer]).then_inc(keys_loaded, 16)

                @block.tensor
                def _(pe):
                    pe.wait_ge(keys_loaded, 16)
                    def turn(t):
                        pe.wait_ge(found_ready, t + 1)
                        if t >= 1:
                            pe.wait_ge(turned_out, t)
                        for k in range(3):
                            last = nc.tensor.transpose(pt[:, k * P:(k + 1) * P], found[:, k, :], masks[:, IDENT, :])
                        last.then_inc(turned, 1)

                    for t in range(TILES):
                        for b in range(4):
                            if t:
                                pe.wait_ge(scores_copied, 4 * (t - 1) + b + 1)
                            for q in range(4):
                                hz = 4 * b + q
                                last = nc.tensor.matmul(ps[b][:, q * KEYS:(q + 1) * KEYS],
                                                        lhsT=qT[:, hz, t * P:(t + 1) * P],
                                                        rhs=keysT[:, hz * KEYS:(hz + 1) * KEYS], start=True, stop=True)
                            last.then_inc(scores_done, 1)
                        if t:
                            turn(t - 1)
                    turn(TILES - 1)

                @block.scalar
                def _(act):
                    with act.Fori(0, TILES) as t:
                        act.wait_ge(sc_free, t + 1)
                        for b in range(4):
                            act.wait_ge(scores_done, t * 4 + (b + 1))
                            nc.scalar.activation(sc[:, 4 * b:4 * b + 4, :].rearrange("p h k -> p (h k)"), ps[b][:, :],
                                                 ACT.Copy).then_inc(scores_copied, 1)
                        act.wait_ge(exp_in, t + 1)
                        nc.scalar.activation(found[:, 2, :], found[:, 2, :], ACT.Exp).then_inc(exp_out, 1)
                        act.wait_ge(turned, t + 2)
                        nc.scalar.activation(idT[:, :, bass.ds(t * P, P)], pt[:, 0:3 * P].rearrange("p (k n) -> p k n", k=3),
                                             ACT.Copy).then_inc(turned_out, 1)

                @block.vector
                def _(dve):
                    v = nc.vector

                    def best8(ins_of, n):
                        dve_steps.settle(dve)
                        dve.sem_inc(batches_begun, 1)
                        for j in range(n):
                            dve_steps.did(ins_of(j))

                    dve.sem_inc(sc_free, 1)
                    dve.sem_inc(turned, 1)
                    H = PEER_HEADS
                    steps = 5 * H2 + 2 + 9 + 5 * H + 12
                    with dve_steps.loop(dve, TILES, steps) as t:
                        dve.wait_ge(scores_copied, t * 4 + 4)
                        best8(lambda j: v.max(best[:, j, 0:8], sc[:, j, :]), H2)
                        best8(lambda j: v.max_index(besti[:, j, 0:8], best[:, j, 0:8], sc[:, j, :]), H2)
                        best8(lambda j: v.match_replace(sc[:, j, :], best[:, j, 0:8], sc[:, j, :], NEG), H2)
                        best8(lambda j: v.max(best[:, j, 8:16], sc[:, j, :]), H2)
                        best8(lambda j: v.max_index(besti[:, j, 8:16], best[:, j, 8:16], sc[:, j, :]), H2)
                        dve_steps.settle(dve)
                        v.tensor_copy(bestf[:, :, :], besti[:, :, :]).then_inc(sc_free, 1)
                        dve.wait_ge(sc_free, t + 2)
                        dve_steps.did(v.tensor_copy(idstep[:, :, 0:1], bestf[:, :, 0:1]))
                        dve_steps.did(v.tensor_tensor(idstep[:, :, 1:TOPK], bestf[:, :, 1:TOPK], bestf[:, :, 0:TOPK - 1],
                                                      ALU.subtract))
                        bz = best[:, :, :].rearrange("p (h z) k -> p h z k", z=2)
                        for i in range(8):
                            n = PAIRS_OF[i]
                            dve_steps.did(v.tensor_tensor(
                                cand[:, :, PAIR_AT[i]:PAIR_AT[i] + n],
                                bz[:, :, 0, i:i + 1].broadcast_to([P, H, n]), bz[:, :, 1, 0:n], ALU.add))
                        dve_steps.did(v.tensor_tensor(cand[:, :, PAIR_AT[8]:PAIRS], bz[:, :, 0, 8:16],
                                                      bz[:, :, 1, 0:1].broadcast_to([P, H, 8]), ALU.add))
                        best8(lambda j: v.max(top[:, j, 0:8], cand[:, j, :]), H)
                        best8(lambda j: v.max_index(posi[:, j, 0:8], top[:, j, 0:8], cand[:, j, :]), H)
                        best8(lambda j: v.match_replace(cand[:, j, :], top[:, j, 0:8], cand[:, j, :], NEG), H)
                        best8(lambda j: v.max(top[:, j, 8:16], cand[:, j, :]), H)
                        best8(lambda j: v.max_index(posi[:, j, 8:16], top[:, j, 8:16], cand[:, j, :]), H)
                        dve_steps.settle(dve)
                        dve.wait_ge(turned, t + 1)
                        f3 = lambda k: found[:, k, :].rearrange("p (h r) -> p h r", h=H)
                        dve_steps.did(v.tensor_copy(posf[:, :].rearrange("p (h r) -> p h r", h=H), posi[:, :, :]))
                        v.tensor_tensor(f3(2), top[:, :, :], top[:, :, 0:1].broadcast_to([P, H, TOPK]),
                                        ALU.subtract).then_inc(exp_in, 1)

                        def ranks(table):
                            return bcast(table, 1, ENTRIES)

                        def lookup(dst, steps_of):
                            dve_steps.settle(dve)
                            dve_steps.did(v.tensor_tensor(
                                prod[:, :, :].rearrange("p (h r) m -> p h r m", h=H),
                                passed[:, :, :].rearrange("p (h r) m -> p h r m", h=H), steps_of, ALU.mult))
                            dve_steps.settle(dve)
                            dve_steps.did(v.tensor_reduce(dst, prod[:, :, :], AX.X, ALU.add))

                        dve_steps.settle(dve)
                        dve_steps.did(v.tensor_tensor(passed[:, :, :], bcast(posf[:, :], 2, TOPK), ranks(row("pair_at")), ALU.is_ge))
                        lookup(start_of[:, :], bcast(bcast(row("pairs_before"), 1, TOPK), 1, H))
                        iz = idstep[:, :, :].rearrange("p (h z) k -> p h z k", z=2)
                        lookup(found[:, 0, :], bcast(iz[:, :, 0, :], 2, TOPK))
                        dve_steps.settle(dve)
                        dve_steps.did(v.tensor_tensor(posf[:, :], posf[:, :], start_of[:, :], ALU.subtract))
                        dve_steps.settle(dve)
                        dve_steps.did(v.tensor_tensor(passed[:, :, :], bcast(posf[:, :], 2, TOPK), ranks(row("rank")), ALU.is_ge))
                        lookup(found[:, 1, :], bcast(iz[:, :, 1, :], 2, TOPK))
                        dve.wait_ge(exp_out, t + 1)
                        dve_steps.did(v.tensor_reduce(total[:, :], f3(2), AX.X, ALU.add))
                        dve_steps.settle(dve)
                        dve_steps.did(v.reciprocal(total[:, :], total[:, :]))
                        dve_steps.settle(dve)
                        v.tensor_tensor(f3(2), f3(2), bcast(total[:, :], 2, TOPK), ALU.mult).then_inc(found_ready, 1)

        def scatter_gates(layer, tag, idT):
            HALF = 8
            with ExitStack() as ph:
                staged = sb(f"staged{tag}", [P, KEYS, P], into=ph)
                hot1 = sb(f"hot1{tag}", [P, 2 * HALF, KEYS], into=ph)
                hot2 = sb(f"hot2{tag}", [P, 2 * HALF, KEYS], into=ph)
                ps = [pb(f"pg{tag}{j}", into=ph) for j in range(4)]
                hots_ready, hots_used, g_copied, staged_full, staged_free = (
                    sem(f"{n}{tag}") for n in ("hots_ready", "hots_used", "g_copied", "staged_full", "staged_free"))
                ROUNDS = P // (2 * HALF)
                with nc.Block() as block:
                    @block.vector
                    def _(dve):
                        dve.sem_inc(hots_used, 2)
                        with dve.Fori(0, TOK // (2 * HALF)) as i:
                            for half in range(2):
                                dve.wait_ge(hots_used, i * 2 + (half + 1))
                                for j in range(HALF):
                                    k = half * HALF + j
                                    at_t = lambda r: idT[:, r, bass.ds(i * 2 * HALF + k, 1)]
                                    nc.vector.tensor_scalar(hot2[:, k, :], row("iota"), at_t(1), None, ALU.is_equal)
                                    last = nc.vector.tensor_scalar(hot1[:, k, :], row("iota"), at_t(0), at_t(2),
                                                                   ALU.is_equal, ALU.mult)
                                last.then_inc(hots_ready, 1)

                    @block.tensor
                    def _(pe):
                        with pe.Fori(0, TOK // (2 * HALF)) as i:
                            for half in range(2):
                                pe.wait_ge(hots_ready, i * 2 + (half + 1))
                                for q in range(2):
                                    b = 2 * half + q
                                    pe.wait_ge(g_copied, i * 4 + (b + 1))
                                    for j in range(4):
                                        k = half * HALF + q * 4 + j
                                        last = nc.tensor.matmul(ps[b][:, j * P:(j + 1) * P], lhsT=hot2[:, k, :],
                                                                rhs=hot1[:, k, :], start=True, stop=True)
                                last.then_inc(hots_used, 1)

                    @block.scalar
                    def _(act):
                        act.sem_inc(g_copied, 4)
                        with act.Fori(0, TILES) as t:
                            act.wait_ge(staged_free, t * 16 + 16)
                            with act.Fori(0, ROUNDS) as r:
                                for half in range(2):
                                    act.wait_ge(hots_used, t * (2 * ROUNDS) + r * 2 + (half + 3))
                                    for q in range(2):
                                        b = 2 * half + q
                                        nc.scalar.activation(staged[:, :, bass.ds(r * 16 + 4 * b, 4)],
                                                             ps[b][:, :].rearrange("p (t i) -> p i t", t=4),
                                                             ACT.Copy).then_inc(g_copied, 1)

                    @block.sync
                    def _(sp):
                        sp.sem_inc(staged_free, 16)
                        with sp.Fori(0, TILES) as t:
                            sp.wait_ge(g_copied, t * (4 * ROUNDS) + (4 * ROUNDS + 4))
                            sp.dma_start(gates_dram[:, :, bass.ds(t * P, P)].rearrange("i p t -> p i t"),
                                         staged[:, :, :]).then_inc(staged_free, 16)
                        sp.wait_ge(staged_free, (TILES + 1) * 16)

        def experts(layer, tag):
            first = take(N_PEER)
            NB = BLOCKS_PER_GROUP
            NGROUPS = EXPERT_BLOCKS // NB
            with ExitStack() as ph:
                gbuf = sb(f"gbuf{tag}", [P, 2, NB, TOK], into=ph)
                gelu = sb(f"gelu{tag}", [P, 2, TOK], into=ph)
                act_t = sb(f"act{tag}", [P, NB, TOK], into=ph)
                hs = [pb(f"hs{tag}{j}", into=ph) for j in range(2)]
                hp = [pb(f"hp{tag}{j}", into=ph) for j in range(2)]
                os_ = [pb(f"os{tag}{j}", into=ph) for j in range(2)]
                op_ = [pb(f"op{tag}{j}", into=ph) for j in range(2)]
                gelu_done, acts_done, outs_done, outs_free = (
                    sem(f"{n}{tag}") for n in ("gelu_done", "acts_done", "outs_done", "outs_free"))
                gates_in = [sem(f"gates_in{tag}{j}") for j in range(2)]
                with nc.Block() as block:
                    @block.sync
                    def _(sp):
                        feed(sp, first, N_PEER)

                    @block.gpsimd
                    def _(pool):
                        def load_gates(j, group):
                            pool.dma_start(gbuf[:, j, :, :], gates_dram[bass.ds(group * NB, NB), :, :]
                                           .rearrange("i p t -> p i t")).then_inc(gates_in[j], 16)

                        for j in range(2):
                            load_gates(j, j)
                        with pool.Fori(0, NGROUPS // 2 - 1) as i:
                            for j in range(2):
                                pool.wait_ge(acts_done, i * (2 * NB) + ((j + 1) * NB + 2))
                                load_gates(j, i * 2 + (j + 2))

                    @block.tensor
                    def _(pe):
                        with pe.Fori(0, NGROUPS) as g:
                            for e in range(NB):
                                loaded(pe, e, g + first // SLOTS)
                                pe.wait_ge(gelu_done, g * NB + (e + 1))
                                for c in range(NCH):
                                    last = pair_matmul(hs[e % 2][:, :], hp[e % 2][:, 0:PROMPT],
                                                       ring[:, e, c * P:(c + 1) * P], hT, c, c == 0, c == NCH - 1)
                                last.then_inc(blocks_used, 1)
                            for e in range(NB):
                                loaded(pe, NB + e, g + first // SLOTS)
                            for d in range(NCH):
                                pe.wait_ge(outs_free, g * NCH + (d + 1))
                                for e in range(NB):
                                    if d == 0:
                                        pe.wait_ge(acts_done, g * NB + (e + 3))
                                    last = pair_matmul(os_[d % 2][:, :], op_[d % 2][:, 0:PROMPT],
                                                       ring[:, NB + e, d * P:(d + 1) * P], act_t, e, e == 0, e == NB - 1)
                                last.then_inc(outs_done, 1)
                            pe.wait_ge(outs_done, g * NCH + NCH)
                            pe.sem_inc(blocks_used, NB)

                    @block.scalar
                    def _(act):
                        act.sem_inc(gelu_done, 2)
                        with act.Fori(0, NGROUPS) as g:
                            for e in range(NB):
                                act.wait_ge(blocks_used, g * SLOTS + (first + e + 1))
                                act.wait_ge(acts_done, g * NB + (e + 1))
                                nc.scalar.activation(gelu[:, e % 2, 0:SAMPLE], hs[e % 2][:, :], ACT.Gelu)
                                nc.scalar.activation(gelu[:, e % 2, SAMPLE:TOK], hp[e % 2][:, 0:PROMPT],
                                                     ACT.Gelu).then_inc(gelu_done, 1)

                    @block.vector
                    def _(dve):
                        dve.sem_inc(acts_done, 2)
                        dve.sem_inc(outs_free, 2)
                        with dve.Fori(0, NGROUPS // 2) as i:
                            for j in range(2):
                                dve.wait_ge(gates_in[j], i * 16 + 16)
                                for e in range(NB):
                                    dve.wait_ge(gelu_done, i * (2 * NB) + (j * NB + e + 3))
                                    nc.vector.tensor_tensor(act_t[:, e, :], gelu[:, e % 2, :], gbuf[:, j, e, :],
                                                            ALU.mult).then_inc(acts_done, 1)
                                for d in range(NCH):
                                    dve.wait_ge(outs_done, i * (2 * NCH) + (j * NCH + d + 1))
                                    for k, src, a, b in ((0, os_[d % 2][:, :], 0, SAMPLE),
                                                         (1, op_[d % 2][:, 0:PROMPT], SAMPLE, TOK)):
                                        last = nc.vector.scalar_tensor_tensor(
                                            xT[:, d, a:b], in0=src, scalar=mods[:, G2 * NCH + d, k:k + 1],
                                            in1=xT[:, d, a:b], op0=ALU.mult, op1=ALU.add)
                                    last.then_inc(outs_free, 1)

        def ssd_mixer():
            with ExitStack() as ph:
                Y = sb("Y", [P, TILES, SSM_INNER], into=ph)
                ssd_scan(Y)
                gate_by_z(Y)
                yT = sb("yT", [P, SSM_INNER // P, TOK], into=ph)
                norm_y(Y, yT)
                project("ssd_out", N_SSD_OUT, yT, add_gated(G1), dve_evac=True, chunks=2 * NCH)

        def ssd_scan(Y):
            first = take(N_SSD)
            with ExitStack() as ph:
                W64 = 2 * HEADS
                wdt_s = sb("wdt_s", [P, NCH, W64], into=ph)
                dt = sb("dt", [P, TILES, W64], into=ph)
                dA = sb("dA", [P, TILES, W64], into=ph)
                t1 = sb("dt_t1", [P, TILES, W64], into=ph)
                t2 = sb("dt_t2", [P, TILES, W64], into=ph)
                t3 = sb("dt_t3", [P, TILES, W64], into=ph)
                negA = sb("negA", [P, W64], into=ph)
                decay = sb("decay", [P, TILES, 6 * HEADS], into=ph)
                IN_F, OUT_F, IN_B, OUT_B, ALL_F, ALL_B = (HEADS * k for k in range(6))
                state_w = sb("state_w", [P, TILES, W64], into=ph)
                with ExitStack() as pp:
                    pdt = pb("pdt", into=pp)
                    pdec = [pb(f"pdec{j}", into=pp) for j in range(TILES)]
                    wdt_loaded, dt_done, dt_act, dA_done, dec_done, dec_exp = (
                        sem(n) for n in ("wdt_loaded", "dt_done", "dt_act", "dA_done", "dec_done", "dec_exp"))
                    with nc.Block() as block:
                        @block.sync
                        def _(sp):
                            sp.dma_start(wdt_s[:, :, :], wdt).then_inc(wdt_loaded, 16)

                        @block.tensor
                        def _(pe):
                            pe.wait_ge(wdt_loaded, 16)
                            for t in range(TILES):
                                for c in range(NCH):
                                    last = nc.tensor.matmul(pdt[:, t * W64:(t + 1) * W64], lhsT=hT[:, c, t * P:(t + 1) * P],
                                                            rhs=wdt_s[:, c, :], start=c == 0, stop=c == NCH - 1)
                            last.then_inc(dt_done, 1)
                            pe.wait_ge(dA_done, 1)
                            for t in range(TILES):
                                f, b = dA[:, t, 0:HEADS], dA[:, t, HEADS:W64]
                                for at_, m, rhs in ((IN_F, LE, f), (OUT_F, GT, f), (IN_B, GE, b), (OUT_B, LT, b),
                                                    (ALL_F, ONES, f), (ALL_B, ONES, b)):
                                    last = nc.tensor.matmul(pdec[t][:, at_:at_ + HEADS], lhsT=masks[:, m, :], rhs=rhs,
                                                            start=True, stop=True)
                            last.then_inc(dec_done, 1)

                        @block.scalar
                        def _(act):
                            nc.scalar.activation(negA[:, :], row("a_log"), ACT.Exp).then_inc(dt_act, 1)
                            act.wait_ge(dt_act, 2)
                            nc.scalar.activation(t2[:, :, :], t2[:, :, :], ACT.Exp).then_inc(dt_act, 1)
                            act.wait_ge(dt_act, 4)
                            nc.scalar.activation(t3[:, :, :], t1[:, :, :], ACT.Ln).then_inc(dt_act, 1)
                            act.wait_ge(dec_done, 1)
                            for t in range(TILES):
                                nc.scalar.activation(decay[:, t, :], pdec[t][:, 0:6 * HEADS], ACT.Exp).then_inc(dec_exp, 1)

                        @block.vector
                        def _(dve):
                            v = nc.vector

                            def step(ins):
                                dve_steps.did(ins)
                                dve_steps.settle(dve)

                            dve.wait_ge(dt_done, 1)
                            step(v.tensor_tensor(dt[:, :, :], pdt[:, 0:TILES * W64].rearrange("p (t h) -> p t h", t=TILES),
                                                 bcast(row("dt_bias"), 1, TILES), ALU.add))
                            dve.wait_ge(dt_act, 1)
                            v.scalar_tensor_tensor(t2[:, :, :], in0=dt[:, :, :], scalar=-1.0, in1=dt[:, :, :],
                                                   op0=ALU.mult, op1=ALU.min).then_inc(dt_act, 1)
                            step(v.tensor_scalar(dt[:, :, :], dt[:, :, :], 0.0, None, ALU.max))
                            dve.wait_ge(dt_act, 3)
                            v.tensor_scalar(t1[:, :, :], t2[:, :, :], 1.0, None, ALU.add).then_inc(dt_act, 1)
                            dve.wait_ge(dt_act, 5)
                            step(v.tensor_scalar(dA[:, :, :], t1[:, :, :], 1.0, None, ALU.is_equal))
                            step(v.scalar_tensor_tensor(t1[:, :, :], in0=t1[:, :, :], scalar=-1.0, in1=dA[:, :, :],
                                                        op0=ALU.add, op1=ALU.add))
                            step(v.tensor_tensor(t3[:, :, :], t3[:, :, :], dA[:, :, :], ALU.add))
                            step(v.reciprocal(t1[:, :, :], t1[:, :, :]))
                            step(v.tensor_tensor(t3[:, :, :], t3[:, :, :], t2[:, :, :], ALU.mult))
                            step(v.tensor_tensor(t3[:, :, :], t3[:, :, :], t1[:, :, :], ALU.mult))
                            step(v.tensor_tensor(dt[:, :, :], dt[:, :, :], t3[:, :, :], ALU.add))
                            v.scalar_tensor_tensor(dA[:, :, :], in0=dt[:, :, :], scalar=-1.0,
                                                   in1=bcast(negA[:, :], 1, TILES), op0=ALU.mult, op1=ALU.mult).then_inc(dA_done, 1)
                            dve.wait_ge(dec_exp, TILES)
                            v.tensor_tensor(state_w[:, :, 0:HEADS], dt[:, :, 0:HEADS], decay[:, :, OUT_F:OUT_F + HEADS], ALU.mult)
                            v.tensor_tensor(state_w[:, :, HEADS:W64], dt[:, :, HEADS:W64], decay[:, :, OUT_B:OUT_B + HEADS], ALU.mult)
                scan_groups(Y, first, dt, dA, decay, state_w)

        SSM_BLOCK = [lambda g: g * 2, lambda g: g * 2 + 1, lambda g: g + 16, lambda g: g + 24]

        def scan_groups(Y, first, dt, dA, decay, state_w):
            IN_F, OUT_F, IN_B, OUT_B, ALL_F, ALL_B = (HEADS * k for k in range(6))
            LAST = SAMPLE_TILES - 1
            BF, CF = 2, 3
            with ExitStack() as ph:
                PADDED = 8 * (GRID_W + 2) + PROMPT + 2
                upad = sb("su", [P, 2, PADDED], into=ph)
                conv = sb("sv", [P, 2, PADDED], into=ph)
                chan = sb("chan", [P, 4, TOK], into=ph)
                tokm = sb("tokm", [P, TILES, 3 * P], into=ph)
                xdt = sb("xdt", [P, 2, GW], into=ph)
                xw = sb("xw", [P, 2, GW], into=ph)
                xD = sb("xD", [P, GW], into=ph)
                spans = sb("spans", [P, 2, HPG, P], into=ph)
                E = sb("E", [P, HPG, P], into=ph)
                CBm = sb("CBm", [P, 2, P], into=ph)
                mix = sb("mix", [P, 2, HPG, P], into=ph)
                off = sb("off", [P, 2, GW], into=ph)
                init = sb("init", [P, 2, GW], into=ph)
                SF = sb("SF", [P, SAMPLE_TILES, GW], into=ph)
                SB = sb("SB", [P, SAMPLE_TILES, GW], into=ph)
                last_s = sb("last_s", [P, 2, GW], into=ph)
                ps = [pb(f"gs{j}", into=ph) for j in range(2)]
                p_seg = pb("p_seg", into=ph)
                p_cb = pb("p_cb", into=ph)
                p_y = pb("p_y", into=ph)
                p_off = pb("p_off", into=ph)
                p_st = pb("p_st", into=ph)
                pq = [p_cb, p_y]
                p_t = ps[0]
                S = {n: sem("scan_" + n) for n in (
                    "init_in", "copied", "conved", "silued", "turned", "turned_out", "weighted", "spanned",
                    "seg", "exped", "cb", "cb_used", "mixed", "y", "y_used", "off", "st", "st_used", "states",
                    "final", "final_out", "last_free", "dma_turns")}
                GPR = 2
                with nc.Block() as block:
                    @block.sync
                    def _(sp):
                        feed(sp, first, N_SSD)

                    @block.gpsimd
                    def _(pool):
                        p = nc.gpsimd
                        pool.sem_inc(S["last_free"], 1)
                        pool.sem_inc(S["exped"], 1)
                        with pool.Fori(0, SSM_GROUPS) as g:
                            pool.wait_ge(S["y_used"], g * TILES + 1)
                            pool.sem_inc(S["dma_turns"], 1)
                            pool.dma_start(init[:, :, :], state_in[g]).then_inc(S["init_in"], 16)
                            for t in range(TILES):
                                pool.wait_ge(S["seg"], g * TILES + (t + 1))
                                for d, m in ((0, GT), (1, LT)):
                                    last = p.tensor_tensor(
                                        spans[:, d, :, :], bcast(masks[:, m, :], 1, HPG),
                                        bcast(dA[:, t, bass.ds(g * HPG + d * HEADS, HPG)], 2, P), ALU.mult)
                                last.then_inc(S["spanned"], 1)
                            pool.wait_ge(S["final"], g + 1)
                            pool.sem_inc(S["dma_turns"], 1)
                            pool.dma_start(state_out[g], last_s[:, :, :]).then_inc(S["final_out"], 16)
                            pool.wait_ge(S["final_out"], g * 16 + 16)
                            pool.sem_inc(S["last_free"], 1)

                    @block.tensor
                    def _(pe):
                        mm = nc.tensor.matmul
                        pe.sem_inc(S["seg"], 1)
                        with pe.Fori(0, SSM_GROUPS // GPR) as r:
                            for j in range(GPR):
                                def n(per, k):
                                    return r * (GPR * per) + (j * per + k)
                                for b in range(4):
                                    s = 4 * j + b
                                    loaded(pe, s, r + first // SLOTS)
                                    pe.wait_ge(S["copied"], n(4, b + 1))
                                    if b == 0:
                                        pe.wait_ge(S["turned_out"], n(TILES, 1))
                                        pe.wait_ge(S["cb_used"], n(TILES, 1))
                                        pe.wait_ge(S["y_used"], n(TILES, 1))
                                    for c in range(NCH):
                                        last = pair_matmul(ps[b % 2][:, :], pq[b % 2][:, 0:PROMPT],
                                                           ring[:, s, c * P:(c + 1) * P], hT, c, c == 0, c == NCH - 1)
                                    last.then_inc(blocks_used, 1)
                                pe.wait_ge(S["silued"], n(4, 3))
                                for t in range(TILES):
                                    pe.wait_ge(S["turned_out"], n(TILES, t + 1))
                                    for b in range(3):
                                        last = nc.tensor.transpose(p_t[:, b * P:(b + 1) * P], chan[:, b, t * P:(t + 1) * P],
                                                                   masks[:, IDENT, :])
                                    last.then_inc(S["turned"], 1)
                                k = 0
                                for t, d in [(3, 1), (2, 1), (1, 1), (0, 0), (1, 0), (2, 0), (4, 0), (4, 1)]:
                                    pe.wait_ge(S["weighted"], n(8, k + 1))
                                    pe.wait_ge(S["st_used"], n(8, k + 1))
                                    mm(p_st[:, 0:GW], lhsT=tokm[:, t, 2 * P:3 * P], rhs=xw[:, k % 2, :],
                                       start=True, stop=True).then_inc(S["st"], 1)
                                    k += 1
                                pe.wait_ge(S["silued"], n(4, 4))
                                for t in range(TILES):
                                    tok = slice(t * P, (t + 1) * P)
                                    pe.wait_ge(S["cb_used"], n(TILES, t + 1))
                                    mm(p_cb[:, 0:P], lhsT=chan[:, BF, tok], rhs=chan[:, CF, tok], start=True,
                                       stop=True).then_inc(S["cb"], 1)
                                    pe.wait_ge(S["spanned"], n(TILES, t + 1))
                                    pe.wait_ge(S["exped"], n(TILES, t + 1))
                                    for h in range(HPG):
                                        mm(p_seg[:, h * P:(h + 1) * P], lhsT=spans[:, 0, h, :], rhs=masks[:, LE, :],
                                           start=True, stop=False)
                                        last = mm(p_seg[:, h * P:(h + 1) * P], lhsT=spans[:, 1, h, :],
                                                  rhs=masks[:, GE, :], start=False, stop=True)
                                    last.then_inc(S["seg"], 1)
                                    pe.wait_ge(S["y_used"], n(TILES, t + 1))
                                    if t < SAMPLE_TILES:
                                        pe.wait_ge(S["states"], n(1, 1))
                                        mm(p_off[:, 0:GW], lhsT=chan[:, CF, tok], rhs=SF[:, t, :], start=True, stop=True)
                                        mm(p_off[:, GW:2 * GW], lhsT=chan[:, CF, tok], rhs=SB[:, t, :], start=True,
                                           stop=True).then_inc(S["off"], 1)
                                    pe.wait_ge(S["mixed"], n(TILES, t + 2))
                                    for h in range(HPG):
                                        out = p_y[:, h * HEADDIM:(h + 1) * HEADDIM]
                                        mm(out, lhsT=mix[:, 0, h, :], rhs=xdt[:, 0, h * HEADDIM:(h + 1) * HEADDIM],
                                           start=True, stop=False)
                                        last = mm(out, lhsT=mix[:, 1, h, :], rhs=xdt[:, 1, h * HEADDIM:(h + 1) * HEADDIM],
                                                  start=False, stop=True)
                                    last.then_inc(S["y"], 1)

                    def silu(act, g, b):
                        a = nc.scalar.activation
                        act.wait_ge(S["conved"], g * 4 + (b + 3))
                        blk = SSM_BLOCK[b]
                        bias = cols[:, bass.ds(blk(g) + COL_AT["ssd_conv_b"][0], 1)]
                        v = conv[:, b % 2, :]
                        a(chan[:, b, 0:SAMPLE].rearrange("p (r w) -> p r w", w=GRID_W), grid(v), ACT.Silu, bias=bias)
                        a(chan[:, b, SAMPLE:TOK], row_p(v), ACT.Silu, bias=bias).then_inc(S["silued"], 1)

                    @block.scalar
                    def _(act):
                        a = nc.scalar.activation
                        act.sem_inc(S["copied"], 2)
                        act.sem_inc(S["turned_out"], 1)
                        with act.Fori(0, SSM_GROUPS) as g:
                            for b in range(4):
                                act.wait_ge(blocks_used, g * 4 + (first + b + 1))
                                act.wait_ge(S["conved"], g * 4 + (b + 1))
                                a(grid(upad[:, b % 2, :]), ps[b % 2][:, :].rearrange("p (r w) -> p r w", w=GRID_W), ACT.Copy)
                                a(row_p(upad[:, b % 2, :]), pq[b % 2][:, 0:PROMPT], ACT.Copy).then_inc(S["copied"], 1)
                                if b:
                                    silu(act, g, b - 1)
                            silu(act, g, 3)
                            for t in range(TILES):
                                act.wait_ge(S["turned"], g * TILES + (t + 1))
                                a(tokm[:, t, :], p_t[:, 0:3 * P], ACT.Copy).then_inc(S["turned_out"], 1)
                            for t in range(TILES):
                                act.wait_ge(S["seg"], g * TILES + (t + 2))
                                act.wait_ge(S["mixed"], g * TILES + (t + 1))
                                a(E[:, :, :].rearrange("p h l -> p (h l)"), p_seg[:, :], ACT.Exp).then_inc(S["exped"], 1)

                    @block.vector
                    def _(dve):
                        v = nc.vector
                        D = dve_steps
                        heads = lambda ap: ap.rearrange("p (h q) -> p h q", h=HPG)
                        D.did(v.memset(upad[:, :, :], 0.0))
                        D.settle(dve)
                        for name, k in (("conved", 2), ("st_used", 1), ("cb_used", 1), ("mixed", 1), ("y_used", 1)):
                            dve.sem_inc(S[name], k)
                        STEPS = 4 * 3 + 2 + 6 * 2 + 2 + TILES * 5 + SAMPLE_TILES * 4
                        with D.loop(dve, SSM_GROUPS, STEPS) as g:
                            hd = lambda ap3, t, at_: bcast(ap3[:, t, bass.ds(g * HPG + at_, HPG)], 2, HEADDIM)
                            for b in range(4):
                                dve.wait_ge(S["copied"], g * 4 + (b + 3))
                                if b >= 2:
                                    dve.wait_ge(S["silued"], g * 4 + (b - 1))
                                blk = SSM_BLOCK[b]
                                w = lambda k: cols[:, bass.ds(blk(g) * 3 + (COL_AT["ssd_conv_w"][0] + k), 1)]
                                conv3(dve, conv[:, b % 2, :], upad[:, b % 2, :], w)
                                dve.sem_inc(S["conved"], 1)
                            dve.wait_ge(S["init_in"], g * 16 + 16)
                            D.did(v.tensor_copy(SF[:, 0, :], init[:, 0, :]))
                            D.did(v.tensor_copy(SB[:, LAST, :], init[:, 1, :]))
                            k = 0
                            order = [(3, 1), (2, 1), (1, 1), (0, 0), (1, 0), (2, 0), (4, 0), (4, 1)]

                            def weigh(k):
                                t, d = order[k]
                                dve.wait_ge(S["turned_out"], g * TILES + (t + 2))
                                v.tensor_tensor(heads(xw[:, k % 2, :]), heads(tokm[:, t, 0:GW]),
                                                hd(state_w, t, d * HEADS), ALU.mult).then_inc(S["weighted"], 1)

                            weigh(0)
                            for k, (t, d) in enumerate(order):
                                if k + 1 < len(order):
                                    weigh(k + 1)
                                dve.wait_ge(S["st"], g * 8 + (k + 1))
                                if t == SAMPLE_TILES:
                                    if d == 0:
                                        dve.wait_ge(S["last_free"], g + 1)
                                    ins = v.tensor_copy(last_s[:, d, :], p_st[:, 0:GW])
                                    D.did(ins)
                                    D.settle(dve)
                                    dve.sem_inc(S["st_used"], 1)
                                    if d == 1:
                                        dve.sem_inc(S["final"], 1)
                                    continue
                                src, dst = (SF[:, t, :], SF[:, t + 1, :]) if d == 0 else (SB[:, t, :], SB[:, t - 1, :])
                                D.settle(dve)
                                D.did(v.tensor_tensor(heads(dst), heads(src), hd(decay, t, ALL_B if d else ALL_F), ALU.mult))
                                D.settle(dve)
                                D.did(v.tensor_tensor(dst, dst, p_st[:, 0:GW], ALU.add))
                                D.settle(dve)
                                dve.sem_inc(S["st_used"], 1)
                            dve.sem_inc(S["states"], 1)
                            for t in range(TILES):
                                for d in range(2):
                                    D.did(v.tensor_tensor(heads(xdt[:, d, :]), heads(tokm[:, t, 0:GW]),
                                                          hd(dt, t, d * HEADS), ALU.mult))
                                dve.wait_ge(S["cb"], g * TILES + (t + 1))
                                D.did(v.tensor_tensor(CBm[:, 0, :], p_cb[:, 0:P], masks[:, LE, :], ALU.mult))
                                D.did(v.tensor_tensor(CBm[:, 1, :], p_cb[:, 0:P], masks[:, GE, :], ALU.mult))
                                D.settle(dve)
                                dve.sem_inc(S["cb_used"], 1)
                                dve.wait_ge(S["exped"], g * TILES + (t + 2))
                                for d in range(2):
                                    last = v.tensor_tensor(mix[:, d, :, :], E[:, :, :], bcast(CBm[:, d, :], 1, HPG), ALU.mult)
                                last.then_inc(S["mixed"], 1)
                                D.did(v.tensor_tensor(heads(xD[:, :]), heads(tokm[:, t, 0:GW]),
                                                      bcast(rows[:, bass.ds(g * HPG + ROW_AT["d"][0], HPG)], 2, HEADDIM), ALU.mult))
                                y_out_t = Y[:, t, bass.ds(g * GW, GW)]
                                if t < SAMPLE_TILES:
                                    dve.wait_ge(S["off"], g * SAMPLE_TILES + (t + 1))
                                    D.did(v.tensor_tensor(heads(off[:, 0, :]), heads(p_off[:, 0:GW]), hd(decay, t, IN_F), ALU.mult))
                                    D.did(v.tensor_tensor(heads(off[:, 1, :]), heads(p_off[:, GW:2 * GW]), hd(decay, t, IN_B), ALU.mult))
                                    D.settle(dve)
                                    D.did(v.tensor_tensor(off[:, 0, :], off[:, 0, :], off[:, 1, :], ALU.add))
                                    D.settle(dve)
                                    D.did(v.tensor_tensor(xD[:, :], xD[:, :], off[:, 0, :], ALU.add))
                                dve.wait_ge(S["y"], g * TILES + (t + 1))
                                D.settle(dve)
                                v.tensor_tensor(y_out_t, p_y[:, 0:GW], xD[:, :], ALU.add).then_inc(S["y_used"], 1)

        def gate_by_z(Y):
            first = take(N_Z)
            with ExitStack() as ph:
                zs = sb("zs", [P, 2, 512], into=ph)
                ps = [pb(f"pz{j}", into=ph) for j in range(2)]
                z_done, z_out, gated = (sem(n) for n in ("z_done", "z_out", "gated"))
                with nc.Block() as block:
                    @block.sync
                    def _(sp):
                        feed(sp, first, N_Z)

                    @block.tensor
                    def _(pe):
                        pe.sem_inc(z_out, 2)
                        with pe.Fori(0, 2) as r:
                            for j in range(2):
                                for s in range(4 * j, 4 * j + 4):
                                    loaded(pe, s, r + first // SLOTS)
                                for t in range(TILES):
                                    k = j * TILES + t
                                    pe.wait_ge(z_out, r * (2 * TILES) + (k + 1))
                                    for c in range(NCH):
                                        last = nc.tensor.matmul(
                                            ps[k % 2][:, :], lhsT=hT[:, c, t * P:(t + 1) * P],
                                            rhs=ring[:, 4 * j + c // 2, (c % 2) * 512:(c % 2) * 512 + 512],
                                            start=c == 0, stop=c == NCH - 1)
                                    last.then_inc(z_done, 1)
                                pe.wait_ge(z_done, r * (2 * TILES) + ((j + 1) * TILES))
                                pe.sem_inc(blocks_used, 4)

                    @block.scalar
                    def _(act):
                        act.sem_inc(gated, 2)
                        with act.Fori(0, 2) as r:
                            for k in range(2 * TILES):
                                act.wait_ge(z_done, r * (2 * TILES) + (k + 1))
                                act.wait_ge(gated, r * (2 * TILES) + (k + 1))
                                nc.scalar.activation(zs[:, k % 2, :], ps[k % 2][:, :], ACT.Silu).then_inc(z_out, 1)

                    @block.vector
                    def _(dve):
                        with dve.Fori(0, 2) as r:
                            for k in range(2 * TILES):
                                dve.wait_ge(z_out, r * (2 * TILES) + (k + 3))
                                y = Y[:, k % TILES, bass.ds(r * 1024 + (k // TILES) * 512, 512)]
                                nc.vector.tensor_tensor(y, y, zs[:, k % 2, :], ALU.mult).then_inc(gated, 1)

        def norm_y(Y, yT):
            with ExitStack() as ph:
                junk = sb("junk", [P, SSM_INNER], into=ph)
                ss = sb("ss", [P, TILES], into=ph)
                ps = [pb(f"pyt{j}", into=ph) for j in range(2)]
                summed, rooted, scaled, turned, out = (sem(n) for n in ("y_summed", "y_rooted", "y_scaled", "y_turned", "y_out"))
                with nc.Block() as block:
                    @block.vector
                    def _(dve):
                        v = nc.vector
                        for t in range(TILES):
                            dve_steps.did(v.tensor_tensor_reduce(out=junk[:, :], in0=Y[:, t, :], in1=Y[:, t, :], scale=1.0,
                                                                 scalar=0.0, op0=ALU.mult, op1=ALU.add,
                                                                 accum_out=ss[:, t:t + 1]))
                            dve_steps.settle(dve)
                        dve.sem_inc(summed, 1)
                        dve.wait_ge(rooted, 1)
                        dve_steps.did(v.reciprocal(ss[:, :], ss[:, :]))
                        dve_steps.settle(dve)
                        for t in range(TILES):
                            v.tensor_scalar(Y[:, t, :], Y[:, t, :], ss[:, t:t + 1], None, ALU.mult).then_inc(scaled, 1)
                            for b in range(4):
                                k = 4 * t + b
                                dve.wait_ge(turned, k + 1)
                                v.tensor_tensor(yT[:, 4 * b:4 * b + 4, t * P:(t + 1) * P],
                                                ps[k % 2][:, :].rearrange("p (b t) -> p b t", b=4),
                                                bcast(col("ssd_norm_w", 4 * b, 4 * b + 4), 2, P), ALU.mult).then_inc(out, 1)

                    @block.scalar
                    def _(act):
                        act.wait_ge(summed, 1)
                        nc.scalar.activation(ss[:, :], ss[:, :], ACT.Sqrt, bias=eps[:, :], scale=1.0 / SSM_INNER).then_inc(rooted, 1)

                    @block.tensor
                    def _(pe):
                        for t in range(TILES):
                            pe.wait_ge(scaled, t + 1)
                            for b in range(4):
                                k = 4 * t + b
                                if k >= 2:
                                    pe.wait_ge(out, k - 1)
                                for q in range(4):
                                    last = nc.tensor.transpose(ps[k % 2][:, q * P:(q + 1) * P],
                                                               Y[:, t, (4 * b + q) * P:(4 * b + q + 1) * P], masks[:, IDENT, :])
                                last.then_inc(turned, 1)

        def finish():
            stored = sem("stored")
            with nc.Block() as block:
                @block.sync
                def _(sp):
                    sp.dma_start(y_out, hT[:, :, :]).then_inc(stored, 16)
                    sp.wait_ge(stored, 16)

        def scale_of(t):
            return lambda c, k: t[:, c, k:k + 1]

        def shift_of(comp):
            return lambda c, k: mods[:, comp * NCH + c, k:k + 1]

        stages = []
        for layer in range(DEPTH):
            stages += [
                lambda layer=layer: adaln(layer),
                lambda layer=layer: norm_modulate(f"m{layer}", hT, scale_of(scale_mix), shift_of(SH1)),
                ssd_mixer if layer % 2 else even_mixer,
                lambda layer=layer: norm_modulate(f"f{layer}", hT, scale_of(scale_ffn), shift_of(SH2)),
                lambda layer=layer: peer(layer),
            ]
        for stage in stages:
            stage()
        norm_modulate("last", hT, lambda c, k: col("norm_final", c, c + 1), None)
        finish()


def kernel(**inputs):
    import numpy as np
    import concourse.bacc as bacc
    from concourse.bass_utils import run_bass_kernel_spmd

    a = {k: np.asarray(v) for k, v in inputs.items()}

    def chunks(v):
        return v.reshape(-1, P).T

    def out_blocks(w):
        k, n = w.shape
        return w.reshape(k // P, P, n // P, P).transpose(2, 1, 0, 3).reshape(n // P, P, k)

    w_ssd = a["ssd_w_in"][0]
    w_z, w_xbc, w_dt = w_ssd[:, :SSM_INNER], w_ssd[:, SSM_INNER:SSM_INNER + 4096], w_ssd[:, SSM_INNER + 4096:]
    xbc = out_blocks(w_xbc)
    order = [b for g in range(SSM_GROUPS) for b in (2 * g, 2 * g + 1, 16 + g, 24 + g)]
    z = w_z.reshape(4, 2, P, 4, 512).transpose(3, 0, 2, 1, 4).reshape(16, P, 1024)
    ssd_out = a["ssd_w_out"][0].reshape(2, NCH, P, NCH, P).transpose(3, 0, 2, 1, 4).reshape(16, P, 1024)

    def experts_of(layer):
        G, B = EXPERT_BLOCKS // BLOCKS_PER_GROUP, BLOCKS_PER_GROUP
        u = a["peer_u"][layer].reshape(G, B, KEYS, NCH, P).transpose(0, 1, 4, 3, 2).reshape(G, B, P, 1024)
        v = a["peer_v"][layer].reshape(G, B, P, 1024)
        return np.concatenate([u, v], axis=1).reshape(2 * EXPERT_BLOCKS, P, 1024)

    stream = np.concatenate([
        out_blocks(a["adaln_w"][0]), out_blocks(a["even_w_in"][0]), out_blocks(a["even_w_out"][0]),
        out_blocks(a["peer_w_q"][0]), experts_of(0),
        out_blocks(a["adaln_w"][1]), xbc[order], z, ssd_out, out_blocks(a["peer_w_q"][1]), experts_of(1)])
    keys = a["peer_keys"].transpose(0, 4, 1, 2, 3).reshape(DEPTH, P, 2 * PEER_HEADS * KEYS)
    wdt = w_dt.reshape(NCH, P, 64).transpose(1, 0, 2)
    xin = np.concatenate([a["x_sample"][0], a["x_prompt"][0]]).T.reshape(NCH, P, TOK).transpose(1, 0, 2)
    cond = np.stack([a["c"][0], a["c_ctx"]], axis=1).reshape(NCH, P, 2).transpose(1, 0, 2).reshape(P, 2 * NCH)
    cols = np.concatenate([
        cond, chunks(a["adaln_b"].reshape(-1)), chunks(a["norm_mix"].reshape(-1)), chunks(a["norm_ffn"].reshape(-1)),
        chunks(a["norm_final"]), a["even_conv_w"][0].reshape(3, 4, P).transpose(2, 1, 0).reshape(P, 12),
        a["ssd_conv_w"][0].reshape(3, 32, P).transpose(2, 1, 0).reshape(P, 96), chunks(a["ssd_conv_b"][0]),
        chunks(a["ssd_norm_w"][0])], axis=1)
    f32 = np.float32
    rows = np.concatenate([
        a["ssd_dt_bias"][0].reshape(-1), a["ssd_a_log"][0].reshape(-1), a["ssd_d"][0], np.arange(P, dtype=f32),
        np.arange(TOPK, dtype=f32), np.array(PAIR_AT, f32), np.array([0] + PAIRS_OF[:-1], f32)])
    rows = np.broadcast_to(rows[None, :], (P, NROWS))
    k, l = np.arange(P)[:, None], np.arange(P)[None, :]
    masks = np.stack([k <= l, k < l, k >= l, k > l, k >= 0 * l, k == l], axis=1).astype(f32)

    def angles(n):
        return 2 * np.pi * (np.outer(np.arange(n), np.arange(n)) % n) / n

    at, ac = angles(SAMPLE), angles(P)
    scale_s, scale_p = (SAMPLE * P) ** -0.5, 1.0 / P
    tiles = lambda m: m.reshape(SAMPLE_TILES, P, SAMPLE).transpose(1, 0, 2).reshape(P, -1)
    dft = np.concatenate([tiles(np.cos(at) * scale_s), tiles(-np.sin(at) * scale_s), np.cos(ac), np.sin(ac),
                          np.cos(ac) * scale_p, -np.sin(ac) * scale_p], axis=1).astype(f32)

    def states(s):
        return s[0, 0].reshape(SSM_GROUPS, GW, P).transpose(0, 2, 1)

    state_in = np.stack([states(a["state_ssd_fwd"]), states(a["state_ssd_bwd"])], axis=2)

    nc = bacc.Bacc("TRN2", target_bir_lowering=False, num_devices=1)
    arrays = dict(stream=stream, keys=keys, wdt=wdt, xin=xin, cols=cols, rows=rows, masks=masks, dft=dft,
                  state_in=state_in)
    arrays = {n: np.ascontiguousarray(v) for n, v in arrays.items()}
    aps = [nc.dram_tensor(f"in_{n}", v.shape, F32, kind="ExternalInput").ap() for n, v in arrays.items()]
    y = nc.dram_tensor("y", (P, NCH, TOK), F32, kind="ExternalOutput").ap()
    state_out = nc.dram_tensor("state_out", (SSM_GROUPS, P, 2, GW), F32, kind="ExternalOutput").ap()
    gates = nc.dram_tensor("gates", (KEYS, P, TOK), F32, kind="Internal").ap()
    hybrid_trunk(nc, *aps, y, state_out, gates)
    r = run_bass_kernel_spmd(nc, [{f"in_{n}": v for n, v in arrays.items()}], core_ids=[0]).results[0]
    y = r["y"].transpose(1, 0, 2).reshape(D_MODEL, TOK).T
    st = r["state_out"].transpose(2, 0, 3, 1).reshape(2, 1, 1, HEADS, HEADDIM, P)
    return (np.ascontiguousarray(y[None, SAMPLE:]), np.ascontiguousarray(y[None, :SAMPLE]),
            np.ascontiguousarray(st[0]), np.ascontiguousarray(st[1]))
```

```python
import concourse.bass as bass
from concourse import mybir
from contextlib import ExitStack, contextmanager

F32 = mybir.dt.float32
F32R = mybir.dt.float32r
U32 = mybir.dt.uint32
ALU = mybir.AluOpType
ACT = mybir.ActivationFunctionType
AX = mybir.AxisListType

P = 128
D_MODEL = 1024
NCH = D_MODEL // P
SAMPLE, PROMPT = 512, 128
TOK = SAMPLE + PROMPT
TILES = TOK // P
HALF_TOK = TOK // 2
HALVES = (slice(0, HALF_TOK), slice(HALF_TOK, TOK))
PARTS = ((0, slice(0, HALF_TOK), 0, slice(0, HALF_TOK)),
         (0, slice(HALF_TOK, SAMPLE), 1, slice(0, SAMPLE - HALF_TOK)),
         (1, slice(SAMPLE, TOK), 1, slice(SAMPLE - HALF_TOK, HALF_TOK)))
SAMPLE_TILES = SAMPLE // P
DEPTH = 2
GRID_W = 64
EPS = 1e-6
MODS = 6
EVEN_IN = 2048
GROUPS = 4
SSM_INNER = 2048
HEADS = 32
SSM_GROUPS = 8
HPG = HEADS // SSM_GROUPS
HEADDIM = 64
GW = HPG * HEADDIM
PEER_HEADS = 8
TOPK = 16
ENTRIES = PEER_HEADS * TOPK
KEYS = 128
EXPERT_BLOCKS = 128
BLOCKS_PER_GROUP = 4
SCATTER_TOK = 64
SLOTS = 8
HALF_RING = SLOTS // 2
NEG = -3.0e38
SH1, SC1, G1, SH2, SC2, G2 = range(MODS)

N_ADALN = MODS * NCH
N_EVEN_IN = EVEN_IN // P
N_EVEN_OUT = NCH
N_WQ = 2048 // P
N_PEER = 2 * EXPERT_BLOCKS
N_SSD = 4 * SSM_GROUPS
N_Z = 16
N_SSD_OUT = 2 * NCH

PAIRS_OF = [TOPK // (i + 1) for i in range(TOPK)]
PAIR_AT = [sum(PAIRS_OF[:i]) for i in range(TOPK)]
PAIRS = sum(PAIRS_OF)

COL_SIZES = [("cond", NCH * 2), ("adaln_b", DEPTH * N_ADALN), ("norm_mix", DEPTH * NCH),
             ("norm_ffn", DEPTH * NCH), ("norm_final", NCH), ("even_conv_w", 12), ("ssd_conv_w", 96),
             ("ssd_conv_b", 32), ("ssd_norm_w", 16)]
COL_AT, NCOLS = {}, 0
for _name, _n in COL_SIZES:
    COL_AT[_name] = (NCOLS, _n)
    NCOLS += _n
ROW_SIZES = [("dt_bias", 64), ("a_log", 64), ("d", 32), ("iota", 128), ("rank", TOPK), ("pair_at", TOPK),
             ("pairs_before", TOPK)]
ROW_AT, NROWS = {}, 0
for _name, _n in ROW_SIZES:
    ROW_AT[_name] = (NROWS, _n)
    NROWS += _n
LE, LT, GE, GT, ONES, IDENT = range(6)


class Steps:

    def __init__(self, sem):
        self.sem, self.base, self.k = sem, 0, 0

    def did(self, ins):
        self.k += 1
        return ins.then_inc(self.sem, 1)

    def settle(self, eng):
        eng.wait_ge(self.sem, self.base + self.k)

    @contextmanager
    def loop(self, eng, n, per):
        start = self.base + self.k
        with eng.Fori(0, n) as i:
            self.base, self.k = i * per + start, 0
            yield i
            assert self.k == per, (self.k, per)
        self.base, self.k = start + n * per, 0


def bcast(ap, axis, n):
    v = ap.unsqueeze(axis)
    shape = list(v.shape)
    shape[axis] = n
    return v.broadcast_to(shape)


def hybrid_trunk(nc, stream, keys, wdt, xin, cols_d, rows_d, masks_d, dft_d, state_in, y_out, state_out,
                 gates_dram):
    ctx = ExitStack()
    with ctx:
        def sb(name, shape, dt=F32, into=ctx):
            return into.enter_context(nc.sbuf_tensor(name, shape, dt))

        def pb(name, cols=512, into=ctx):
            return into.enter_context(nc.psum_tensor(name, [P, cols], F32))

        def sem(name, into=ctx):
            return ctx.enter_context(nc.semaphore(name))

        xT = sb("xT", [P, NCH, TOK])
        ring = sb("ring", [P, SLOTS, 1024])
        cols = sb("cols", [P, NCOLS])
        rows = sb("rows", [P, NROWS])
        masks = sb("masks", [P, 6, P])
        mods = sb("mods", [P, N_ADALN, 2])
        scale_mix = sb("scale_mix", [P, NCH, 2])
        scale_ffn = sb("scale_ffn", [P, NCH, 2])
        scond = sb("scond", [P, NCH, 2])
        eps = sb("eps", [P, 1])
        zero = sb("zero", [P, 1])

        def col(name, a=0, b=None):
            at, n = COL_AT[name]
            return cols[:, at + a:at + (n if b is None else b)]

        def row(name):
            at, n = ROW_AT[name]
            return rows[:, at:at + n]

        half_loaded = [sem(f"half_loaded{k}") for k in range(2)]
        blocks_used = sem("blocks_used")
        consts_loaded = sem("consts_loaded")
        x_loaded = sem("x_loaded")
        dve_steps = Steps(sem("dve_steps"))
        act_steps = Steps(sem("act_steps"))
        pool_steps = Steps(sem("pool_steps"))
        at = [0]

        def take(n):
            first = at[0]
            at[0] += n
            return first

        def load_half(sp, k, block):
            sp.dma_start(ring[:, k * HALF_RING:(k + 1) * HALF_RING, :],
                         stream[bass.ds(block, HALF_RING)].rearrange("b p n -> p b n")).then_inc(half_loaded[k], 16)

        def feed(sp, first, n):
            last = min(first + n + SLOTS, N_BLOCKS) - SLOTS
            if last == first:
                return
            with sp.Fori(0, (last - first) // SLOTS) as i:
                for k in range(2):
                    sp.wait_ge(blocks_used, i * SLOTS + (first + (k + 1) * HALF_RING))
                    load_half(sp, k, i * SLOTS + (first + SLOTS + k * HALF_RING))

        def loaded(pe, s, round_):
            if s % HALF_RING == 0:
                pe.wait_ge(half_loaded[s // HALF_RING], round_ * 16 + 16)

        N_BLOCKS = stream.shape[0]

        def pair_matmul(out_s, out_p, lhsT, rhs, c, start, stop):
            nc.tensor.matmul(out_s, lhsT=lhsT, rhs=rhs[:, c, 0:SAMPLE], start=start, stop=stop)
            return nc.tensor.matmul(out_p, lhsT=lhsT, rhs=rhs[:, c, SAMPLE:TOK], start=start, stop=stop)

        def norm_modulate(tag, dst, scale, shift, split=False):
            with ExitStack() as ph:
                sq = sb(f"sq{tag}", [P, 2, TOK], into=ph)
                rms = sb(f"rms{tag}", [P, TOK], into=ph)
                whole = sb(f"whole{tag}", [P, NCH, TOK], into=ph) if split else dst
                modulated = sem(f"modulated_{tag}")
                sum_s, sum_p = pb(f"sums{tag}", into=ph), pb(f"sump{tag}", into=ph)
                squared, summed, rooted, scaled = (sem(f"{n}_{tag}") for n in ("squared", "summed", "rooted", "scaled"))
                with nc.Block() as block:
                    @block.scalar
                    def _(act):
                        for c in range(NCH):
                            if c >= 2:
                                act.wait_ge(summed, c - 1)
                            nc.scalar.activation(sq[:, c % 2, :], xT[:, c, :], ACT.Square).then_inc(squared, 1)
                        act.wait_ge(summed, NCH)
                        nc.scalar.activation(rms[:, 0:SAMPLE], sum_s[:, :], ACT.Sqrt, bias=eps[:, :],
                                             scale=1.0 / D_MODEL).then_inc(rooted, 1)
                        nc.scalar.activation(rms[:, SAMPLE:TOK], sum_p[:, 0:PROMPT], ACT.Sqrt, bias=eps[:, :],
                                             scale=1.0 / D_MODEL).then_inc(rooted, 1)
                        for c in range(NCH):
                            act.wait_ge(scaled, c + 1)
                            for k, part in ((0, slice(0, SAMPLE)), (1, slice(SAMPLE, TOK))):
                                last = nc.scalar.activation(whole[:, c, part], whole[:, c, part], ACT.Identity,
                                                            scale=scale(c, k), bias=shift(c, k) if shift else 0.0)
                            last.then_inc(modulated, 1)

                    @block.tensor
                    def _(pe):
                        for c in range(NCH):
                            pe.wait_ge(squared, c + 1)
                            nc.tensor.matmul(sum_s[:, :], lhsT=masks[:, ONES, :], rhs=sq[:, c % 2, 0:SAMPLE],
                                             start=c == 0, stop=c == NCH - 1)
                            nc.tensor.matmul(sum_p[:, 0:PROMPT], lhsT=masks[:, ONES, :], rhs=sq[:, c % 2, SAMPLE:TOK],
                                             start=c == 0, stop=c == NCH - 1).then_inc(summed, 1)

                    @block.vector
                    def _(dve):
                        dve.wait_ge(rooted, 2)
                        dve_steps.did(nc.vector.reciprocal(rms[:, :], rms[:, :]))
                        dve_steps.settle(dve)
                        for c in range(NCH):
                            nc.vector.tensor_tensor(whole[:, c, :], xT[:, c, :], rms[:, :], ALU.mult).then_inc(scaled, 1)
                        if split:
                            for c in range(NCH):
                                dve.wait_ge(modulated, c + 1)
                                dve_steps.did(nc.vector.tensor_copy(dst[:, c, 0, :], whole[:, c, :]))
                                dve_steps.settle(dve)
                                nc.vector.tensor_tensor(dst[:, c, 1, :], whole[:, c, :], dst[:, c, 0, :].bitcast(F32),
                                                        ALU.subtract)

        def adaln(layer):
            tag = f"ada{layer}"
            first = take(N_ADALN)
            with ExitStack() as ph:
                COLS = 96
                ps = [pb(f"ps{tag}{k}", into=ph) for k in range(4)]
                silu_done = sem(f"silu_done{layer}")
                half_free = sem(f"half_free{layer}")
                with nc.Block() as block:
                    @block.sync
                    def _(sp):
                        feed(sp, first, N_ADALN)

                    @block.scalar
                    def _(act):
                        nc.scalar.activation(scond[:, :, :], col("cond").rearrange("p (c k) -> p c k", k=2),
                                             ACT.Silu).then_inc(silu_done, 1)

                    @block.tensor
                    def _(pe):
                        pe.wait_ge(silu_done, 1)
                        pe.sem_inc(half_free, 4)
                        with pe.Fori(0, N_ADALN // (2 * SLOTS)) as i:
                            for s in range(2 * SLOTS):
                                loaded(pe, s % SLOTS, i * 2 + (first // SLOTS + s // SLOTS))
                                if s % HALF_RING == 0:
                                    pe.wait_ge(half_free, i * 4 + (s // HALF_RING + 1))
                                for c in range(NCH):
                                    last = nc.tensor.matmul(
                                        ps[s // HALF_RING][:, (s % HALF_RING) * P:(s % HALF_RING) * P + COLS]
                                        .rearrange("p (r k) -> p r k", k=2),
                                        lhsT=ring[:, s % SLOTS, c * P:(c + 1) * P], rhs=bcast(scond[:, c, :], 1, COLS // 2),
                                        start=c == 0, stop=c == NCH - 1)
                                last.then_inc(blocks_used, 1)

                    @block.vector
                    def _(dve):
                        with dve_steps.loop(dve, N_ADALN // (2 * SLOTS), 0) as i:
                            for k in range(4):
                                dve.wait_ge(blocks_used, i * (2 * SLOTS) + (first + (k + 1) * HALF_RING))
                                m = i * (2 * SLOTS) + k * HALF_RING
                                bias = cols[:, bass.ds(m + (COL_AT["adaln_b"][0] + layer * N_ADALN), HALF_RING)]
                                nc.vector.tensor_tensor(
                                    mods[:, bass.ds(m, HALF_RING), :],
                                    ps[k][:, :].rearrange("p (b c) -> p b c", b=HALF_RING)[:, :, 0:2],
                                    bcast(bias, 2, 2), ALU.add).then_inc(half_free, 1)
                        dve.wait_ge(half_free, 4 + N_ADALN // HALF_RING)
                        for dst, comp, w in ((scale_mix, SC1, "norm_mix"), (scale_ffn, SC2, "norm_ffn")):
                            nc.vector.scalar_tensor_tensor(
                                dst[:, :, :], in0=mods[:, comp * NCH:(comp + 1) * NCH, :], scalar=1.0,
                                in1=bcast(col(w, layer * NCH, (layer + 1) * NCH), 2, 2), op0=ALU.add, op1=ALU.mult)

        def project(tag, n_blocks, rhs, evacuate, per_steps=0, dve_evac=False, chunks=NCH):
            first = take(n_blocks)
            each = chunks // NCH
            per_round = SLOTS // each
            with ExitStack() as ph:
                ps = [pb(f"ps{tag}{j}", into=ph) for j in range(2)]
                pp = [pb(f"pp{tag}{j}", into=ph) for j in range(2)]
                pair_free = sem(f"pair_free_{tag}")
                with nc.Block() as block:
                    @block.sync
                    def _(sp):
                        feed(sp, first, n_blocks)

                    @block.tensor
                    def _(pe):
                        with pe.Fori(0, n_blocks // SLOTS) as i:
                            for o in range(per_round):
                                pe.wait_ge(pair_free, i * per_round + (o + 1))
                                for s in range(o * each, (o + 1) * each):
                                    loaded(pe, s, i + first // SLOTS)
                                    for c in range(NCH):
                                        cc = (s - o * each) * NCH + c
                                        last = pair_matmul(ps[o % 2][:, :], pp[o % 2][:, 0:PROMPT],
                                                           ring[:, s, c * P:(c + 1) * P], rhs, cc,
                                                           cc == 0, cc == chunks - 1)
                                    last.then_inc(blocks_used, 1)

                    def evac(eng, steps):
                        eng.sem_inc(pair_free, 2)
                        with steps.loop(eng, n_blocks // SLOTS, per_steps) as i:
                            for o in range(per_round):
                                eng.wait_ge(blocks_used, i * SLOTS + (first + (o + 1) * each))
                                evacuate(eng, i * per_round + o, ps[o % 2][:, :], pp[o % 2][:, 0:PROMPT]).then_inc(pair_free, 1)

                    if dve_evac:
                        @block.vector
                        def _(dve):
                            evac(dve, dve_steps)
                    else:
                        @block.scalar
                        def _(act):
                            evac(act, act_steps)

        def split_matmuls(outs, w_hi, w_lo, rhs, c, start, stop):
            for n, (w, part) in enumerate(((w_hi, 0), (w_hi, 1), (w_lo, 0))):
                for out, cols_ in zip(outs, HALVES):
                    last = nc.tensor.matmul(out[:, 0:HALF_TOK], lhsT=w, rhs=rhs[:, c, part, cols_],
                                            start=start and n == 0, stop=stop and n == 2)
            return last

        def project_split(tag, n_blocks, rhs, evacuate, chunks=NCH):
            first = take(n_blocks)
            each = chunks // NCH
            per_round = SLOTS // each
            with ExitStack() as ph:
                wide = sb(f"wide{tag}", [P, 2, 2, 1024], F32R, into=ph)
                ps = [[pb(f"ps{tag}{j}{h}", into=ph) for h in range(2)] for j in range(2)]
                pair_free, wide_used, hi_done = (sem(f"{n}_{tag}") for n in ("pair_free", "wide_used", "hi_done"))
                with nc.Block() as block:
                    @block.sync
                    def _(sp):
                        feed(sp, first, n_blocks)

                    @block.scalar
                    def _(act):
                        act.sem_inc(wide_used, 2)
                        with act.Fori(0, n_blocks // SLOTS) as i:
                            for s in range(SLOTS):
                                loaded(act, s, i + first // SLOTS)
                                act.wait_ge(wide_used, i * SLOTS + (s + 1))
                                nc.scalar.activation(wide[:, s % 2, 0, :], ring[:, s, :], ACT.Copy).then_inc(hi_done, 1)

                    @block.gpsimd
                    def _(pool):
                        with pool.Fori(0, n_blocks // SLOTS) as i:
                            for s in range(SLOTS):
                                pool.wait_ge(hi_done, i * SLOTS + (s + 1))
                                nc.gpsimd.tensor_tensor(wide[:, s % 2, 1, :], ring[:, s, :], wide[:, s % 2, 0, :].bitcast(F32),
                                                        ALU.subtract).then_inc(blocks_used, 1)

                    @block.tensor
                    def _(pe):
                        with pe.Fori(0, n_blocks // SLOTS) as i:
                            for o in range(per_round):
                                pe.wait_ge(pair_free, i * per_round + (o + 1))
                                for s in range(o * each, (o + 1) * each):
                                    pe.wait_ge(blocks_used, i * SLOTS + (first + s + 1))
                                    for c in range(NCH):
                                        cc = (s - o * each) * NCH + c
                                        last = split_matmuls(ps[o % 2], wide[:, s % 2, 0, c * P:(c + 1) * P],
                                                             wide[:, s % 2, 1, c * P:(c + 1) * P], rhs, cc,
                                                             cc == 0, cc == chunks - 1)
                                    last.then_inc(wide_used, 1)

                    @block.vector
                    def _(dve):
                        dve.sem_inc(pair_free, 2)
                        with dve.Fori(0, n_blocks // SLOTS) as i:
                            for o in range(per_round):
                                dve.wait_ge(wide_used, i * SLOTS + ((o + 1) * each + 2))
                                evacuate(i * per_round + o, ps[o % 2]).then_inc(pair_free, 1)

        def copy_halves(dst):
            def f(m, ps):
                for h in range(2):
                    last = nc.vector.tensor_copy(dst[:, bass.ds(m, 1), HALVES[h]].rearrange("p a t -> p (a t)"),
                                                 ps[h][:, 0:HALF_TOK])
                return last
            return f

        def add_gated_halves(gate):
            def f(m, ps):
                for k, part, h, at_ in PARTS:
                    x = xT[:, bass.ds(m, 1), part].rearrange("p a t -> p (a t)")
                    last = nc.vector.scalar_tensor_tensor(
                        x, in0=ps[h][:, at_], scalar=mods[:, bass.ds(m + gate * NCH, 1), k:k + 1].rearrange("p a k -> p (a k)"),
                        in1=x, op0=ALU.mult, op1=ALU.add)
                return last
            return f

        def split_into(dst, src, n):
            his = sem(f"his_{src.name}")
            with nc.Block() as block:
                @block.scalar
                def _(act):
                    for c in range(n):
                        nc.scalar.activation(dst[:, c, 0, :], src[:, c, :], ACT.Copy).then_inc(his, 1)

                @block.vector
                def _(dve):
                    for c in range(n):
                        dve.wait_ge(his, c + 1)
                        nc.vector.tensor_tensor(dst[:, c, 1, :], src[:, c, :], dst[:, c, 0, :].bitcast(F32), ALU.subtract)

        def copy_into(dst):
            def f(act, m, s, p):
                nc.scalar.activation(dst[:, bass.ds(m, 1), 0:SAMPLE].rearrange("p a t -> p (a t)"), s, ACT.Copy)
                return nc.scalar.activation(dst[:, bass.ds(m, 1), SAMPLE:TOK].rearrange("p a t -> p (a t)"), p, ACT.Copy)
            return f

        def add_gated(gate):
            def f(dve, m, s, p):
                for k, src, a, b in ((0, s, 0, SAMPLE), (1, p, SAMPLE, TOK)):
                    x = xT[:, bass.ds(m, 1), a:b].rearrange("p a t -> p (a t)")
                    last = nc.vector.scalar_tensor_tensor(
                        x, in0=src, scalar=mods[:, bass.ds(m + gate * NCH, 1), k:k + 1].rearrange("p a k -> p (a k)"),
                        in1=x, op0=ALU.mult, op1=ALU.add)
                return last
            return f

        with nc.Block() as block:
            @block.sync
            def _(sp):
                sp.dma_start(cols[:, :], cols_d).then_inc(consts_loaded, 16)
                sp.dma_start(rows[:, :], rows_d).then_inc(consts_loaded, 16)
                sp.dma_start(masks[:, :, :], masks_d).then_inc(consts_loaded, 16)
                for k in range(2):
                    load_half(sp, k, k * HALF_RING)
                sp.dma_start(xT[:, :, :], xin).then_inc(x_loaded, 16)
                sp.wait_ge(consts_loaded, 48)
                sp.wait_ge(x_loaded, 16)

            @block.vector
            def _(dve):
                nc.vector.memset(eps[:, :], EPS)

        def even_mixer():
            with ExitStack() as ph:
                pT = sb("pT", [P, N_EVEN_IN, TOK], into=ph)
                with ExitStack() as h_life:
                    h2 = sb("h2_even", [P, NCH, 2, TOK], F32R, into=h_life)
                    norm_modulate("m0", h2, scale_of(scale_mix), shift_of(SH1), split=True)
                    project_split("even_in", N_EVEN_IN, h2, copy_halves(pT))
                between = ExitStack()
                dft = sb("dft", [P, 2 * SAMPLE_TILES * SAMPLE + 4 * P], into=between)
                dft_loaded = sem("dft_loaded")
                cos_t = dft[:, 0:2048].rearrange("p (t u) -> p t u", u=SAMPLE)
                sin_t = dft[:, 2048:4096].rearrange("p (t u) -> p t u", u=SAMPLE)
                both_c = dft[:, 4096:4096 + 256]
                cos_p, sin_p = dft[:, 4352:4480], dft[:, 4480:4608]
                by_c = sb("by_c", [P, TILES, GROUPS, 2 * P], into=between)
                PADDED = 8 * (GRID_W + 2) + PROMPT + 2
                upad = sb("upad", [P, 2, PADDED], into=between)
                conv = sb("conv", [P, 2, PADDED], into=between)
                banks = ExitStack()
                pc = [pb(f"pc{j}", into=banks) for j in range(2)]
                pf = [pb(f"pf{j}", into=banks) for j in range(2)]
                pfp = [pb(f"pfp{j}", into=banks) for j in range(2)]
                chan_done, chan_used, pos_done, pos_free = (sem(n) for n in ("chan_done", "chan_used", "pos_done", "pos_free"))
                with nc.Block() as block:
                    @block.sync
                    def _(sp):
                        sp.dma_start(dft[:, :], dft_d).then_inc(dft_loaded, 16)

                    @block.tensor
                    def _(pe):
                        pe.wait_ge(dft_loaded, 16)
                        n = 0
                        for t in range(TILES):
                            for g in range(0, GROUPS, 2):
                                if n >= 2:
                                    pe.wait_ge(chan_used, n - 1)
                                for k in range(2):
                                    last = nc.tensor.matmul(pc[n % 2][:, 256 * k:256 * k + 256],
                                                            lhsT=pT[:, g + k, t * P:(t + 1) * P], rhs=both_c,
                                                            start=True, stop=True)
                                last.then_inc(chan_done, 1)
                                n += 1
                        pe.wait_ge(chan_used, n)
                        for g in range(GROUPS):
                            if g >= 2:
                                pe.wait_ge(pos_free, g - 1)
                            for t in range(SAMPLE_TILES):
                                nc.tensor.matmul(pf[g % 2][:, :], lhsT=by_c[:, t, g, 0:P], rhs=cos_t[:, t, :],
                                                 start=t == 0, stop=False)
                                nc.tensor.matmul(pf[g % 2][:, :], lhsT=by_c[:, t, g, P:2 * P], rhs=sin_t[:, t, :],
                                                 start=False, stop=t == SAMPLE_TILES - 1)
                            nc.tensor.matmul(pfp[g % 2][:, 0:P], lhsT=by_c[:, SAMPLE_TILES, g, 0:P], rhs=cos_p,
                                             start=True, stop=False)
                            nc.tensor.matmul(pfp[g % 2][:, 0:P], lhsT=by_c[:, SAMPLE_TILES, g, P:2 * P], rhs=sin_p,
                                             start=False, stop=True).then_inc(pos_done, 1)

                    @block.scalar
                    def _(act):
                        n = 0
                        for t in range(TILES):
                            for g in range(0, GROUPS, 2):
                                act.wait_ge(chan_done, n + 1)
                                nc.scalar.activation(by_c[:, t, g:g + 2, :].rearrange("p g c -> p (g c)"), pc[n % 2][:, :],
                                                     ACT.Copy).then_inc(chan_used, 1)
                                n += 1
                        for g in range(GROUPS):
                            act.wait_ge(pos_done, g + 1)
                            nc.scalar.activation(pT[:, g, 0:SAMPLE], pf[g % 2][:, :], ACT.Copy)
                            nc.scalar.activation(pT[:, g, SAMPLE:TOK], pfp[g % 2][:, 0:P], ACT.Copy).then_inc(pos_free, 1)

                    @block.vector
                    def _(dve):
                        dve_steps.did(nc.vector.memset(upad[:, :, :], 0.0))
                        dve_steps.settle(dve)
                        for j in range(4):
                            u, v = upad[:, j % 2, :], conv[:, j % 2, :]
                            us = grid(u)
                            dve_steps.did(nc.vector.tensor_tensor(
                                us, pT[:, 8 + j, 0:SAMPLE].rearrange("p (r w) -> p r w", w=GRID_W),
                                pT[:, 12 + j, 0:SAMPLE].rearrange("p (r w) -> p r w", w=GRID_W), ALU.mult))
                            dve_steps.did(nc.vector.tensor_tensor(row_p(u), pT[:, 8 + j, SAMPLE:TOK],
                                                                  pT[:, 12 + j, SAMPLE:TOK], ALU.mult))
                            dve_steps.settle(dve)
                            conv3(dve, v, u, lambda k: col("even_conv_w", 3 * j + k, 3 * j + k + 1))
                            for dst, src in ((pT[:, 4 + j, 0:SAMPLE].rearrange("p (r w) -> p r w", w=GRID_W), grid(v)),
                                             (pT[:, 4 + j, SAMPLE:TOK], row_p(v))):
                                dve_steps.did(nc.vector.tensor_tensor(dst, dst, src, ALU.mult))
                banks.close()
                between.close()
                y2 = sb("y2_even", [P, NCH, 2, TOK], F32R, into=ph)
                split_into(y2, pT, NCH)
                project_split("even_out", N_EVEN_OUT, y2, add_gated_halves(G1))

        def grid(u):
            return u[:, 0:8 * (GRID_W + 2)].rearrange("p (r w) -> p r w", w=GRID_W + 2)[:, :, 1:GRID_W + 1]

        def row_p(u):
            return u[:, 8 * (GRID_W + 2) + 1:8 * (GRID_W + 2) + 1 + PROMPT]

        def conv3(dve, v, u, w):
            n = 8 * (GRID_W + 2) + PROMPT + 2
            dve_steps.did(nc.vector.tensor_scalar(v[:, 1:n - 1], u[:, 1:n - 1], w(1), None, ALU.mult))
            for k, shift in ((0, 0), (2, 2)):
                dve_steps.settle(dve)
                dve_steps.did(nc.vector.scalar_tensor_tensor(v[:, 1:n - 1], in0=u[:, shift:n - 2 + shift], scalar=w(k),
                                                             in1=v[:, 1:n - 1], op0=ALU.mult, op1=ALU.add))
            dve_steps.settle(dve)

        def peer(layer):
            tag = f"_p{layer}"
            with ExitStack() as h_life:
                h2 = sb(f"h2{tag}", [P, NCH, 2, TOK], F32R, into=h_life)
                norm_modulate(f"f{layer}", h2, scale_of(scale_ffn), shift_of(SH2), split=True)
                with ExitStack() as ids_life:
                    idT = sb(f"idT{tag}", [P, 3, TOK], into=ids_life)
                    with ExitStack() as ph:
                        qT = sb(f"qT{tag}", [P, N_WQ, TOK], into=ph)
                        project_split(f"q{layer}", N_WQ, h2, copy_halves(qT))
                        keysT = sb(f"keysT{tag}", [P, 2 * PEER_HEADS * KEYS], into=ph)
                        top_keys(layer, tag, ph, qT, keysT, idT)
                    scatter_gates(layer, tag, idT)
                experts(layer, tag, h2)

        def top_keys(layer, tag, ph, qT, keysT, idT):
            H2 = 2 * PEER_HEADS
            sc = sb(f"sc{tag}", [P, H2, KEYS], into=ph)
            best = sb(f"best{tag}", [P, H2, TOPK], into=ph)
            besti = sb(f"besti{tag}", [P, H2, TOPK], U32, into=ph)
            bestf = sb(f"bestf{tag}", [P, H2, TOPK], into=ph)
            idstep = sb(f"idstep{tag}", [P, H2, TOPK], into=ph)
            cand = sb(f"cand{tag}", [P, PEER_HEADS, PAIRS], into=ph)
            top = sb(f"top{tag}", [P, PEER_HEADS, TOPK], into=ph)
            posi = sb(f"posi{tag}", [P, PEER_HEADS, TOPK], U32, into=ph)
            posf = sb(f"posf{tag}", [P, ENTRIES], into=ph)
            start_of = sb(f"start_of{tag}", [P, ENTRIES], into=ph)
            passed = sb(f"passed{tag}", [P, ENTRIES, TOPK], into=ph)
            prod = sb(f"prod{tag}", [P, ENTRIES, TOPK], into=ph)
            found = sb(f"found{tag}", [P, 3, ENTRIES], into=ph)
            total = sb(f"total{tag}", [P, PEER_HEADS], into=ph)
            ps = [pb(f"pk{tag}{j}", into=ph) for j in range(4)]
            pt = pb(f"pt{tag}", into=ph)
            batches_begun = sem(f"batches_begun{tag}")
            (keys_loaded, scores_done, scores_copied, sc_free, exp_in, exp_out, found_ready, turned, turned_out) = (
                sem(f"{n}{tag}") for n in ("keys_loaded", "scores_done", "scores_copied", "sc_free", "exp_in",
                                           "exp_out", "found_ready", "turned", "turned_out"))
            with nc.Block() as block:
                @block.sync
                def _(sp):
                    sp.dma_start(keysT[:, :], keys[layer]).then_inc(keys_loaded, 16)

                @block.tensor
                def _(pe):
                    pe.wait_ge(keys_loaded, 16)
                    def turn(t):
                        pe.wait_ge(found_ready, t + 1)
                        if t >= 1:
                            pe.wait_ge(turned_out, t)
                        for k in range(3):
                            last = nc.tensor.transpose(pt[:, k * P:(k + 1) * P], found[:, k, :], masks[:, IDENT, :])
                        last.then_inc(turned, 1)

                    for t in range(TILES):
                        for b in range(4):
                            if t:
                                pe.wait_ge(scores_copied, 4 * (t - 1) + b + 1)
                            for q in range(4):
                                hz = 4 * b + q
                                last = nc.tensor.matmul(ps[b][:, q * KEYS:(q + 1) * KEYS],
                                                        lhsT=qT[:, hz, t * P:(t + 1) * P],
                                                        rhs=keysT[:, hz * KEYS:(hz + 1) * KEYS], start=True, stop=True)
                            last.then_inc(scores_done, 1)
                        if t:
                            turn(t - 1)
                    turn(TILES - 1)

                @block.scalar
                def _(act):
                    with act.Fori(0, TILES) as t:
                        act.wait_ge(sc_free, t + 1)
                        for b in range(4):
                            act.wait_ge(scores_done, t * 4 + (b + 1))
                            nc.scalar.activation(sc[:, 4 * b:4 * b + 4, :].rearrange("p h k -> p (h k)"), ps[b][:, :],
                                                 ACT.Copy).then_inc(scores_copied, 1)
                        act.wait_ge(exp_in, t + 1)
                        nc.scalar.activation(found[:, 2, :], found[:, 2, :], ACT.Exp).then_inc(exp_out, 1)
                        act.wait_ge(turned, t + 2)
                        nc.scalar.activation(idT[:, :, bass.ds(t * P, P)], pt[:, 0:3 * P].rearrange("p (k n) -> p k n", k=3),
                                             ACT.Copy).then_inc(turned_out, 1)

                @block.vector
                def _(dve):
                    v = nc.vector

                    def best8(ins_of, n):
                        dve_steps.settle(dve)
                        dve.sem_inc(batches_begun, 1)
                        for j in range(n):
                            dve_steps.did(ins_of(j))

                    dve.sem_inc(sc_free, 1)
                    dve.sem_inc(turned, 1)
                    H = PEER_HEADS
                    steps = 5 * H2 + 2 + 9 + 5 * H + 12
                    with dve_steps.loop(dve, TILES, steps) as t:
                        dve.wait_ge(scores_copied, t * 4 + 4)
                        best8(lambda j: v.max(best[:, j, 0:8], sc[:, j, :]), H2)
                        best8(lambda j: v.max_index(besti[:, j, 0:8], best[:, j, 0:8], sc[:, j, :]), H2)
                        best8(lambda j: v.match_replace(sc[:, j, :], best[:, j, 0:8], sc[:, j, :], NEG), H2)
                        best8(lambda j: v.max(best[:, j, 8:16], sc[:, j, :]), H2)
                        best8(lambda j: v.max_index(besti[:, j, 8:16], best[:, j, 8:16], sc[:, j, :]), H2)
                        dve_steps.settle(dve)
                        v.tensor_copy(bestf[:, :, :], besti[:, :, :]).then_inc(sc_free, 1)
                        dve.wait_ge(sc_free, t + 2)
                        dve_steps.did(v.tensor_copy(idstep[:, :, 0:1], bestf[:, :, 0:1]))
                        dve_steps.did(v.tensor_tensor(idstep[:, :, 1:TOPK], bestf[:, :, 1:TOPK], bestf[:, :, 0:TOPK - 1],
                                                      ALU.subtract))
                        bz = best[:, :, :].rearrange("p (h z) k -> p h z k", z=2)
                        for i in range(8):
                            n = PAIRS_OF[i]
                            dve_steps.did(v.tensor_tensor(
                                cand[:, :, PAIR_AT[i]:PAIR_AT[i] + n],
                                bz[:, :, 0, i:i + 1].broadcast_to([P, H, n]), bz[:, :, 1, 0:n], ALU.add))
                        dve_steps.did(v.tensor_tensor(cand[:, :, PAIR_AT[8]:PAIRS], bz[:, :, 0, 8:16],
                                                      bz[:, :, 1, 0:1].broadcast_to([P, H, 8]), ALU.add))
                        best8(lambda j: v.max(top[:, j, 0:8], cand[:, j, :]), H)
                        best8(lambda j: v.max_index(posi[:, j, 0:8], top[:, j, 0:8], cand[:, j, :]), H)
                        best8(lambda j: v.match_replace(cand[:, j, :], top[:, j, 0:8], cand[:, j, :], NEG), H)
                        best8(lambda j: v.max(top[:, j, 8:16], cand[:, j, :]), H)
                        best8(lambda j: v.max_index(posi[:, j, 8:16], top[:, j, 8:16], cand[:, j, :]), H)
                        dve_steps.settle(dve)
                        dve.wait_ge(turned, t + 1)
                        f3 = lambda k: found[:, k, :].rearrange("p (h r) -> p h r", h=H)
                        dve_steps.did(v.tensor_copy(posf[:, :].rearrange("p (h r) -> p h r", h=H), posi[:, :, :]))
                        v.tensor_tensor(f3(2), top[:, :, :], top[:, :, 0:1].broadcast_to([P, H, TOPK]),
                                        ALU.subtract).then_inc(exp_in, 1)

                        def ranks(table):
                            return bcast(table, 1, ENTRIES)

                        def lookup(dst, steps_of):
                            dve_steps.settle(dve)
                            dve_steps.did(v.tensor_tensor(
                                prod[:, :, :].rearrange("p (h r) m -> p h r m", h=H),
                                passed[:, :, :].rearrange("p (h r) m -> p h r m", h=H), steps_of, ALU.mult))
                            dve_steps.settle(dve)
                            dve_steps.did(v.tensor_reduce(dst, prod[:, :, :], AX.X, ALU.add))

                        dve_steps.settle(dve)
                        dve_steps.did(v.tensor_tensor(passed[:, :, :], bcast(posf[:, :], 2, TOPK), ranks(row("pair_at")), ALU.is_ge))
                        lookup(start_of[:, :], bcast(bcast(row("pairs_before"), 1, TOPK), 1, H))
                        iz = idstep[:, :, :].rearrange("p (h z) k -> p h z k", z=2)
                        lookup(found[:, 0, :], bcast(iz[:, :, 0, :], 2, TOPK))
                        dve_steps.settle(dve)
                        dve_steps.did(v.tensor_tensor(posf[:, :], posf[:, :], start_of[:, :], ALU.subtract))
                        dve_steps.settle(dve)
                        dve_steps.did(v.tensor_tensor(passed[:, :, :], bcast(posf[:, :], 2, TOPK), ranks(row("rank")), ALU.is_ge))
                        lookup(found[:, 1, :], bcast(iz[:, :, 1, :], 2, TOPK))
                        dve.wait_ge(exp_out, t + 1)
                        dve_steps.did(v.tensor_reduce(total[:, :], f3(2), AX.X, ALU.add))
                        dve_steps.settle(dve)
                        dve_steps.did(v.reciprocal(total[:, :], total[:, :]))
                        dve_steps.settle(dve)
                        v.tensor_tensor(f3(2), f3(2), bcast(total[:, :], 2, TOPK), ALU.mult).then_inc(found_ready, 1)

        def scatter_gates(layer, tag, idT):
            HALF = 8
            PIECES = TOK // SCATTER_TOK
            ROUNDS = SCATTER_TOK // (2 * HALF)
            with ExitStack() as ph:
                staged = sb(f"staged{tag}", [P, 2, KEYS, SCATTER_TOK], into=ph)
                hot1 = sb(f"hot1{tag}", [P, 2, HALF, KEYS], into=ph)
                hot2 = sb(f"hot2{tag}", [P, 2, HALF, KEYS], into=ph)
                ps = [pb(f"pg{tag}{j}", into=ph) for j in range(4)]
                diff_ready, hots_ready, hots_used, g_copied = (
                    sem(f"{n}{tag}") for n in ("diff_ready", "hots_ready", "hots_used", "g_copied"))
                staged_free = [sem(f"staged_free{tag}{j}") for j in range(2)]
                iota = bcast(row("iota"), 1, HALF)

                def entries(r, i, half):
                    return bcast(idT[:, r, bass.ds(i * 2 * HALF + half * HALF, HALF)], 2, KEYS)

                with nc.Block() as block:
                    @block.vector
                    def _(dve):
                        with dve.Fori(0, TOK // (2 * HALF)) as i:
                            for half in range(2):
                                dve.wait_ge(hots_used, i * 2 + (half + 1))
                                nc.vector.tensor_tensor(hot2[:, half, :, :], iota, entries(1, i, half), ALU.is_equal)
                                dve.wait_ge(diff_ready, i * 2 + (half + 1))
                                hot = hot1[:, half, :, :]
                                nc.vector.scalar_tensor_tensor(hot, in0=hot, scalar=0.0, in1=entries(2, i, half),
                                                               op0=ALU.is_equal, op1=ALU.mult).then_inc(hots_ready, 1)

                    @block.gpsimd
                    def _(pool):
                        pool.sem_inc(hots_used, 2)
                        with pool.Fori(0, TOK // (2 * HALF)) as i:
                            for half in range(2):
                                pool.wait_ge(hots_used, i * 2 + (half + 1))
                                nc.gpsimd.tensor_tensor(hot1[:, half, :, :], iota, entries(0, i, half),
                                                        ALU.subtract).then_inc(diff_ready, 1)

                    @block.tensor
                    def _(pe):
                        with pe.Fori(0, TOK // (2 * HALF)) as i:
                            for half in range(2):
                                pe.wait_ge(hots_ready, i * 2 + (half + 1))
                                for q in range(2):
                                    b = 2 * half + q
                                    pe.wait_ge(g_copied, i * 4 + (b + 1))
                                    for j in range(4):
                                        k = q * 4 + j
                                        last = nc.tensor.matmul(ps[b][:, j * P:(j + 1) * P], lhsT=hot2[:, half, k, :],
                                                                rhs=hot1[:, half, k, :], start=True, stop=True)
                                last.then_inc(hots_used, 1)

                    @block.scalar
                    def _(act):
                        act.sem_inc(g_copied, 4)
                        with act.Fori(0, PIECES // 2) as w:
                            for buf in range(2):
                                act.wait_ge(staged_free[buf], w * 16 + 16)
                                with act.Fori(0, ROUNDS) as r:
                                    for half in range(2):
                                        act.wait_ge(hots_used, w * (4 * ROUNDS) + r * 2 + (buf * 2 * ROUNDS + half + 3))
                                        for q in range(2):
                                            b = 2 * half + q
                                            nc.scalar.activation(staged[:, buf, :, bass.ds(r * 16 + 4 * b, 4)],
                                                                 ps[b][:, :].rearrange("p (t i) -> p i t", t=4),
                                                                 ACT.Copy).then_inc(g_copied, 1)

                    @block.sync
                    def _(sp):
                        for buf in range(2):
                            sp.sem_inc(staged_free[buf], 16)
                        with sp.Fori(0, PIECES // 2) as w:
                            for buf in range(2):
                                sp.wait_ge(g_copied, w * (8 * ROUNDS) + ((buf + 1) * 4 * ROUNDS + 4))
                                sp.dma_start(gates_dram[w * 2 + buf], staged[:, buf, :, :]).then_inc(staged_free[buf], 16)
                        for buf in range(2):
                            sp.wait_ge(staged_free[buf], (PIECES // 2 + 1) * 16)

        def experts(layer, tag, h2):
            first = take(N_PEER)
            NB = BLOCKS_PER_GROUP
            NGROUPS = EXPERT_BLOCKS // NB
            ROUND0 = first // SLOTS
            more = at[0] < N_BLOCKS
            with ExitStack() as ph:
                wide_u = sb(f"wide_u{tag}", [P, 2, 2, 1024], F32R, into=ph)
                wide_v = sb(f"wide_v{tag}", [P, NB, 2, 1024], F32R, into=ph)
                acts = sb(f"acts{tag}", [P, NB, 2, TOK], F32R, into=ph)
                gelu = sb(f"gelu{tag}", [P, 2, TOK], into=ph)
                gbuf = sb(f"gbuf{tag}", [P, 2, TOK // SCATTER_TOK, 2, SCATTER_TOK], into=ph)
                by_piece = lambda ap: ap.rearrange("p (w t) -> p w t", t=SCATTER_TOK)
                hs = [[pb(f"hs{tag}{j}{h}", into=ph) for h in range(2)] for j in range(2)]
                outs = [[pb(f"os{tag}{j}{h}", into=ph) for h in range(2)] for j in range(2)]
                his_done, u_split, v_split, h_done, gelu_done, acts_done, outs_done, outs_free = (
                    sem(f"{n}{tag}") for n in ("his_done", "u_split", "v_split", "h_done", "gelu_done", "acts_done",
                                               "outs_done", "outs_free"))
                gates_in = [sem(f"gates_in{tag}{j}") for j in range(2)]

                def groups(eng, body):
                    with eng.Fori(0, NGROUPS - 1) as g:
                        body(g, False)
                    body(NGROUPS - 1, True)

                with nc.Block() as block:
                    @block.sync
                    def _(sp):
                        def load_gates(j, block_):
                            sp.dma_start(gbuf[:, j, :, :, :].rearrange("p w b t -> p w (b t)"),
                                         gates_dram[:, :, bass.ds(block_, 2), :].rearrange("w p b t -> p w (b t)"))\
                              .then_inc(gates_in[j], 16)

                        def group(g, last):
                            def ring_half(k, split):
                                if last and not more:
                                    return
                                sp.wait_ge(split, g * NB + NB)
                                load_half(sp, k, g * SLOTS + (first + SLOTS + k * HALF_RING))

                            for k, split in ((0, u_split), (1, v_split)):
                                ring_half(k, split)
                                if not last:
                                    sp.wait_ge(acts_done, g * NB + (2 * k + 4))
                                    load_gates(k, g * NB + (NB + 2 * k))

                        for j in range(2):
                            load_gates(j, 2 * j)
                        groups(sp, group)
                        sp.wait_ge(v_split, EXPERT_BLOCKS)
                        sp.wait_ge(u_split, EXPERT_BLOCKS)
                        sp.sem_inc(blocks_used, N_PEER)

                    def split_order(hi_or_lo_u, hi_or_lo_v, g, last, before=lambda e: None):
                        for e, of_v in enumerate(((0, 1), (2,), (3,), ())):
                            before(e)
                            if e < 2:
                                hi_or_lo_u(g, e + 2)
                            for v in of_v:
                                hi_or_lo_v(g, v)
                            if e >= 2 and not last:
                                hi_or_lo_u(g, e + 2)

                    @block.scalar
                    def _(act):
                        act.sem_inc(gelu_done, 2)

                        def hi_u(g, e):
                            if e % NB == 0:
                                act.wait_ge(half_loaded[0], (g + (ROUND0 + e // NB + 1)) * 16)
                            nc.scalar.activation(wide_u[:, e % 2, 0, :], ring[:, e % NB, :], ACT.Copy).then_inc(his_done, 1)

                        def hi_v(g, e):
                            if e == 0:
                                act.wait_ge(half_loaded[1], (g + (ROUND0 + 1)) * 16)
                            nc.scalar.activation(wide_v[:, e, 0, :], ring[:, NB + e, :], ACT.Copy).then_inc(his_done, 1)

                        def group(g, last):
                            def gelus(e):
                                act.wait_ge(h_done, g * NB + (e + 1))
                                act.wait_ge(acts_done, g * NB + (e + 1))
                                for h in range(2):
                                    ins = nc.scalar.activation(gelu[:, e % 2, HALVES[h]], hs[e % 2][h][:, 0:HALF_TOK], ACT.Gelu)
                                ins.then_inc(gelu_done, 1)
                            split_order(hi_u, hi_v, g, last, gelus)

                        hi_u(0, 0)
                        hi_u(0, 1)
                        groups(act, group)

                    @block.gpsimd
                    def _(pool):
                        def lo(dst, slot, n, done):
                            pool.wait_ge(his_done, n)
                            nc.gpsimd.tensor_tensor(dst[:, 1, :], ring[:, slot, :], dst[:, 0, :].bitcast(F32),
                                                    ALU.subtract).then_inc(done, 1)

                        def group(g, last):
                            n = [2]

                            def lo_u(g, e):
                                n[0] += 1
                                lo(wide_u[:, e % 2, :, :], e % NB, g * (2 * NB) + n[0], u_split)

                            def lo_v(g, e):
                                n[0] += 1
                                lo(wide_v[:, e, :, :], NB + e, g * (2 * NB) + n[0], v_split)

                            split_order(lo_u, lo_v, g, last)

                        for e in range(2):
                            lo(wide_u[:, e, :, :], e, e + 1, u_split)
                        groups(pool, group)

                    @block.tensor
                    def _(pe):
                        with pe.Fori(0, NGROUPS) as g:
                            for e in range(NB):
                                pe.wait_ge(u_split, g * NB + (e + 1))
                                pe.wait_ge(gelu_done, g * NB + (e + 1))
                                for c in range(NCH):
                                    last = split_matmuls(hs[e % 2], wide_u[:, e % 2, 0, c * P:(c + 1) * P],
                                                         wide_u[:, e % 2, 1, c * P:(c + 1) * P], h2, c, c == 0, c == NCH - 1)
                                last.then_inc(h_done, 1)
                            order = [(d, e) for d in (0, 1) for e in range(NB - 1)] + [(0, NB - 1), (1, NB - 1)]
                            order += [(d, e) for d in range(2, NCH) for e in range(NB)]
                            for d, e in order:
                                if e == 0:
                                    pe.wait_ge(outs_free, g * NCH + (d + 1))
                                if d == 0:
                                    pe.wait_ge(v_split, g * NB + (e + 1))
                                    pe.wait_ge(acts_done, g * NB + (e + 3))
                                last = split_matmuls(outs[d % 2], wide_v[:, e, 0, d * P:(d + 1) * P],
                                                     wide_v[:, e, 1, d * P:(d + 1) * P], acts, e, e == 0, e == NB - 1)
                                if e == NB - 1:
                                    last.then_inc(outs_done, 1)

                    @block.vector
                    def _(dve):
                        dve.sem_inc(acts_done, 2)
                        dve.sem_inc(outs_free, 2)
                        with dve_steps.loop(dve, NGROUPS, 2 * NB) as g:
                            for e in range(NB):
                                if e % 2 == 0:
                                    dve.wait_ge(gates_in[e // 2], g * 16 + 16)
                                dve.wait_ge(gelu_done, g * NB + (e + 3))
                                a = gelu[:, e % 2, :]
                                dve_steps.did(nc.vector.tensor_tensor(by_piece(a), by_piece(a), gbuf[:, e // 2, :, e % 2, :],
                                                                      ALU.mult))
                                dve_steps.settle(dve)
                                dve_steps.did(nc.vector.tensor_copy(acts[:, e, 0, :], a))
                                dve_steps.settle(dve)
                                nc.vector.tensor_tensor(acts[:, e, 1, :], a, acts[:, e, 0, :].bitcast(F32),
                                                        ALU.subtract).then_inc(acts_done, 1)
                            for d in range(NCH):
                                dve.wait_ge(outs_done, g * NCH + (d + 1))
                                for k, part, h, at_ in PARTS:
                                    last = nc.vector.scalar_tensor_tensor(
                                        xT[:, d, part], in0=outs[d % 2][h][:, at_], scalar=mods[:, G2 * NCH + d, k:k + 1],
                                        in1=xT[:, d, part], op0=ALU.mult, op1=ALU.add)
                                last.then_inc(outs_free, 1)

        def ssd_mixer():
            with ExitStack() as ph:
                Y = sb("Y", [P, TILES, SSM_INNER], into=ph)
                with ExitStack() as h_life:
                    hT = sb("hT", [P, NCH, TOK], into=h_life)
                    norm_modulate("m1", hT, scale_of(scale_mix), shift_of(SH1))
                    ssd_scan(Y, hT)
                    gate_by_z(Y, hT)
                yT = sb("yT", [P, SSM_INNER // P, TOK], into=ph)
                norm_y(Y, yT)
                project("ssd_out", N_SSD_OUT, yT, add_gated(G1), dve_evac=True, chunks=2 * NCH)

        def ssd_scan(Y, hT):
            first = take(N_SSD)
            with ExitStack() as ph:
                W64 = 2 * HEADS
                wdt_s = sb("wdt_s", [P, NCH, W64], into=ph)
                dt = sb("dt", [P, TILES, W64], into=ph)
                dA = sb("dA", [P, TILES, W64], into=ph)
                t1 = sb("dt_t1", [P, TILES, W64], into=ph)
                t2 = sb("dt_t2", [P, TILES, W64], into=ph)
                t3 = sb("dt_t3", [P, TILES, W64], into=ph)
                negA = sb("negA", [P, W64], into=ph)
                decay = sb("decay", [P, TILES, 6 * HEADS], into=ph)
                IN_F, OUT_F, IN_B, OUT_B, ALL_F, ALL_B = (HEADS * k for k in range(6))
                state_w = sb("state_w", [P, TILES, W64], into=ph)
                with ExitStack() as pp:
                    pdt = pb("pdt", into=pp)
                    pdec = [pb(f"pdec{j}", into=pp) for j in range(TILES)]
                    wdt_loaded, dt_done, dt_act, dA_done, dec_done, dec_exp = (
                        sem(n) for n in ("wdt_loaded", "dt_done", "dt_act", "dA_done", "dec_done", "dec_exp"))
                    with nc.Block() as block:
                        @block.sync
                        def _(sp):
                            sp.dma_start(wdt_s[:, :, :], wdt).then_inc(wdt_loaded, 16)

                        @block.tensor
                        def _(pe):
                            pe.wait_ge(wdt_loaded, 16)
                            for t in range(TILES):
                                for c in range(NCH):
                                    last = nc.tensor.matmul(pdt[:, t * W64:(t + 1) * W64], lhsT=hT[:, c, t * P:(t + 1) * P],
                                                            rhs=wdt_s[:, c, :], start=c == 0, stop=c == NCH - 1)
                            last.then_inc(dt_done, 1)
                            pe.wait_ge(dA_done, 1)
                            for t in range(TILES):
                                f, b = dA[:, t, 0:HEADS], dA[:, t, HEADS:W64]
                                for at_, m, rhs in ((IN_F, LE, f), (OUT_F, GT, f), (IN_B, GE, b), (OUT_B, LT, b),
                                                    (ALL_F, ONES, f), (ALL_B, ONES, b)):
                                    last = nc.tensor.matmul(pdec[t][:, at_:at_ + HEADS], lhsT=masks[:, m, :], rhs=rhs,
                                                            start=True, stop=True)
                            last.then_inc(dec_done, 1)

                        @block.scalar
                        def _(act):
                            nc.scalar.activation(negA[:, :], row("a_log"), ACT.Exp).then_inc(dt_act, 1)
                            act.wait_ge(dt_act, 2)
                            nc.scalar.activation(t2[:, :, :], t2[:, :, :], ACT.Exp).then_inc(dt_act, 1)
                            act.wait_ge(dt_act, 4)
                            nc.scalar.activation(t3[:, :, :], t1[:, :, :], ACT.Ln).then_inc(dt_act, 1)
                            act.wait_ge(dec_done, 1)
                            for t in range(TILES):
                                nc.scalar.activation(decay[:, t, :], pdec[t][:, 0:6 * HEADS], ACT.Exp).then_inc(dec_exp, 1)

                        @block.vector
                        def _(dve):
                            v = nc.vector

                            def step(ins):
                                dve_steps.did(ins)
                                dve_steps.settle(dve)

                            dve.wait_ge(dt_done, 1)
                            step(v.tensor_tensor(dt[:, :, :], pdt[:, 0:TILES * W64].rearrange("p (t h) -> p t h", t=TILES),
                                                 bcast(row("dt_bias"), 1, TILES), ALU.add))
                            dve.wait_ge(dt_act, 1)
                            v.scalar_tensor_tensor(t2[:, :, :], in0=dt[:, :, :], scalar=-1.0, in1=dt[:, :, :],
                                                   op0=ALU.mult, op1=ALU.min).then_inc(dt_act, 1)
                            step(v.tensor_scalar(dt[:, :, :], dt[:, :, :], 0.0, None, ALU.max))
                            dve.wait_ge(dt_act, 3)
                            v.tensor_scalar(t1[:, :, :], t2[:, :, :], 1.0, None, ALU.add).then_inc(dt_act, 1)
                            dve.wait_ge(dt_act, 5)
                            step(v.tensor_scalar(dA[:, :, :], t1[:, :, :], 1.0, None, ALU.is_equal))
                            step(v.scalar_tensor_tensor(t1[:, :, :], in0=t1[:, :, :], scalar=-1.0, in1=dA[:, :, :],
                                                        op0=ALU.add, op1=ALU.add))
                            step(v.tensor_tensor(t3[:, :, :], t3[:, :, :], dA[:, :, :], ALU.add))
                            step(v.reciprocal(t1[:, :, :], t1[:, :, :]))
                            step(v.tensor_tensor(t3[:, :, :], t3[:, :, :], t2[:, :, :], ALU.mult))
                            step(v.tensor_tensor(t3[:, :, :], t3[:, :, :], t1[:, :, :], ALU.mult))
                            step(v.tensor_tensor(dt[:, :, :], dt[:, :, :], t3[:, :, :], ALU.add))
                            v.scalar_tensor_tensor(dA[:, :, :], in0=dt[:, :, :], scalar=-1.0,
                                                   in1=bcast(negA[:, :], 1, TILES), op0=ALU.mult, op1=ALU.mult).then_inc(dA_done, 1)
                            dve.wait_ge(dec_exp, TILES)
                            v.tensor_tensor(state_w[:, :, 0:HEADS], dt[:, :, 0:HEADS], decay[:, :, OUT_F:OUT_F + HEADS], ALU.mult)
                            v.tensor_tensor(state_w[:, :, HEADS:W64], dt[:, :, HEADS:W64], decay[:, :, OUT_B:OUT_B + HEADS], ALU.mult)
                scan_groups(Y, hT, first, dt, dA, decay, state_w)

        SSM_BLOCK = [lambda g: g * 2, lambda g: g * 2 + 1, lambda g: g + 16, lambda g: g + 24]

        def scan_groups(Y, hT, first, dt, dA, decay, state_w):
            IN_F, OUT_F, IN_B, OUT_B, ALL_F, ALL_B = (HEADS * k for k in range(6))
            LAST = SAMPLE_TILES - 1
            BF, CF = 2, 3
            with ExitStack() as ph:
                PADDED = 8 * (GRID_W + 2) + PROMPT + 2
                upad = sb("su", [P, 2, PADDED], into=ph)
                conv = sb("sv", [P, 2, PADDED], into=ph)
                chan = sb("chan", [P, 4, TOK], into=ph)
                tokm = sb("tokm", [P, TILES, 3 * P], into=ph)
                xdt = sb("xdt", [P, 2, GW], into=ph)
                xw = sb("xw", [P, 2, GW], into=ph)
                xD = sb("xD", [P, GW], into=ph)
                spans = sb("spans", [P, 2, HPG, P], into=ph)
                E = sb("E", [P, HPG, P], into=ph)
                CBm = sb("CBm", [P, 2, P], into=ph)
                mix = sb("mix", [P, 2, HPG, P], into=ph)
                off = sb("off", [P, 2, GW], into=ph)
                init = sb("init", [P, 2, GW], into=ph)
                SF = sb("SF", [P, SAMPLE_TILES, GW], into=ph)
                SB = sb("SB", [P, SAMPLE_TILES, GW], into=ph)
                last_s = sb("last_s", [P, 2, GW], into=ph)
                ps = [pb(f"gs{j}", into=ph) for j in range(2)]
                p_seg = pb("p_seg", into=ph)
                p_cb = pb("p_cb", into=ph)
                p_y = pb("p_y", into=ph)
                p_off = pb("p_off", into=ph)
                p_st = pb("p_st", into=ph)
                pq = [p_cb, p_y]
                p_t = ps[0]
                S = {n: sem("scan_" + n) for n in (
                    "init_in", "copied", "conved", "silued", "turned", "turned_out", "weighted", "spanned",
                    "seg", "exped", "cb", "cb_used", "mixed", "y", "y_used", "off", "st", "st_used", "states",
                    "final", "final_out", "last_free", "dma_turns")}
                GPR = 2
                with nc.Block() as block:
                    @block.sync
                    def _(sp):
                        feed(sp, first, N_SSD)

                    @block.gpsimd
                    def _(pool):
                        p = nc.gpsimd
                        pool.sem_inc(S["last_free"], 1)
                        pool.sem_inc(S["exped"], 1)
                        with pool.Fori(0, SSM_GROUPS) as g:
                            pool.wait_ge(S["y_used"], g * TILES + 1)
                            pool.sem_inc(S["dma_turns"], 1)
                            pool.dma_start(init[:, :, :], state_in[g]).then_inc(S["init_in"], 16)
                            for t in range(TILES):
                                pool.wait_ge(S["seg"], g * TILES + (t + 1))
                                for d, m in ((0, GT), (1, LT)):
                                    last = p.tensor_tensor(
                                        spans[:, d, :, :], bcast(masks[:, m, :], 1, HPG),
                                        bcast(dA[:, t, bass.ds(g * HPG + d * HEADS, HPG)], 2, P), ALU.mult)
                                last.then_inc(S["spanned"], 1)
                            pool.wait_ge(S["final"], g + 1)
                            pool.sem_inc(S["dma_turns"], 1)
                            pool.dma_start(state_out[g], last_s[:, :, :]).then_inc(S["final_out"], 16)
                            pool.wait_ge(S["final_out"], g * 16 + 16)
                            pool.sem_inc(S["last_free"], 1)

                    @block.tensor
                    def _(pe):
                        mm = nc.tensor.matmul
                        pe.sem_inc(S["seg"], 1)
                        with pe.Fori(0, SSM_GROUPS // GPR) as r:
                            for j in range(GPR):
                                def n(per, k):
                                    return r * (GPR * per) + (j * per + k)
                                for b in range(4):
                                    s = 4 * j + b
                                    loaded(pe, s, r + first // SLOTS)
                                    pe.wait_ge(S["copied"], n(4, b + 1))
                                    if b == 0:
                                        pe.wait_ge(S["turned_out"], n(TILES, 1))
                                        pe.wait_ge(S["cb_used"], n(TILES, 1))
                                        pe.wait_ge(S["y_used"], n(TILES, 1))
                                    for c in range(NCH):
                                        last = pair_matmul(ps[b % 2][:, :], pq[b % 2][:, 0:PROMPT],
                                                           ring[:, s, c * P:(c + 1) * P], hT, c, c == 0, c == NCH - 1)
                                    last.then_inc(blocks_used, 1)
                                pe.wait_ge(S["silued"], n(4, 3))
                                for t in range(TILES):
                                    pe.wait_ge(S["turned_out"], n(TILES, t + 1))
                                    for b in range(3):
                                        last = nc.tensor.transpose(p_t[:, b * P:(b + 1) * P], chan[:, b, t * P:(t + 1) * P],
                                                                   masks[:, IDENT, :])
                                    last.then_inc(S["turned"], 1)
                                k = 0
                                for t, d in [(3, 1), (2, 1), (1, 1), (0, 0), (1, 0), (2, 0), (4, 0), (4, 1)]:
                                    pe.wait_ge(S["weighted"], n(8, k + 1))
                                    pe.wait_ge(S["st_used"], n(8, k + 1))
                                    mm(p_st[:, 0:GW], lhsT=tokm[:, t, 2 * P:3 * P], rhs=xw[:, k % 2, :],
                                       start=True, stop=True).then_inc(S["st"], 1)
                                    k += 1
                                pe.wait_ge(S["silued"], n(4, 4))
                                for t in range(TILES):
                                    tok = slice(t * P, (t + 1) * P)
                                    pe.wait_ge(S["cb_used"], n(TILES, t + 1))
                                    mm(p_cb[:, 0:P], lhsT=chan[:, BF, tok], rhs=chan[:, CF, tok], start=True,
                                       stop=True).then_inc(S["cb"], 1)
                                    pe.wait_ge(S["spanned"], n(TILES, t + 1))
                                    pe.wait_ge(S["exped"], n(TILES, t + 1))
                                    for h in range(HPG):
                                        mm(p_seg[:, h * P:(h + 1) * P], lhsT=spans[:, 0, h, :], rhs=masks[:, LE, :],
                                           start=True, stop=False)
                                        last = mm(p_seg[:, h * P:(h + 1) * P], lhsT=spans[:, 1, h, :],
                                                  rhs=masks[:, GE, :], start=False, stop=True)
                                    last.then_inc(S["seg"], 1)
                                    pe.wait_ge(S["y_used"], n(TILES, t + 1))
                                    if t < SAMPLE_TILES:
                                        pe.wait_ge(S["states"], n(1, 1))
                                        mm(p_off[:, 0:GW], lhsT=chan[:, CF, tok], rhs=SF[:, t, :], start=True, stop=True)
                                        mm(p_off[:, GW:2 * GW], lhsT=chan[:, CF, tok], rhs=SB[:, t, :], start=True,
                                           stop=True).then_inc(S["off"], 1)
                                    pe.wait_ge(S["mixed"], n(TILES, t + 2))
                                    for h in range(HPG):
                                        out = p_y[:, h * HEADDIM:(h + 1) * HEADDIM]
                                        mm(out, lhsT=mix[:, 0, h, :], rhs=xdt[:, 0, h * HEADDIM:(h + 1) * HEADDIM],
                                           start=True, stop=False)
                                        last = mm(out, lhsT=mix[:, 1, h, :], rhs=xdt[:, 1, h * HEADDIM:(h + 1) * HEADDIM],
                                                  start=False, stop=True)
                                    last.then_inc(S["y"], 1)

                    def silu(act, g, b):
                        a = nc.scalar.activation
                        act.wait_ge(S["conved"], g * 4 + (b + 3))
                        blk = SSM_BLOCK[b]
                        bias = cols[:, bass.ds(blk(g) + COL_AT["ssd_conv_b"][0], 1)]
                        v = conv[:, b % 2, :]
                        a(chan[:, b, 0:SAMPLE].rearrange("p (r w) -> p r w", w=GRID_W), grid(v), ACT.Silu, bias=bias)
                        a(chan[:, b, SAMPLE:TOK], row_p(v), ACT.Silu, bias=bias).then_inc(S["silued"], 1)

                    @block.scalar
                    def _(act):
                        a = nc.scalar.activation
                        act.sem_inc(S["copied"], 2)
                        act.sem_inc(S["turned_out"], 1)
                        with act.Fori(0, SSM_GROUPS) as g:
                            for b in range(4):
                                act.wait_ge(blocks_used, g * 4 + (first + b + 1))
                                act.wait_ge(S["conved"], g * 4 + (b + 1))
                                a(grid(upad[:, b % 2, :]), ps[b % 2][:, :].rearrange("p (r w) -> p r w", w=GRID_W), ACT.Copy)
                                a(row_p(upad[:, b % 2, :]), pq[b % 2][:, 0:PROMPT], ACT.Copy).then_inc(S["copied"], 1)
                                if b:
                                    silu(act, g, b - 1)
                            silu(act, g, 3)
                            for t in range(TILES):
                                act.wait_ge(S["turned"], g * TILES + (t + 1))
                                a(tokm[:, t, :], p_t[:, 0:3 * P], ACT.Copy).then_inc(S["turned_out"], 1)
                            for t in range(TILES):
                                act.wait_ge(S["seg"], g * TILES + (t + 2))
                                act.wait_ge(S["mixed"], g * TILES + (t + 1))
                                a(E[:, :, :].rearrange("p h l -> p (h l)"), p_seg[:, :], ACT.Exp).then_inc(S["exped"], 1)

                    @block.vector
                    def _(dve):
                        v = nc.vector
                        D = dve_steps
                        heads = lambda ap: ap.rearrange("p (h q) -> p h q", h=HPG)
                        D.did(v.memset(upad[:, :, :], 0.0))
                        D.settle(dve)
                        for name, k in (("conved", 2), ("st_used", 1), ("cb_used", 1), ("mixed", 1), ("y_used", 1)):
                            dve.sem_inc(S[name], k)
                        STEPS = 4 * 3 + 2 + 6 * 2 + 2 + TILES * 5 + SAMPLE_TILES * 4
                        with D.loop(dve, SSM_GROUPS, STEPS) as g:
                            hd = lambda ap3, t, at_: bcast(ap3[:, t, bass.ds(g * HPG + at_, HPG)], 2, HEADDIM)
                            for b in range(4):
                                dve.wait_ge(S["copied"], g * 4 + (b + 3))
                                if b >= 2:
                                    dve.wait_ge(S["silued"], g * 4 + (b - 1))
                                blk = SSM_BLOCK[b]
                                w = lambda k: cols[:, bass.ds(blk(g) * 3 + (COL_AT["ssd_conv_w"][0] + k), 1)]
                                conv3(dve, conv[:, b % 2, :], upad[:, b % 2, :], w)
                                dve.sem_inc(S["conved"], 1)
                            dve.wait_ge(S["init_in"], g * 16 + 16)
                            D.did(v.tensor_copy(SF[:, 0, :], init[:, 0, :]))
                            D.did(v.tensor_copy(SB[:, LAST, :], init[:, 1, :]))
                            k = 0
                            order = [(3, 1), (2, 1), (1, 1), (0, 0), (1, 0), (2, 0), (4, 0), (4, 1)]

                            def weigh(k):
                                t, d = order[k]
                                dve.wait_ge(S["turned_out"], g * TILES + (t + 2))
                                v.tensor_tensor(heads(xw[:, k % 2, :]), heads(tokm[:, t, 0:GW]),
                                                hd(state_w, t, d * HEADS), ALU.mult).then_inc(S["weighted"], 1)

                            weigh(0)
                            for k, (t, d) in enumerate(order):
                                if k + 1 < len(order):
                                    weigh(k + 1)
                                dve.wait_ge(S["st"], g * 8 + (k + 1))
                                if t == SAMPLE_TILES:
                                    if d == 0:
                                        dve.wait_ge(S["last_free"], g + 1)
                                    ins = v.tensor_copy(last_s[:, d, :], p_st[:, 0:GW])
                                    D.did(ins)
                                    D.settle(dve)
                                    dve.sem_inc(S["st_used"], 1)
                                    if d == 1:
                                        dve.sem_inc(S["final"], 1)
                                    continue
                                src, dst = (SF[:, t, :], SF[:, t + 1, :]) if d == 0 else (SB[:, t, :], SB[:, t - 1, :])
                                D.settle(dve)
                                D.did(v.tensor_tensor(heads(dst), heads(src), hd(decay, t, ALL_B if d else ALL_F), ALU.mult))
                                D.settle(dve)
                                D.did(v.tensor_tensor(dst, dst, p_st[:, 0:GW], ALU.add))
                                D.settle(dve)
                                dve.sem_inc(S["st_used"], 1)
                            dve.sem_inc(S["states"], 1)
                            for t in range(TILES):
                                for d in range(2):
                                    D.did(v.tensor_tensor(heads(xdt[:, d, :]), heads(tokm[:, t, 0:GW]),
                                                          hd(dt, t, d * HEADS), ALU.mult))
                                dve.wait_ge(S["cb"], g * TILES + (t + 1))
                                D.did(v.tensor_tensor(CBm[:, 0, :], p_cb[:, 0:P], masks[:, LE, :], ALU.mult))
                                D.did(v.tensor_tensor(CBm[:, 1, :], p_cb[:, 0:P], masks[:, GE, :], ALU.mult))
                                D.settle(dve)
                                dve.sem_inc(S["cb_used"], 1)
                                dve.wait_ge(S["exped"], g * TILES + (t + 2))
                                for d in range(2):
                                    last = v.tensor_tensor(mix[:, d, :, :], E[:, :, :], bcast(CBm[:, d, :], 1, HPG), ALU.mult)
                                last.then_inc(S["mixed"], 1)
                                D.did(v.tensor_tensor(heads(xD[:, :]), heads(tokm[:, t, 0:GW]),
                                                      bcast(rows[:, bass.ds(g * HPG + ROW_AT["d"][0], HPG)], 2, HEADDIM), ALU.mult))
                                y_out_t = Y[:, t, bass.ds(g * GW, GW)]
                                if t < SAMPLE_TILES:
                                    dve.wait_ge(S["off"], g * SAMPLE_TILES + (t + 1))
                                    D.did(v.tensor_tensor(heads(off[:, 0, :]), heads(p_off[:, 0:GW]), hd(decay, t, IN_F), ALU.mult))
                                    D.did(v.tensor_tensor(heads(off[:, 1, :]), heads(p_off[:, GW:2 * GW]), hd(decay, t, IN_B), ALU.mult))
                                    D.settle(dve)
                                    D.did(v.tensor_tensor(off[:, 0, :], off[:, 0, :], off[:, 1, :], ALU.add))
                                    D.settle(dve)
                                    D.did(v.tensor_tensor(xD[:, :], xD[:, :], off[:, 0, :], ALU.add))
                                dve.wait_ge(S["y"], g * TILES + (t + 1))
                                D.settle(dve)
                                v.tensor_tensor(y_out_t, p_y[:, 0:GW], xD[:, :], ALU.add).then_inc(S["y_used"], 1)

        def gate_by_z(Y, hT):
            first = take(N_Z)
            with ExitStack() as ph:
                zs = sb("zs", [P, 2, 512], into=ph)
                ps = [pb(f"pz{j}", into=ph) for j in range(2)]
                z_done, z_out, gated = (sem(n) for n in ("z_done", "z_out", "gated"))
                with nc.Block() as block:
                    @block.sync
                    def _(sp):
                        feed(sp, first, N_Z)

                    @block.tensor
                    def _(pe):
                        pe.sem_inc(z_out, 2)
                        with pe.Fori(0, 2) as r:
                            for j in range(2):
                                for s in range(4 * j, 4 * j + 4):
                                    loaded(pe, s, r + first // SLOTS)
                                for t in range(TILES):
                                    k = j * TILES + t
                                    pe.wait_ge(z_out, r * (2 * TILES) + (k + 1))
                                    for c in range(NCH):
                                        last = nc.tensor.matmul(
                                            ps[k % 2][:, :], lhsT=hT[:, c, t * P:(t + 1) * P],
                                            rhs=ring[:, 4 * j + c // 2, (c % 2) * 512:(c % 2) * 512 + 512],
                                            start=c == 0, stop=c == NCH - 1)
                                    last.then_inc(z_done, 1)
                                pe.wait_ge(z_done, r * (2 * TILES) + ((j + 1) * TILES))
                                pe.sem_inc(blocks_used, 4)

                    @block.scalar
                    def _(act):
                        act.sem_inc(gated, 2)
                        with act.Fori(0, 2) as r:
                            for k in range(2 * TILES):
                                act.wait_ge(z_done, r * (2 * TILES) + (k + 1))
                                act.wait_ge(gated, r * (2 * TILES) + (k + 1))
                                nc.scalar.activation(zs[:, k % 2, :], ps[k % 2][:, :], ACT.Silu).then_inc(z_out, 1)

                    @block.vector
                    def _(dve):
                        with dve.Fori(0, 2) as r:
                            for k in range(2 * TILES):
                                dve.wait_ge(z_out, r * (2 * TILES) + (k + 3))
                                y = Y[:, k % TILES, bass.ds(r * 1024 + (k // TILES) * 512, 512)]
                                nc.vector.tensor_tensor(y, y, zs[:, k % 2, :], ALU.mult).then_inc(gated, 1)

        def norm_y(Y, yT):
            with ExitStack() as ph:
                junk = sb("junk", [P, SSM_INNER], into=ph)
                ss = sb("ss", [P, TILES], into=ph)
                ps = [pb(f"pyt{j}", into=ph) for j in range(2)]
                summed, rooted, scaled, turned, out = (sem(n) for n in ("y_summed", "y_rooted", "y_scaled", "y_turned", "y_out"))
                with nc.Block() as block:
                    @block.vector
                    def _(dve):
                        v = nc.vector
                        for t in range(TILES):
                            dve_steps.did(v.tensor_tensor_reduce(out=junk[:, :], in0=Y[:, t, :], in1=Y[:, t, :], scale=1.0,
                                                                 scalar=0.0, op0=ALU.mult, op1=ALU.add,
                                                                 accum_out=ss[:, t:t + 1]))
                            dve_steps.settle(dve)
                        dve.sem_inc(summed, 1)
                        dve.wait_ge(rooted, 1)
                        dve_steps.did(v.reciprocal(ss[:, :], ss[:, :]))
                        dve_steps.settle(dve)
                        for t in range(TILES):
                            v.tensor_scalar(Y[:, t, :], Y[:, t, :], ss[:, t:t + 1], None, ALU.mult).then_inc(scaled, 1)
                            for b in range(4):
                                k = 4 * t + b
                                dve.wait_ge(turned, k + 1)
                                v.tensor_tensor(yT[:, 4 * b:4 * b + 4, t * P:(t + 1) * P],
                                                ps[k % 2][:, :].rearrange("p (b t) -> p b t", b=4),
                                                bcast(col("ssd_norm_w", 4 * b, 4 * b + 4), 2, P), ALU.mult).then_inc(out, 1)

                    @block.scalar
                    def _(act):
                        act.wait_ge(summed, 1)
                        nc.scalar.activation(ss[:, :], ss[:, :], ACT.Sqrt, bias=eps[:, :], scale=1.0 / SSM_INNER).then_inc(rooted, 1)

                    @block.tensor
                    def _(pe):
                        for t in range(TILES):
                            pe.wait_ge(scaled, t + 1)
                            for b in range(4):
                                k = 4 * t + b
                                if k >= 2:
                                    pe.wait_ge(out, k - 1)
                                for q in range(4):
                                    last = nc.tensor.transpose(ps[k % 2][:, q * P:(q + 1) * P],
                                                               Y[:, t, (4 * b + q) * P:(4 * b + q + 1) * P], masks[:, IDENT, :])
                                last.then_inc(turned, 1)

        def scale_of(t):
            return lambda c, k: t[:, c, k:k + 1]

        def shift_of(comp):
            return lambda c, k: mods[:, comp * NCH + c, k:k + 1]

        stages = []
        for layer in range(DEPTH):
            stages += [
                lambda layer=layer: adaln(layer),
                ssd_mixer if layer % 2 else even_mixer,
                lambda layer=layer: peer(layer),
            ]
        for stage in stages:
            stage()
        yT_out = sb("yT_out", [P, NCH, TOK])
        norm_modulate("last", yT_out, lambda c, k: col("norm_final", c, c + 1), None)
        stored = sem("stored")
        with nc.Block() as block:
            @block.sync
            def _(sp):
                sp.dma_start(y_out, yT_out[:, :, :]).then_inc(stored, 16)
                sp.wait_ge(stored, 16)


def kernel(**inputs):
    import numpy as np
    import concourse.bacc as bacc
    from concourse.bass_utils import run_bass_kernel_spmd

    a = {k: np.asarray(v) for k, v in inputs.items()}

    def chunks(v):
        return v.reshape(-1, P).T

    def out_blocks(w):
        k, n = w.shape
        return w.reshape(k // P, P, n // P, P).transpose(2, 1, 0, 3).reshape(n // P, P, k)

    w_ssd = a["ssd_w_in"][0]
    w_z, w_xbc, w_dt = w_ssd[:, :SSM_INNER], w_ssd[:, SSM_INNER:SSM_INNER + 4096], w_ssd[:, SSM_INNER + 4096:]
    xbc = out_blocks(w_xbc)
    order = [b for g in range(SSM_GROUPS) for b in (2 * g, 2 * g + 1, 16 + g, 24 + g)]
    z = w_z.reshape(4, 2, P, 4, 512).transpose(3, 0, 2, 1, 4).reshape(16, P, 1024)
    ssd_out = a["ssd_w_out"][0].reshape(2, NCH, P, NCH, P).transpose(3, 0, 2, 1, 4).reshape(16, P, 1024)

    def experts_of(layer):
        G, B = EXPERT_BLOCKS // BLOCKS_PER_GROUP, BLOCKS_PER_GROUP
        u = a["peer_u"][layer].reshape(G, B, KEYS, NCH, P).transpose(0, 1, 4, 3, 2).reshape(G, B, P, 1024)
        v = a["peer_v"][layer].reshape(G, B, P, 1024)
        return np.concatenate([u, v], axis=1).reshape(2 * EXPERT_BLOCKS, P, 1024)

    stream = np.concatenate([
        out_blocks(a["adaln_w"][0]), out_blocks(a["even_w_in"][0]), out_blocks(a["even_w_out"][0]),
        out_blocks(a["peer_w_q"][0]), experts_of(0),
        out_blocks(a["adaln_w"][1]), xbc[order], z, ssd_out, out_blocks(a["peer_w_q"][1]), experts_of(1)])
    keys = a["peer_keys"].transpose(0, 4, 1, 2, 3).reshape(DEPTH, P, 2 * PEER_HEADS * KEYS)
    wdt = w_dt.reshape(NCH, P, 64).transpose(1, 0, 2)
    xin = np.concatenate([a["x_sample"][0], a["x_prompt"][0]]).T.reshape(NCH, P, TOK).transpose(1, 0, 2)
    cond = np.stack([a["c"][0], a["c_ctx"]], axis=1).reshape(NCH, P, 2).transpose(1, 0, 2).reshape(P, 2 * NCH)
    cols = np.concatenate([
        cond, chunks(a["adaln_b"].reshape(-1)), chunks(a["norm_mix"].reshape(-1)), chunks(a["norm_ffn"].reshape(-1)),
        chunks(a["norm_final"]), a["even_conv_w"][0].reshape(3, 4, P).transpose(2, 1, 0).reshape(P, 12),
        a["ssd_conv_w"][0].reshape(3, 32, P).transpose(2, 1, 0).reshape(P, 96), chunks(a["ssd_conv_b"][0]),
        chunks(a["ssd_norm_w"][0])], axis=1)
    f32 = np.float32
    rows = np.concatenate([
        a["ssd_dt_bias"][0].reshape(-1), a["ssd_a_log"][0].reshape(-1), a["ssd_d"][0], np.arange(P, dtype=f32),
        np.arange(TOPK, dtype=f32), np.array(PAIR_AT, f32), np.array([0] + PAIRS_OF[:-1], f32)])
    rows = np.broadcast_to(rows[None, :], (P, NROWS))
    k, l = np.arange(P)[:, None], np.arange(P)[None, :]
    masks = np.stack([k <= l, k < l, k >= l, k > l, k >= 0 * l, k == l], axis=1).astype(f32)

    def angles(n):
        return 2 * np.pi * (np.outer(np.arange(n), np.arange(n)) % n) / n

    at, ac = angles(SAMPLE), angles(P)
    scale_s, scale_p = (SAMPLE * P) ** -0.5, 1.0 / P
    tiles = lambda m: m.reshape(SAMPLE_TILES, P, SAMPLE).transpose(1, 0, 2).reshape(P, -1)
    dft = np.concatenate([tiles(np.cos(at) * scale_s), tiles(-np.sin(at) * scale_s), np.cos(ac), np.sin(ac),
                          np.cos(ac) * scale_p, -np.sin(ac) * scale_p], axis=1).astype(f32)

    def states(s):
        return s[0, 0].reshape(SSM_GROUPS, GW, P).transpose(0, 2, 1)

    state_in = np.stack([states(a["state_ssd_fwd"]), states(a["state_ssd_bwd"])], axis=2)

    nc = bacc.Bacc("TRN2", target_bir_lowering=False, num_devices=1)
    arrays = dict(stream=stream, keys=keys, wdt=wdt, xin=xin, cols=cols, rows=rows, masks=masks, dft=dft,
                  state_in=state_in)
    arrays = {n: np.ascontiguousarray(v) for n, v in arrays.items()}
    aps = [nc.dram_tensor(f"in_{n}", v.shape, F32, kind="ExternalInput").ap() for n, v in arrays.items()]
    y = nc.dram_tensor("y", (P, NCH, TOK), F32, kind="ExternalOutput").ap()
    state_out = nc.dram_tensor("state_out", (SSM_GROUPS, P, 2, GW), F32, kind="ExternalOutput").ap()
    gates = nc.dram_tensor("gates", (TOK // SCATTER_TOK, P, KEYS, SCATTER_TOK), F32, kind="Internal").ap()
    hybrid_trunk(nc, *aps, y, state_out, gates)
    r = run_bass_kernel_spmd(nc, [{f"in_{n}": v for n, v in arrays.items()}], core_ids=[0]).results[0]
    y = r["y"].transpose(1, 0, 2).reshape(D_MODEL, TOK).T
    st = r["state_out"].transpose(2, 0, 3, 1).reshape(2, 1, 1, HEADS, HEADDIM, P)
    return (np.ascontiguousarray(y[None, SAMPLE:]), np.ascontiguousarray(y[None, :SAMPLE]),
            np.ascontiguousarray(st[0]), np.ascontiguousarray(st[1]))
```

```python
import concourse.bass as bass
from concourse import mybir
from contextlib import ExitStack, contextmanager

F32 = mybir.dt.float32
F32R = mybir.dt.float32r
U32 = mybir.dt.uint32
ALU = mybir.AluOpType
ACT = mybir.ActivationFunctionType
AX = mybir.AxisListType

P = 128
D_MODEL = 1024
NCH = D_MODEL // P
SAMPLE, PROMPT = 512, 128
TOK = SAMPLE + PROMPT
TILES = TOK // P
HALF_TOK = TOK // 2
HALVES = (slice(0, HALF_TOK), slice(HALF_TOK, TOK))
PARTS = ((0, slice(0, HALF_TOK), 0, slice(0, HALF_TOK)),
         (0, slice(HALF_TOK, SAMPLE), 1, slice(0, SAMPLE - HALF_TOK)),
         (1, slice(SAMPLE, TOK), 1, slice(SAMPLE - HALF_TOK, HALF_TOK)))
SAMPLE_TILES = SAMPLE // P
DEPTH = 2
GRID_W = 64
EPS = 1e-6
MODS = 6
EVEN_IN = 2048
GROUPS = 4
SSM_INNER = 2048
HEADS = 32
SSM_GROUPS = 8
HPG = HEADS // SSM_GROUPS
HEADDIM = 64
GW = HPG * HEADDIM
PEER_HEADS = 8
TOPK = 16
ENTRIES = PEER_HEADS * TOPK
KEYS = 128
EXPERT_BLOCKS = 128
BLOCKS_PER_GROUP = 4
SCATTER_TOK = 64
SLOTS = 8
HALF_RING = SLOTS // 2
NEG = -3.0e38
SH1, SC1, G1, SH2, SC2, G2 = range(MODS)

N_ADALN = MODS * NCH
N_EVEN_IN = EVEN_IN // P
N_EVEN_OUT = NCH
N_WQ = 2048 // P
EARLY_PER_TILE = 8
EARLY = EARLY_PER_TILE * TILES
N_LATE = 2 * (EXPERT_BLOCKS - EARLY)
N_SSD = 4 * SSM_GROUPS
N_Z = 16
N_SSD_OUT = 2 * NCH

PAIRS_OF = [TOPK // (i + 1) for i in range(TOPK)]
PAIR_AT = [sum(PAIRS_OF[:i]) for i in range(TOPK)]
PAIRS = sum(PAIRS_OF)

COL_SIZES = [("cond", NCH * 2), ("adaln_b", DEPTH * N_ADALN), ("norm_mix", DEPTH * NCH),
             ("norm_ffn", DEPTH * NCH), ("norm_final", NCH), ("even_conv_w", 12), ("ssd_conv_w", 96),
             ("ssd_conv_b", 32), ("ssd_norm_w", 16)]
COL_AT, NCOLS = {}, 0
for _name, _n in COL_SIZES:
    COL_AT[_name] = (NCOLS, _n)
    NCOLS += _n
ROW_SIZES = [("dt_bias", 64), ("a_log", 64), ("d", 32), ("iota", 128), ("rank", TOPK), ("pair_at", TOPK),
             ("pairs_before", TOPK)]
ROW_AT, NROWS = {}, 0
for _name, _n in ROW_SIZES:
    ROW_AT[_name] = (NROWS, _n)
    NROWS += _n
LE, LT, GE, GT, ONES, IDENT = range(6)


class Steps:

    def __init__(self, sem):
        self.sem, self.base, self.k = sem, 0, 0

    def did(self, ins):
        self.k += 1
        return ins.then_inc(self.sem, 1)

    def settle(self, eng):
        eng.wait_ge(self.sem, self.base + self.k)

    @contextmanager
    def loop(self, eng, n, per):
        start = self.base + self.k
        with eng.Fori(0, n) as i:
            self.base, self.k = i * per + start, 0
            yield i
            assert self.k == per, (self.k, per)
        self.base, self.k = start + n * per, 0


def bcast(ap, axis, n):
    v = ap.unsqueeze(axis)
    shape = list(v.shape)
    shape[axis] = n
    return v.broadcast_to(shape)


def hybrid_trunk(nc, stream, keys, wdt, xin, cols_d, rows_d, masks_d, dft_d, state_in, y_out, state_out,
                 gates_dram, hidden_dram):
    ctx = ExitStack()
    with ctx:
        def sb(name, shape, dt=F32, into=ctx):
            return into.enter_context(nc.sbuf_tensor(name, shape, dt))

        def pb(name, cols=512, into=ctx):
            return into.enter_context(nc.psum_tensor(name, [P, cols], F32))

        def sem(name, into=ctx):
            return ctx.enter_context(nc.semaphore(name))

        xT = sb("xT", [P, NCH, TOK])
        ring = sb("ring", [P, SLOTS, 1024])
        cols = sb("cols", [P, NCOLS])
        rows = sb("rows", [P, NROWS])
        masks = sb("masks", [P, 6, P])
        mods = sb("mods", [P, N_ADALN, 2])
        scale_mix = sb("scale_mix", [P, NCH, 2])
        scale_ffn = sb("scale_ffn", [P, NCH, 2])
        scond = sb("scond", [P, NCH, 2])
        eps = sb("eps", [P, 1])
        zero = sb("zero", [P, 1])

        def col(name, a=0, b=None):
            at, n = COL_AT[name]
            return cols[:, at + a:at + (n if b is None else b)]

        def row(name):
            at, n = ROW_AT[name]
            return rows[:, at:at + n]

        half_loaded = [sem(f"half_loaded{k}") for k in range(2)]
        blocks_used = sem("blocks_used")
        consts_loaded = sem("consts_loaded")
        x_loaded = sem("x_loaded")
        dve_steps = Steps(sem("dve_steps"))
        act_steps = Steps(sem("act_steps"))
        pool_steps = Steps(sem("pool_steps"))
        at = [0]

        def take(n):
            first = at[0]
            at[0] += n
            return first

        def load_half(sp, k, block):
            sp.dma_start(ring[:, k * HALF_RING:(k + 1) * HALF_RING, :],
                         stream[bass.ds(block, HALF_RING)].rearrange("b p n -> p b n")).then_inc(half_loaded[k], 16)

        def feed(sp, first, n):
            last = min(first + n + SLOTS, N_BLOCKS) - SLOTS
            if last == first:
                return
            with sp.Fori(0, (last - first) // SLOTS) as i:
                for k in range(2):
                    sp.wait_ge(blocks_used, i * SLOTS + (first + (k + 1) * HALF_RING))
                    load_half(sp, k, i * SLOTS + (first + SLOTS + k * HALF_RING))

        def loaded(pe, s, round_):
            if s % HALF_RING == 0:
                pe.wait_ge(half_loaded[s // HALF_RING], round_ * 16 + 16)

        N_BLOCKS = stream.shape[0]

        def pair_matmul(out_s, out_p, lhsT, rhs, c, start, stop):
            nc.tensor.matmul(out_s, lhsT=lhsT, rhs=rhs[:, c, 0:SAMPLE], start=start, stop=stop)
            return nc.tensor.matmul(out_p, lhsT=lhsT, rhs=rhs[:, c, SAMPLE:TOK], start=start, stop=stop)

        def norm_modulate(tag, dst, scale, shift, split=False):
            with ExitStack() as ph:
                sq = sb(f"sq{tag}", [P, 2, TOK], into=ph)
                rms = sb(f"rms{tag}", [P, TOK], into=ph)
                whole = sb(f"whole{tag}", [P, NCH, TOK], into=ph) if split else dst
                modulated = sem(f"modulated_{tag}")
                sum_s, sum_p = pb(f"sums{tag}", into=ph), pb(f"sump{tag}", into=ph)
                squared, summed, rooted, scaled = (sem(f"{n}_{tag}") for n in ("squared", "summed", "rooted", "scaled"))
                with nc.Block() as block:
                    @block.scalar
                    def _(act):
                        for c in range(NCH):
                            if c >= 2:
                                act.wait_ge(summed, c - 1)
                            nc.scalar.activation(sq[:, c % 2, :], xT[:, c, :], ACT.Square).then_inc(squared, 1)
                        act.wait_ge(summed, NCH)
                        nc.scalar.activation(rms[:, 0:SAMPLE], sum_s[:, :], ACT.Sqrt, bias=eps[:, :],
                                             scale=1.0 / D_MODEL).then_inc(rooted, 1)
                        nc.scalar.activation(rms[:, SAMPLE:TOK], sum_p[:, 0:PROMPT], ACT.Sqrt, bias=eps[:, :],
                                             scale=1.0 / D_MODEL).then_inc(rooted, 1)
                        for c in range(NCH):
                            act.wait_ge(scaled, c + 1)
                            for k, part in ((0, slice(0, SAMPLE)), (1, slice(SAMPLE, TOK))):
                                last = nc.scalar.activation(whole[:, c, part], whole[:, c, part], ACT.Identity,
                                                            scale=scale(c, k), bias=shift(c, k) if shift else 0.0)
                            last.then_inc(modulated, 1)

                    @block.tensor
                    def _(pe):
                        for c in range(NCH):
                            pe.wait_ge(squared, c + 1)
                            nc.tensor.matmul(sum_s[:, :], lhsT=masks[:, ONES, :], rhs=sq[:, c % 2, 0:SAMPLE],
                                             start=c == 0, stop=c == NCH - 1)
                            nc.tensor.matmul(sum_p[:, 0:PROMPT], lhsT=masks[:, ONES, :], rhs=sq[:, c % 2, SAMPLE:TOK],
                                             start=c == 0, stop=c == NCH - 1).then_inc(summed, 1)

                    @block.vector
                    def _(dve):
                        dve.wait_ge(rooted, 2)
                        dve_steps.did(nc.vector.reciprocal(rms[:, :], rms[:, :]))
                        dve_steps.settle(dve)
                        for c in range(NCH):
                            nc.vector.tensor_tensor(whole[:, c, :], xT[:, c, :], rms[:, :], ALU.mult).then_inc(scaled, 1)
                        if split:
                            for c in range(NCH):
                                dve.wait_ge(modulated, c + 1)
                                dve_steps.did(nc.vector.tensor_copy(dst[:, c, 0, :], whole[:, c, :]))
                                dve_steps.settle(dve)
                                nc.vector.tensor_tensor(dst[:, c, 1, :], whole[:, c, :], dst[:, c, 0, :].bitcast(F32),
                                                        ALU.subtract)

        def adaln(layer):
            tag = f"ada{layer}"
            first = take(N_ADALN)
            with ExitStack() as ph:
                COLS = 96
                ps = [pb(f"ps{tag}{k}", into=ph) for k in range(4)]
                silu_done = sem(f"silu_done{layer}")
                half_free = sem(f"half_free{layer}")
                with nc.Block() as block:
                    @block.sync
                    def _(sp):
                        feed(sp, first, N_ADALN)

                    @block.scalar
                    def _(act):
                        nc.scalar.activation(scond[:, :, :], col("cond").rearrange("p (c k) -> p c k", k=2),
                                             ACT.Silu).then_inc(silu_done, 1)

                    @block.tensor
                    def _(pe):
                        pe.wait_ge(silu_done, 1)
                        pe.sem_inc(half_free, 4)
                        with pe.Fori(0, N_ADALN // (2 * SLOTS)) as i:
                            for s in range(2 * SLOTS):
                                loaded(pe, s % SLOTS, i * 2 + (first // SLOTS + s // SLOTS))
                                if s % HALF_RING == 0:
                                    pe.wait_ge(half_free, i * 4 + (s // HALF_RING + 1))
                                for c in range(NCH):
                                    last = nc.tensor.matmul(
                                        ps[s // HALF_RING][:, (s % HALF_RING) * P:(s % HALF_RING) * P + COLS]
                                        .rearrange("p (r k) -> p r k", k=2),
                                        lhsT=ring[:, s % SLOTS, c * P:(c + 1) * P], rhs=bcast(scond[:, c, :], 1, COLS // 2),
                                        start=c == 0, stop=c == NCH - 1)
                                last.then_inc(blocks_used, 1)

                    @block.vector
                    def _(dve):
                        with dve_steps.loop(dve, N_ADALN // (2 * SLOTS), 0) as i:
                            for k in range(4):
                                dve.wait_ge(blocks_used, i * (2 * SLOTS) + (first + (k + 1) * HALF_RING))
                                m = i * (2 * SLOTS) + k * HALF_RING
                                bias = cols[:, bass.ds(m + (COL_AT["adaln_b"][0] + layer * N_ADALN), HALF_RING)]
                                nc.vector.tensor_tensor(
                                    mods[:, bass.ds(m, HALF_RING), :],
                                    ps[k][:, :].rearrange("p (b c) -> p b c", b=HALF_RING)[:, :, 0:2],
                                    bcast(bias, 2, 2), ALU.add).then_inc(half_free, 1)
                        dve.wait_ge(half_free, 4 + N_ADALN // HALF_RING)
                        for dst, comp, w in ((scale_mix, SC1, "norm_mix"), (scale_ffn, SC2, "norm_ffn")):
                            nc.vector.scalar_tensor_tensor(
                                dst[:, :, :], in0=mods[:, comp * NCH:(comp + 1) * NCH, :], scalar=1.0,
                                in1=bcast(col(w, layer * NCH, (layer + 1) * NCH), 2, 2), op0=ALU.add, op1=ALU.mult)

        def project(tag, n_blocks, rhs, evacuate, per_steps=0, dve_evac=False, chunks=NCH):
            first = take(n_blocks)
            each = chunks // NCH
            per_round = SLOTS // each
            with ExitStack() as ph:
                ps = [pb(f"ps{tag}{j}", into=ph) for j in range(2)]
                pp = [pb(f"pp{tag}{j}", into=ph) for j in range(2)]
                pair_free = sem(f"pair_free_{tag}")
                with nc.Block() as block:
                    @block.sync
                    def _(sp):
                        feed(sp, first, n_blocks)

                    @block.tensor
                    def _(pe):
                        with pe.Fori(0, n_blocks // SLOTS) as i:
                            for o in range(per_round):
                                pe.wait_ge(pair_free, i * per_round + (o + 1))
                                for s in range(o * each, (o + 1) * each):
                                    loaded(pe, s, i + first // SLOTS)
                                    for c in range(NCH):
                                        cc = (s - o * each) * NCH + c
                                        last = pair_matmul(ps[o % 2][:, :], pp[o % 2][:, 0:PROMPT],
                                                           ring[:, s, c * P:(c + 1) * P], rhs, cc,
                                                           cc == 0, cc == chunks - 1)
                                    last.then_inc(blocks_used, 1)

                    def evac(eng, steps):
                        eng.sem_inc(pair_free, 2)
                        with steps.loop(eng, n_blocks // SLOTS, per_steps) as i:
                            for o in range(per_round):
                                eng.wait_ge(blocks_used, i * SLOTS + (first + (o + 1) * each))
                                evacuate(eng, i * per_round + o, ps[o % 2][:, :], pp[o % 2][:, 0:PROMPT]).then_inc(pair_free, 1)

                    if dve_evac:
                        @block.vector
                        def _(dve):
                            evac(dve, dve_steps)
                    else:
                        @block.scalar
                        def _(act):
                            evac(act, act_steps)

        def split_matmuls(outs, w_hi, w_lo, rhs, c, start, stop):
            for n, (w, part) in enumerate(((w_hi, 0), (w_hi, 1), (w_lo, 0))):
                for out, cols_ in zip(outs, HALVES):
                    last = nc.tensor.matmul(out[:, 0:HALF_TOK], lhsT=w, rhs=rhs[:, c, part, cols_],
                                            start=start and n == 0, stop=stop and n == 2)
            return last

        def project_split(tag, n_blocks, rhs, evacuate, chunks=NCH):
            first = take(n_blocks)
            each = chunks // NCH
            per_round = SLOTS // each
            with ExitStack() as ph:
                wide = sb(f"wide{tag}", [P, 2, 2, 1024], F32R, into=ph)
                ps = [[pb(f"ps{tag}{j}{h}", into=ph) for h in range(2)] for j in range(2)]
                pair_free, wide_used, hi_done = (sem(f"{n}_{tag}") for n in ("pair_free", "wide_used", "hi_done"))
                with nc.Block() as block:
                    @block.sync
                    def _(sp):
                        feed(sp, first, n_blocks)

                    @block.scalar
                    def _(act):
                        act.sem_inc(wide_used, 2)
                        with act.Fori(0, n_blocks // SLOTS) as i:
                            for s in range(SLOTS):
                                loaded(act, s, i + first // SLOTS)
                                act.wait_ge(wide_used, i * SLOTS + (s + 1))
                                nc.scalar.activation(wide[:, s % 2, 0, :], ring[:, s, :], ACT.Copy).then_inc(hi_done, 1)

                    @block.gpsimd
                    def _(pool):
                        with pool.Fori(0, n_blocks // SLOTS) as i:
                            for s in range(SLOTS):
                                pool.wait_ge(hi_done, i * SLOTS + (s + 1))
                                nc.gpsimd.tensor_tensor(wide[:, s % 2, 1, :], ring[:, s, :], wide[:, s % 2, 0, :].bitcast(F32),
                                                        ALU.subtract).then_inc(blocks_used, 1)

                    @block.tensor
                    def _(pe):
                        with pe.Fori(0, n_blocks // SLOTS) as i:
                            for o in range(per_round):
                                pe.wait_ge(pair_free, i * per_round + (o + 1))
                                for s in range(o * each, (o + 1) * each):
                                    pe.wait_ge(blocks_used, i * SLOTS + (first + s + 1))
                                    for c in range(NCH):
                                        cc = (s - o * each) * NCH + c
                                        last = split_matmuls(ps[o % 2], wide[:, s % 2, 0, c * P:(c + 1) * P],
                                                             wide[:, s % 2, 1, c * P:(c + 1) * P], rhs, cc,
                                                             cc == 0, cc == chunks - 1)
                                    last.then_inc(wide_used, 1)

                    @block.vector
                    def _(dve):
                        dve.sem_inc(pair_free, 2)
                        with dve.Fori(0, n_blocks // SLOTS) as i:
                            for o in range(per_round):
                                dve.wait_ge(wide_used, i * SLOTS + ((o + 1) * each + 2))
                                evacuate(i * per_round + o, ps[o % 2]).then_inc(pair_free, 1)

        def copy_halves(dst):
            def f(m, ps):
                for h in range(2):
                    last = nc.vector.tensor_copy(dst[:, bass.ds(m, 1), HALVES[h]].rearrange("p a t -> p (a t)"),
                                                 ps[h][:, 0:HALF_TOK])
                return last
            return f

        def add_gated_halves(gate):
            def f(m, ps):
                for k, part, h, at_ in PARTS:
                    x = xT[:, bass.ds(m, 1), part].rearrange("p a t -> p (a t)")
                    last = nc.vector.scalar_tensor_tensor(
                        x, in0=ps[h][:, at_], scalar=mods[:, bass.ds(m + gate * NCH, 1), k:k + 1].rearrange("p a k -> p (a k)"),
                        in1=x, op0=ALU.mult, op1=ALU.add)
                return last
            return f

        def split_into(dst, src, n):
            his = sem(f"his_{src.name}")
            with nc.Block() as block:
                @block.scalar
                def _(act):
                    for c in range(n):
                        nc.scalar.activation(dst[:, c, 0, :], src[:, c, :], ACT.Copy).then_inc(his, 1)

                @block.vector
                def _(dve):
                    for c in range(n):
                        dve.wait_ge(his, c + 1)
                        nc.vector.tensor_tensor(dst[:, c, 1, :], src[:, c, :], dst[:, c, 0, :].bitcast(F32), ALU.subtract)

        def copy_into(dst):
            def f(act, m, s, p):
                nc.scalar.activation(dst[:, bass.ds(m, 1), 0:SAMPLE].rearrange("p a t -> p (a t)"), s, ACT.Copy)
                return nc.scalar.activation(dst[:, bass.ds(m, 1), SAMPLE:TOK].rearrange("p a t -> p (a t)"), p, ACT.Copy)
            return f

        def add_gated(gate):
            def f(dve, m, s, p):
                for k, src, a, b in ((0, s, 0, SAMPLE), (1, p, SAMPLE, TOK)):
                    x = xT[:, bass.ds(m, 1), a:b].rearrange("p a t -> p (a t)")
                    last = nc.vector.scalar_tensor_tensor(
                        x, in0=src, scalar=mods[:, bass.ds(m + gate * NCH, 1), k:k + 1].rearrange("p a k -> p (a k)"),
                        in1=x, op0=ALU.mult, op1=ALU.add)
                return last
            return f

        with nc.Block() as block:
            @block.sync
            def _(sp):
                sp.dma_start(cols[:, :], cols_d).then_inc(consts_loaded, 16)
                sp.dma_start(rows[:, :], rows_d).then_inc(consts_loaded, 16)
                sp.dma_start(masks[:, :, :], masks_d).then_inc(consts_loaded, 16)
                for k in range(2):
                    load_half(sp, k, k * HALF_RING)
                sp.dma_start(xT[:, :, :], xin).then_inc(x_loaded, 16)
                sp.wait_ge(consts_loaded, 48)
                sp.wait_ge(x_loaded, 16)

            @block.vector
            def _(dve):
                nc.vector.memset(eps[:, :], EPS)

        def even_mixer():
            with ExitStack() as ph:
                pT = sb("pT", [P, N_EVEN_IN, TOK], into=ph)
                with ExitStack() as h_life:
                    h2 = sb("h2_even", [P, NCH, 2, TOK], F32R, into=h_life)
                    norm_modulate("m0", h2, scale_of(scale_mix), shift_of(SH1), split=True)
                    project_split("even_in", N_EVEN_IN, h2, copy_halves(pT))
                between = ExitStack()
                dft = sb("dft", [P, 2 * SAMPLE_TILES * SAMPLE + 4 * P], into=between)
                dft_loaded = sem("dft_loaded")
                cos_t = dft[:, 0:2048].rearrange("p (t u) -> p t u", u=SAMPLE)
                sin_t = dft[:, 2048:4096].rearrange("p (t u) -> p t u", u=SAMPLE)
                both_c = dft[:, 4096:4096 + 256]
                cos_p, sin_p = dft[:, 4352:4480], dft[:, 4480:4608]
                by_c = sb("by_c", [P, TILES, GROUPS, 2 * P], into=between)
                PADDED = 8 * (GRID_W + 2) + PROMPT + 2
                upad = sb("upad", [P, 2, PADDED], into=between)
                conv = sb("conv", [P, 2, PADDED], into=between)
                banks = ExitStack()
                pc = [pb(f"pc{j}", into=banks) for j in range(2)]
                pf = [pb(f"pf{j}", into=banks) for j in range(2)]
                pfp = [pb(f"pfp{j}", into=banks) for j in range(2)]
                chan_done, chan_used, pos_done, pos_free = (sem(n) for n in ("chan_done", "chan_used", "pos_done", "pos_free"))
                with nc.Block() as block:
                    @block.sync
                    def _(sp):
                        sp.dma_start(dft[:, :], dft_d).then_inc(dft_loaded, 16)

                    @block.tensor
                    def _(pe):
                        pe.wait_ge(dft_loaded, 16)
                        n = 0
                        for t in range(TILES):
                            for g in range(0, GROUPS, 2):
                                if n >= 2:
                                    pe.wait_ge(chan_used, n - 1)
                                for k in range(2):
                                    last = nc.tensor.matmul(pc[n % 2][:, 256 * k:256 * k + 256],
                                                            lhsT=pT[:, g + k, t * P:(t + 1) * P], rhs=both_c,
                                                            start=True, stop=True)
                                last.then_inc(chan_done, 1)
                                n += 1
                        pe.wait_ge(chan_used, n)
                        for g in range(GROUPS):
                            if g >= 2:
                                pe.wait_ge(pos_free, g - 1)
                            for t in range(SAMPLE_TILES):
                                nc.tensor.matmul(pf[g % 2][:, :], lhsT=by_c[:, t, g, 0:P], rhs=cos_t[:, t, :],
                                                 start=t == 0, stop=False)
                                nc.tensor.matmul(pf[g % 2][:, :], lhsT=by_c[:, t, g, P:2 * P], rhs=sin_t[:, t, :],
                                                 start=False, stop=t == SAMPLE_TILES - 1)
                            nc.tensor.matmul(pfp[g % 2][:, 0:P], lhsT=by_c[:, SAMPLE_TILES, g, 0:P], rhs=cos_p,
                                             start=True, stop=False)
                            nc.tensor.matmul(pfp[g % 2][:, 0:P], lhsT=by_c[:, SAMPLE_TILES, g, P:2 * P], rhs=sin_p,
                                             start=False, stop=True).then_inc(pos_done, 1)

                    @block.scalar
                    def _(act):
                        n = 0
                        for t in range(TILES):
                            for g in range(0, GROUPS, 2):
                                act.wait_ge(chan_done, n + 1)
                                nc.scalar.activation(by_c[:, t, g:g + 2, :].rearrange("p g c -> p (g c)"), pc[n % 2][:, :],
                                                     ACT.Copy).then_inc(chan_used, 1)
                                n += 1
                        for g in range(GROUPS):
                            act.wait_ge(pos_done, g + 1)
                            nc.scalar.activation(pT[:, g, 0:SAMPLE], pf[g % 2][:, :], ACT.Copy)
                            nc.scalar.activation(pT[:, g, SAMPLE:TOK], pfp[g % 2][:, 0:P], ACT.Copy).then_inc(pos_free, 1)

                    @block.vector
                    def _(dve):
                        dve_steps.did(nc.vector.memset(upad[:, :, :], 0.0))
                        dve_steps.settle(dve)
                        for j in range(4):
                            u, v = upad[:, j % 2, :], conv[:, j % 2, :]
                            us = grid(u)
                            dve_steps.did(nc.vector.tensor_tensor(
                                us, pT[:, 8 + j, 0:SAMPLE].rearrange("p (r w) -> p r w", w=GRID_W),
                                pT[:, 12 + j, 0:SAMPLE].rearrange("p (r w) -> p r w", w=GRID_W), ALU.mult))
                            dve_steps.did(nc.vector.tensor_tensor(row_p(u), pT[:, 8 + j, SAMPLE:TOK],
                                                                  pT[:, 12 + j, SAMPLE:TOK], ALU.mult))
                            dve_steps.settle(dve)
                            conv3(dve, v, u, lambda k: col("even_conv_w", 3 * j + k, 3 * j + k + 1))
                            for dst, src in ((pT[:, 4 + j, 0:SAMPLE].rearrange("p (r w) -> p r w", w=GRID_W), grid(v)),
                                             (pT[:, 4 + j, SAMPLE:TOK], row_p(v))):
                                dve_steps.did(nc.vector.tensor_tensor(dst, dst, src, ALU.mult))
                banks.close()
                between.close()
                y2 = sb("y2_even", [P, NCH, 2, TOK], F32R, into=ph)
                split_into(y2, pT, NCH)
                project_split("even_out", N_EVEN_OUT, y2, add_gated_halves(G1))

        def grid(u):
            return u[:, 0:8 * (GRID_W + 2)].rearrange("p (r w) -> p r w", w=GRID_W + 2)[:, :, 1:GRID_W + 1]

        def row_p(u):
            return u[:, 8 * (GRID_W + 2) + 1:8 * (GRID_W + 2) + 1 + PROMPT]

        def conv3(dve, v, u, w):
            n = 8 * (GRID_W + 2) + PROMPT + 2
            dve_steps.did(nc.vector.tensor_scalar(v[:, 1:n - 1], u[:, 1:n - 1], w(1), None, ALU.mult))
            for k, shift in ((0, 0), (2, 2)):
                dve_steps.settle(dve)
                dve_steps.did(nc.vector.scalar_tensor_tensor(v[:, 1:n - 1], in0=u[:, shift:n - 2 + shift], scalar=w(k),
                                                             in1=v[:, 1:n - 1], op0=ALU.mult, op1=ALU.add))
            dve_steps.settle(dve)

        peer_sems = {}

        def peer_sem(name):
            if name not in peer_sems:
                peer_sems[name] = sem("peer_" + name)
            return peer_sems[name]

        def peer(layer):
            tag = f"_p{layer}"
            if layer > 0:
                with nc.Block() as block:
                    @block.sync
                    def _(sp):
                        for s in peer_sems.values():
                            sp.sem_clear(s)
            with ExitStack() as h_life:
                h2 = sb(f"h2{tag}", [P, NCH, 2, TOK], F32R, into=h_life)
                norm_modulate(f"f{layer}", h2, scale_of(scale_ffn), shift_of(SH2), split=True)
                with ExitStack() as ids_life:
                    idT = sb(f"idT{tag}", [P, 3, TOK], into=ids_life)
                    with ExitStack() as ph:
                        qT = sb(f"qT{tag}", [P, N_WQ, TOK], into=ph)
                        project_split(f"q{layer}", N_WQ, h2, copy_halves(qT))
                        keysT = sb(f"keysT{tag}", [P, 2 * PEER_HEADS * KEYS], into=ph)
                        top_keys(layer, tag, ph, h2, qT, keysT, idT)
                    scatter_gates(layer, tag, idT)
                early_values(layer, tag)
                experts(layer, tag, h2)

        def top_keys(layer, tag, ph, h2, qT, keysT, idT):
            first = take(EARLY)
            H2 = 2 * PEER_HEADS
            sc = sb(f"sc{tag}", [P, H2, KEYS], into=ph)
            best = sb(f"best{tag}", [P, H2, TOPK], into=ph)
            besti = sb(f"besti{tag}", [P, H2, TOPK], U32, into=ph)
            bestf = sb(f"bestf{tag}", [P, H2, TOPK], into=ph)
            idstep = sb(f"idstep{tag}", [P, H2, TOPK], into=ph)
            cand = sb(f"cand{tag}", [P, PEER_HEADS, PAIRS], into=ph)
            top = sb(f"top{tag}", [P, PEER_HEADS, TOPK], into=ph)
            posi = sb(f"posi{tag}", [P, PEER_HEADS, TOPK], U32, into=ph)
            posf = sb(f"posf{tag}", [P, ENTRIES], into=ph)
            start_of = sb(f"start_of{tag}", [P, ENTRIES], into=ph)
            passed = sb(f"passed{tag}", [P, ENTRIES, TOPK], into=ph)
            prod = sb(f"prod{tag}", [P, ENTRIES, TOPK], into=ph)
            found = sb(f"found{tag}", [P, 3, ENTRIES], into=ph)
            total = sb(f"total{tag}", [P, PEER_HEADS], into=ph)
            wide = sb(f"wide_early{tag}", [P, 2, 2, 1024], F32R, into=ph)
            gelu = sb(f"gelu_early{tag}", [P, 2, TOK], into=ph)
            ps = [pb(f"pk{tag}{j}", into=ph) for j in range(3)]
            hs = [[pb(f"he{tag}{j}{h}", into=ph) for h in range(2)] for j in range(2)]
            pt = pb(f"pt{tag}", into=ph)
            batches_begun = peer_sem("batches_begun")
            (keys_loaded, scores_done, scores_copied, sc_free, exp_in, exp_out, found_ready, turned, turned_out) = (
                peer_sem("top_" + n) for n in ("keys_loaded", "scores_done", "scores_copied", "sc_free", "exp_in",
                                           "exp_out", "found_ready", "turned", "turned_out"))
            his_done, h_done, gelu_done = (peer_sem("early_" + n) for n in ("his_done", "h_done", "gelu_done"))
            stored = [peer_sem(f"early_stored{j}") for j in range(2)]
            E = EARLY_PER_TILE
            with nc.Block() as block:
                @block.sync
                def _(sp):
                    sp.dma_start(keysT[:, :], keys[layer]).then_inc(keys_loaded, 16)

                    def store(t, e):
                        sp.wait_ge(gelu_done, t * E + (e + 3))
                        sp.dma_start(hidden_dram[bass.ds(t * E + e, 1)].rearrange("a p t -> p (a t)"), gelu[:, e % 2, :])\
                          .then_inc(stored[e % 2], 16)

                    with sp.Fori(0, TILES) as t:
                        for k in range(2):
                            for e in range(2):
                                store(t, k * HALF_RING + e)
                            sp.wait_ge(blocks_used, t * SLOTS + (first + (k + 1) * HALF_RING))
                            load_half(sp, k, t * SLOTS + (first + SLOTS + k * HALF_RING))
                            for e in range(2, 4):
                                store(t, k * HALF_RING + e)
                    for j in range(2):
                        sp.wait_ge(stored[j], 16 + 16 * EARLY // 2)

                @block.gpsimd
                def _(pool):
                    with pool.Fori(0, TILES) as t:
                        for e in range(E):
                            pool.wait_ge(his_done, t * E + (e + 1))
                            nc.gpsimd.tensor_tensor(wide[:, e % 2, 1, :], ring[:, e, :], wide[:, e % 2, 0, :].bitcast(F32),
                                                    ALU.subtract).then_inc(blocks_used, 1)

                @block.tensor
                def _(pe):
                    pe.wait_ge(keys_loaded, 16)
                    def turn(t):
                        pe.wait_ge(found_ready, t + 1)
                        if t >= 1:
                            pe.wait_ge(turned_out, t)
                        for k in range(3):
                            last = nc.tensor.transpose(pt[:, k * P:(k + 1) * P], found[:, k, :], masks[:, IDENT, :])
                        last.then_inc(turned, 1)

                    def activate(t, begin):
                        with pe.Fori(0, 2) as r:
                            for j in range(2):
                                n = t * E + begin + j
                                pe.wait_ge(blocks_used, r * 2 + (first + n + 1))
                                pe.wait_ge(gelu_done, r * 2 + (n + 1))
                                for c in range(NCH):
                                    last = split_matmuls(hs[j], wide[:, j, 0, c * P:(c + 1) * P],
                                                         wide[:, j, 1, c * P:(c + 1) * P], h2, c, c == 0, c == NCH - 1)
                                last.then_inc(h_done, 1)

                    for t in range(TILES):
                        for b in range(4):
                            if t and b < 3:
                                pe.wait_ge(scores_copied, 4 * t if b == 0 else 4 * (t - 1) + b + 1)
                            if b == 3:
                                pe.wait_ge(scores_copied, 4 * t + 1)
                            for q in range(4):
                                hz = 4 * b + q
                                last = nc.tensor.matmul(ps[b % 3][:, q * KEYS:(q + 1) * KEYS],
                                                        lhsT=qT[:, hz, t * P:(t + 1) * P],
                                                        rhs=keysT[:, hz * KEYS:(hz + 1) * KEYS], start=True, stop=True)
                            last.then_inc(scores_done, 1)
                        activate(t, 0)
                        if t:
                            turn(t - 1)
                        activate(t, 4)
                    turn(TILES - 1)

                @block.scalar
                def _(act):
                    act.sem_inc(gelu_done, 2)
                    for j in range(2):
                        act.sem_inc(stored[j], 16)

                    def hi(t, e):
                        if e % HALF_RING == 0:
                            act.wait_ge(half_loaded[e // HALF_RING % 2], (t + (first // SLOTS + e // SLOTS + 1)) * 16)
                        nc.scalar.activation(wide[:, e % 2, 0, :], ring[:, e % SLOTS, :], ACT.Copy).then_inc(his_done, 1)

                    def activate(t, e, last):
                        act.wait_ge(h_done, t * E + (e + 1))
                        act.wait_ge(stored[e % 2], (t * (E // 2) + (e // 2 + 1)) * 16)
                        for h in range(2):
                            ins = nc.scalar.activation(gelu[:, e % 2, HALVES[h]], hs[e % 2][h][:, 0:HALF_TOK], ACT.Gelu)
                        ins.then_inc(gelu_done, 1)
                        if not (last and e + 2 >= E):
                            hi(t, e + 2)

                    def copy_scores(t):
                        act.wait_ge(sc_free, t + 1)
                        for b in range(4):
                            act.wait_ge(scores_done, t * 4 + (b + 1))
                            nc.scalar.activation(sc[:, 4 * b:4 * b + 4, :].rearrange("p h k -> p (h k)"), ps[b % 3][:, :],
                                                 ACT.Copy).then_inc(scores_copied, 1)

                    def exp_of_before(t):
                        act.wait_ge(exp_in, t)
                        nc.scalar.activation(found[:, 2, :], found[:, 2, :], ACT.Exp).then_inc(exp_out, 1)

                    def keep_of_before(t):
                        act.wait_ge(turned, t + 1)
                        nc.scalar.activation(idT[:, :, bass.ds(t * P - P, P)], pt[:, 0:3 * P].rearrange("p (k n) -> p k n", k=3),
                                             ACT.Copy).then_inc(turned_out, 1)

                    def tile_steps(t, is_first, is_last):
                        copy_scores(t)
                        for e in range(E):
                            activate(t, e, is_last)
                            if e == 1 and not is_first:
                                exp_of_before(t)
                            if e == 3 and not is_first:
                                keep_of_before(t)

                    hi(0, 0)
                    hi(0, 1)
                    tile_steps(0, True, False)
                    with act.Fori(1, TILES - 1) as t:
                        tile_steps(t, False, False)
                    tile_steps(TILES - 1, False, True)
                    exp_of_before(TILES)
                    keep_of_before(TILES)

                @block.vector
                def _(dve):
                    v = nc.vector

                    def best8(ins_of, n):
                        dve_steps.settle(dve)
                        dve.sem_inc(batches_begun, 1)
                        for j in range(n):
                            dve_steps.did(ins_of(j))

                    dve.sem_inc(sc_free, 1)
                    dve.sem_inc(turned, 1)
                    H = PEER_HEADS
                    steps = 5 * H2 + 2 + 9 + 5 * H + 12
                    with dve_steps.loop(dve, TILES, steps) as t:
                        dve.wait_ge(scores_copied, t * 4 + 4)
                        best8(lambda j: v.max(best[:, j, 0:8], sc[:, j, :]), H2)
                        best8(lambda j: v.max_index(besti[:, j, 0:8], best[:, j, 0:8], sc[:, j, :]), H2)
                        best8(lambda j: v.match_replace(sc[:, j, :], best[:, j, 0:8], sc[:, j, :], NEG), H2)
                        best8(lambda j: v.max(best[:, j, 8:16], sc[:, j, :]), H2)
                        best8(lambda j: v.max_index(besti[:, j, 8:16], best[:, j, 8:16], sc[:, j, :]), H2)
                        dve_steps.settle(dve)
                        v.tensor_copy(bestf[:, :, :], besti[:, :, :]).then_inc(sc_free, 1)
                        dve.wait_ge(sc_free, t + 2)
                        dve_steps.did(v.tensor_copy(idstep[:, :, 0:1], bestf[:, :, 0:1]))
                        dve_steps.did(v.tensor_tensor(idstep[:, :, 1:TOPK], bestf[:, :, 1:TOPK], bestf[:, :, 0:TOPK - 1],
                                                      ALU.subtract))
                        bz = best[:, :, :].rearrange("p (h z) k -> p h z k", z=2)
                        for i in range(8):
                            n = PAIRS_OF[i]
                            dve_steps.did(v.tensor_tensor(
                                cand[:, :, PAIR_AT[i]:PAIR_AT[i] + n],
                                bz[:, :, 0, i:i + 1].broadcast_to([P, H, n]), bz[:, :, 1, 0:n], ALU.add))
                        dve_steps.did(v.tensor_tensor(cand[:, :, PAIR_AT[8]:PAIRS], bz[:, :, 0, 8:16],
                                                      bz[:, :, 1, 0:1].broadcast_to([P, H, 8]), ALU.add))
                        best8(lambda j: v.max(top[:, j, 0:8], cand[:, j, :]), H)
                        best8(lambda j: v.max_index(posi[:, j, 0:8], top[:, j, 0:8], cand[:, j, :]), H)
                        best8(lambda j: v.match_replace(cand[:, j, :], top[:, j, 0:8], cand[:, j, :], NEG), H)
                        best8(lambda j: v.max(top[:, j, 8:16], cand[:, j, :]), H)
                        best8(lambda j: v.max_index(posi[:, j, 8:16], top[:, j, 8:16], cand[:, j, :]), H)
                        dve_steps.settle(dve)
                        dve.wait_ge(turned, t + 1)
                        f3 = lambda k: found[:, k, :].rearrange("p (h r) -> p h r", h=H)
                        dve_steps.did(v.tensor_copy(posf[:, :].rearrange("p (h r) -> p h r", h=H), posi[:, :, :]))
                        v.tensor_tensor(f3(2), top[:, :, :], top[:, :, 0:1].broadcast_to([P, H, TOPK]),
                                        ALU.subtract).then_inc(exp_in, 1)

                        def ranks(table):
                            return bcast(table, 1, ENTRIES)

                        def lookup(dst, steps_of):
                            dve_steps.settle(dve)
                            dve_steps.did(v.tensor_tensor(
                                prod[:, :, :].rearrange("p (h r) m -> p h r m", h=H),
                                passed[:, :, :].rearrange("p (h r) m -> p h r m", h=H), steps_of, ALU.mult))
                            dve_steps.settle(dve)
                            dve_steps.did(v.tensor_reduce(dst, prod[:, :, :], AX.X, ALU.add))

                        dve_steps.settle(dve)
                        dve_steps.did(v.tensor_tensor(passed[:, :, :], bcast(posf[:, :], 2, TOPK), ranks(row("pair_at")), ALU.is_ge))
                        lookup(start_of[:, :], bcast(bcast(row("pairs_before"), 1, TOPK), 1, H))
                        iz = idstep[:, :, :].rearrange("p (h z) k -> p h z k", z=2)
                        lookup(found[:, 0, :], bcast(iz[:, :, 0, :], 2, TOPK))
                        dve_steps.settle(dve)
                        dve_steps.did(v.tensor_tensor(posf[:, :], posf[:, :], start_of[:, :], ALU.subtract))
                        dve_steps.settle(dve)
                        dve_steps.did(v.tensor_tensor(passed[:, :, :], bcast(posf[:, :], 2, TOPK), ranks(row("rank")), ALU.is_ge))
                        lookup(found[:, 1, :], bcast(iz[:, :, 1, :], 2, TOPK))
                        dve.wait_ge(exp_out, t + 1)
                        dve_steps.did(v.tensor_reduce(total[:, :], f3(2), AX.X, ALU.add))
                        dve_steps.settle(dve)
                        dve_steps.did(v.reciprocal(total[:, :], total[:, :]))
                        dve_steps.settle(dve)
                        v.tensor_tensor(f3(2), f3(2), bcast(total[:, :], 2, TOPK), ALU.mult).then_inc(found_ready, 1)

        def scatter_gates(layer, tag, idT):
            HOTS, EACH = 4, 4
            PIECES = TOK // SCATTER_TOK
            ROUNDS = SCATTER_TOK // (HOTS * EACH)
            with ExitStack() as ph:
                staged = sb(f"staged{tag}", [P, 2, KEYS, SCATTER_TOK], into=ph)
                hot1 = sb(f"hot1{tag}", [P, HOTS, EACH, KEYS], into=ph)
                hot2 = sb(f"hot2{tag}", [P, HOTS, EACH, KEYS], into=ph)
                ps = [pb(f"pg{tag}{j}", into=ph) for j in range(4)]
                diff_ready, squared, last_ready, hots_ready, hots_used, g_copied = (
                    peer_sem("scatter_" + n) for n in ("diff_ready", "squared", "last_ready", "hots_ready",
                                                       "hots_used", "g_copied"))
                staged_free = [peer_sem(f"staged_free{j}") for j in range(2)]
                iota = bcast(row("iota"), 1, EACH)

                def entries(r, i, b):
                    return bcast(idT[:, r, bass.ds(i * (HOTS * EACH) + b * EACH, EACH)], 2, KEYS)

                with nc.Block() as block:
                    @block.vector
                    def _(dve):
                        with dve.Fori(0, TOK // (HOTS * EACH)) as i:
                            for b in range(HOTS):
                                dve.wait_ge(hots_used, i * HOTS + (b + 1))
                                if b < HOTS - 1:
                                    nc.vector.tensor_tensor(hot2[:, b, :, :], iota, entries(1, i, b), ALU.is_equal)
                                dve.wait_ge(diff_ready, i * HOTS + (b + 1))
                                hot = hot1[:, b, :, :]
                                nc.vector.scalar_tensor_tensor(hot, in0=hot, scalar=0.0, in1=entries(2, i, b),
                                                               op0=ALU.is_equal, op1=ALU.mult).then_inc(hots_ready, 1)

                    @block.gpsimd
                    def _(pool):
                        pool.sem_inc(hots_used, HOTS)
                        with pool.Fori(0, TOK // (HOTS * EACH)) as i:
                            for b in range(HOTS):
                                pool.wait_ge(hots_used, i * HOTS + (b + 1))
                                nc.gpsimd.tensor_tensor(hot1[:, b, :, :], iota, entries(0, i, b),
                                                        ALU.subtract).then_inc(diff_ready, 1)

                    @block.tensor
                    def _(pe):
                        with pe.Fori(0, TOK // (HOTS * EACH)) as i:
                            for b in range(HOTS):
                                pe.wait_ge(hots_ready, i * HOTS + (b + 1))
                                if b == HOTS - 1:
                                    pe.wait_ge(last_ready, i + 1)
                                pe.wait_ge(g_copied, i * HOTS + (b + 1))
                                for j in range(EACH):
                                    last = nc.tensor.matmul(ps[b][:, j * P:(j + 1) * P], lhsT=hot2[:, b, j, :],
                                                            rhs=hot1[:, b, j, :], start=True, stop=True)
                                last.then_inc(hots_used, 1)

                    @block.scalar
                    def _(act):
                        act.sem_inc(g_copied, HOTS)
                        with act.Fori(0, PIECES // 2) as w:
                            for buf in range(2):
                                act.wait_ge(staged_free[buf], w * 16 + 16)
                                with act.Fori(0, ROUNDS) as r:
                                    b = HOTS - 1
                                    act.wait_ge(hots_used, w * (2 * HOTS * ROUNDS) + r * HOTS + (buf * HOTS * ROUNDS + b + 1))
                                    for j in range(EACH):
                                        token = w * (2 * SCATTER_TOK) + r * (HOTS * EACH) + (buf * SCATTER_TOK + b * EACH + j)
                                        last = nc.scalar.activation(hot2[:, b, j, :], row("iota"), ACT.Square,
                                                                    bias=idT[:, 1, bass.ds(token, 1)], scale=-1.0)
                                    last.then_inc(squared, 1)
                                    act.wait_ge(squared, w * (2 * ROUNDS) + r + (buf * ROUNDS + 1))
                                    h = hot2[:, b, :, :].rearrange("p t k -> p (t k)")
                                    nc.scalar.activation(h, h, ACT.Relu, bias=masks[:, ONES, 0:1], scale=-1.0).then_inc(last_ready, 1)
                                    for b in range(HOTS):
                                        act.wait_ge(hots_used, w * (2 * HOTS * ROUNDS) + r * HOTS + (buf * HOTS * ROUNDS + b + 1 + HOTS))
                                        nc.scalar.activation(staged[:, buf, :, bass.ds(r * (HOTS * EACH) + b * EACH, EACH)],
                                                             ps[b][:, :].rearrange("p (t i) -> p i t", t=EACH),
                                                             ACT.Copy).then_inc(g_copied, 1)

                    @block.sync
                    def _(sp):
                        for buf in range(2):
                            sp.sem_inc(staged_free[buf], 16)
                        with sp.Fori(0, PIECES // 2) as w:
                            for buf in range(2):
                                sp.wait_ge(g_copied, w * (2 * HOTS * ROUNDS) + ((buf + 1) * HOTS * ROUNDS + HOTS))
                                sp.dma_start(gates_dram[w * 2 + buf], staged[:, buf, :, :]).then_inc(staged_free[buf], 16)
                        for buf in range(2):
                            sp.wait_ge(staged_free[buf], (PIECES // 2 + 1) * 16)

        def early_values(layer, tag):
            first = take(EARLY)
            PAIRS_PER_ROUND = SLOTS // 2
            ROUNDS_ = EARLY // SLOTS
            with ExitStack() as ph:
                wide = sb(f"wide_ev{tag}", [P, 4, 2, 1024], F32R, into=ph)
                acts = sb(f"acts_ev{tag}", [P, 4, 2, TOK], F32R, into=ph)
                hidden = sb(f"hidden_ev{tag}", [P, 2, 2, TOK], into=ph)
                gbuf = sb(f"gbuf_ev{tag}", [P, 2, TOK // SCATTER_TOK, 2, SCATTER_TOK], into=ph)
                by_piece = lambda ap: ap.rearrange("p (w t) -> p w t", t=SCATTER_TOK)
                outs = [[pb(f"ov{tag}{j}{h}", into=ph) for h in range(2)] for j in range(4)]
                his_done, acts_done, outs_done, outs_free = (
                    peer_sem("ev_" + n) for n in ("his_done", "acts_done", "outs_done", "outs_free"))
                factors_in = [peer_sem(f"ev_factors_in{j}") for j in range(2)]

                def rounds(eng, body):
                    with eng.Fori(0, ROUNDS_ - 1) as r:
                        for k in range(PAIRS_PER_ROUND):
                            body(r * PAIRS_PER_ROUND, k, False)
                    for k in range(PAIRS_PER_ROUND):
                        body((ROUNDS_ - 1) * PAIRS_PER_ROUND, k, True)

                with nc.Block() as block:
                    @block.sync
                    def _(sp):
                        def load_factors(m, k):
                            j, at_ = k % 2, m * 2 + 2 * k
                            sp.dma_start(gbuf[:, j, :, :, :].rearrange("p w b t -> p w (b t)"),
                                         gates_dram[:, :, bass.ds(at_, 2), :].rearrange("w p b t -> p w (b t)"))\
                              .then_inc(factors_in[j], 16)
                            sp.dma_start(hidden[:, j, :, :], hidden_dram[bass.ds(at_, 2)].rearrange("b p t -> p b t"))\
                              .then_inc(factors_in[j], 16)

                        def step(m, k, last):
                            if k % 2 == 1:
                                sp.wait_ge(blocks_used, m * 2 + (first + 2 * k + 2))
                                load_half(sp, k // 2, m * 2 + (first + SLOTS + (k // 2) * HALF_RING))
                            if not (last and k >= PAIRS_PER_ROUND - 2):
                                sp.wait_ge(acts_done, m * 2 + (2 * k + 2))
                                load_factors(m, k + 2)

                        for k in range(2):
                            load_factors(0, k)
                        rounds(sp, step)

                    @block.scalar
                    def _(act):
                        with act.Fori(0, ROUNDS_) as r:
                            for e in range(SLOTS):
                                loaded(act, e, r + first // SLOTS)
                                if e % 2 == 0:
                                    act.wait_ge(outs_done, r * (NCH * PAIRS_PER_ROUND) + NCH * (e // 2 + 1))
                                nc.scalar.activation(wide[:, e % 4, 0, :], ring[:, e, :], ACT.Copy).then_inc(his_done, 1)

                    @block.gpsimd
                    def _(pool):
                        with pool.Fori(0, ROUNDS_) as r:
                            for e in range(SLOTS):
                                pool.wait_ge(his_done, r * SLOTS + (e + 1))
                                nc.gpsimd.tensor_tensor(wide[:, e % 4, 1, :], ring[:, e, :], wide[:, e % 4, 0, :].bitcast(F32),
                                                        ALU.subtract).then_inc(blocks_used, 1)

                    @block.tensor
                    def _(pe):
                        pe.sem_inc(outs_done, 2 * NCH)
                        with pe.Fori(0, EARLY // 4) as r:
                            for k in range(2):
                                pe.wait_ge(blocks_used, r * 4 + (first + 2 * k + 2))
                                pe.wait_ge(acts_done, r * 4 + (2 * k + 2))
                                for d in range(NCH):
                                    pe.wait_ge(outs_free, r * (2 * NCH) + (NCH * k + d + 1))
                                    for e in range(2):
                                        last = split_matmuls(outs[d % 4], wide[:, 2 * k + e, 0, d * P:(d + 1) * P],
                                                             wide[:, 2 * k + e, 1, d * P:(d + 1) * P], acts, 2 * k + e,
                                                             e == 0, e == 1)
                                    last.then_inc(outs_done, 1)

                    @block.vector
                    def _(dve):
                        dve.sem_inc(outs_free, 4)

                        def factors(m, k):
                            j = k % 2
                            dve.wait_ge(factors_in[j], m * 16 + (k // 2 + 1) * 32)
                            for e in range(2):
                                a = hidden[:, j, e, :]
                                dve_steps.did(nc.vector.tensor_tensor(by_piece(a), by_piece(a), gbuf[:, j, :, e, :], ALU.mult))
                            dve_steps.settle(dve)
                            for e in range(2):
                                dve_steps.did(nc.vector.tensor_copy(acts[:, 2 * j + e, 0, :], hidden[:, j, e, :]))
                            dve_steps.settle(dve)
                            for e in range(2):
                                nc.vector.tensor_tensor(acts[:, 2 * j + e, 1, :], hidden[:, j, e, :],
                                                        acts[:, 2 * j + e, 0, :].bitcast(F32), ALU.subtract).then_inc(acts_done, 1)

                        def step(m, k, last):
                            if not (last and k == PAIRS_PER_ROUND - 1):
                                factors(m, k + 1)
                            for d in range(NCH):
                                dve.wait_ge(outs_done, m * NCH + (NCH * k + d + 1 + 2 * NCH))
                                for c, part, h, at_ in PARTS:
                                    ins = nc.vector.scalar_tensor_tensor(
                                        xT[:, d, part], in0=outs[d % 4][h][:, at_], scalar=mods[:, G2 * NCH + d, c:c + 1],
                                        in1=xT[:, d, part], op0=ALU.mult, op1=ALU.add)
                                ins.then_inc(outs_free, 1)

                        factors(0, 0)
                        with dve_steps.loop(dve, ROUNDS_ - 1, 4 * PAIRS_PER_ROUND) as r:
                            for k in range(PAIRS_PER_ROUND):
                                step(r * PAIRS_PER_ROUND, k, False)
                        for k in range(PAIRS_PER_ROUND):
                            step((ROUNDS_ - 1) * PAIRS_PER_ROUND, k, True)

        def experts(layer, tag, h2):
            first = take(N_LATE)
            NB = BLOCKS_PER_GROUP
            NGROUPS = (EXPERT_BLOCKS - EARLY) // NB
            ROUND0 = first // SLOTS
            more = at[0] < N_BLOCKS
            with ExitStack() as ph:
                wide_u = sb(f"wide_u{tag}", [P, 2, 2, 1024], F32R, into=ph)
                wide_v = sb(f"wide_v{tag}", [P, NB, 2, 1024], F32R, into=ph)
                acts = sb(f"acts{tag}", [P, NB, 2, TOK], F32R, into=ph)
                gelu = sb(f"gelu{tag}", [P, 2, TOK], into=ph)
                gbuf = sb(f"gbuf{tag}", [P, 2, TOK // SCATTER_TOK, 2, SCATTER_TOK], into=ph)
                by_piece = lambda ap: ap.rearrange("p (w t) -> p w t", t=SCATTER_TOK)
                hs = [[pb(f"hs{tag}{j}{h}", into=ph) for h in range(2)] for j in range(2)]
                outs = [[pb(f"os{tag}{j}{h}", into=ph) for h in range(2)] for j in range(2)]
                his_done, u_split, v_split, h_done, gelu_done, acts_done, outs_done, outs_free = (
                    peer_sem("ex_" + n) for n in ("his_done", "u_split", "v_split", "h_done", "gelu_done", "acts_done",
                                               "outs_done", "outs_free"))
                gates_in = [peer_sem(f"gates_in{j}") for j in range(2)]

                def groups(eng, body):
                    with eng.Fori(0, NGROUPS - 1) as g:
                        body(g, False)
                    body(NGROUPS - 1, True)

                with nc.Block() as block:
                    @block.sync
                    def _(sp):
                        def load_gates(j, block_):
                            sp.dma_start(gbuf[:, j, :, :, :].rearrange("p w b t -> p w (b t)"),
                                         gates_dram[:, :, bass.ds(block_, 2), :].rearrange("w p b t -> p w (b t)"))\
                              .then_inc(gates_in[j], 16)

                        def group(g, last):
                            def ring_half(k, split):
                                if last and not more:
                                    return
                                sp.wait_ge(split, g * NB + NB)
                                load_half(sp, k, g * SLOTS + (first + SLOTS + k * HALF_RING))

                            for k, split in ((0, u_split), (1, v_split)):
                                ring_half(k, split)
                                if not last:
                                    sp.wait_ge(acts_done, g * NB + (2 * k + 4))
                                    load_gates(k, g * NB + (EARLY + NB + 2 * k))

                        for j in range(2):
                            load_gates(j, EARLY + 2 * j)
                        groups(sp, group)
                        sp.wait_ge(v_split, NB * NGROUPS)
                        sp.wait_ge(u_split, NB * NGROUPS)
                        sp.sem_inc(blocks_used, N_LATE)

                    def split_order(hi_or_lo_u, hi_or_lo_v, g, last, before=lambda e: None):
                        for e, of_v in enumerate(((0, 1), (2,), (3,), ())):
                            before(e)
                            if e < 2:
                                hi_or_lo_u(g, e + 2)
                            for v in of_v:
                                hi_or_lo_v(g, v)
                            if e >= 2 and not last:
                                hi_or_lo_u(g, e + 2)

                    @block.scalar
                    def _(act):
                        act.sem_inc(gelu_done, 2)

                        def hi_u(g, e):
                            if e % NB == 0:
                                act.wait_ge(half_loaded[0], (g + (ROUND0 + e // NB + 1)) * 16)
                            nc.scalar.activation(wide_u[:, e % 2, 0, :], ring[:, e % NB, :], ACT.Copy).then_inc(his_done, 1)

                        def hi_v(g, e):
                            if e == 0:
                                act.wait_ge(half_loaded[1], (g + (ROUND0 + 1)) * 16)
                            nc.scalar.activation(wide_v[:, e, 0, :], ring[:, NB + e, :], ACT.Copy).then_inc(his_done, 1)

                        def group(g, last):
                            def gelus(e):
                                act.wait_ge(h_done, g * NB + (e + 1))
                                act.wait_ge(acts_done, g * NB + (e + 1))
                                for h in range(2):
                                    ins = nc.scalar.activation(gelu[:, e % 2, HALVES[h]], hs[e % 2][h][:, 0:HALF_TOK], ACT.Gelu)
                                ins.then_inc(gelu_done, 1)
                            split_order(hi_u, hi_v, g, last, gelus)

                        hi_u(0, 0)
                        hi_u(0, 1)
                        groups(act, group)

                    @block.gpsimd
                    def _(pool):
                        def lo(dst, slot, n, done):
                            pool.wait_ge(his_done, n)
                            nc.gpsimd.tensor_tensor(dst[:, 1, :], ring[:, slot, :], dst[:, 0, :].bitcast(F32),
                                                    ALU.subtract).then_inc(done, 1)

                        def group(g, last):
                            n = [2]

                            def lo_u(g, e):
                                n[0] += 1
                                lo(wide_u[:, e % 2, :, :], e % NB, g * (2 * NB) + n[0], u_split)

                            def lo_v(g, e):
                                n[0] += 1
                                lo(wide_v[:, e, :, :], NB + e, g * (2 * NB) + n[0], v_split)

                            split_order(lo_u, lo_v, g, last)

                        for e in range(2):
                            lo(wide_u[:, e, :, :], e, e + 1, u_split)
                        groups(pool, group)

                    @block.tensor
                    def _(pe):
                        with pe.Fori(0, NGROUPS) as g:
                            for e in range(NB):
                                pe.wait_ge(u_split, g * NB + (e + 1))
                                pe.wait_ge(gelu_done, g * NB + (e + 1))
                                for c in range(NCH):
                                    last = split_matmuls(hs[e % 2], wide_u[:, e % 2, 0, c * P:(c + 1) * P],
                                                         wide_u[:, e % 2, 1, c * P:(c + 1) * P], h2, c, c == 0, c == NCH - 1)
                                last.then_inc(h_done, 1)
                            order = [(d, e) for d in (0, 1) for e in range(NB - 1)] + [(0, NB - 1), (1, NB - 1)]
                            order += [(d, e) for d in range(2, NCH) for e in range(NB)]
                            for d, e in order:
                                if e == 0:
                                    pe.wait_ge(outs_free, g * NCH + (d + 1))
                                if d == 0:
                                    pe.wait_ge(v_split, g * NB + (e + 1))
                                    pe.wait_ge(acts_done, g * NB + (e + 3))
                                last = split_matmuls(outs[d % 2], wide_v[:, e, 0, d * P:(d + 1) * P],
                                                     wide_v[:, e, 1, d * P:(d + 1) * P], acts, e, e == 0, e == NB - 1)
                                if e == NB - 1:
                                    last.then_inc(outs_done, 1)

                    @block.vector
                    def _(dve):
                        dve.sem_inc(acts_done, 2)
                        dve.sem_inc(outs_free, 2)
                        with dve_steps.loop(dve, NGROUPS, 2 * NB) as g:
                            for e in range(NB):
                                if e % 2 == 0:
                                    dve.wait_ge(gates_in[e // 2], g * 16 + 16)
                                dve.wait_ge(gelu_done, g * NB + (e + 3))
                                a = gelu[:, e % 2, :]
                                dve_steps.did(nc.vector.tensor_tensor(by_piece(a), by_piece(a), gbuf[:, e // 2, :, e % 2, :],
                                                                      ALU.mult))
                                dve_steps.settle(dve)
                                dve_steps.did(nc.vector.tensor_copy(acts[:, e, 0, :], a))
                                dve_steps.settle(dve)
                                nc.vector.tensor_tensor(acts[:, e, 1, :], a, acts[:, e, 0, :].bitcast(F32),
                                                        ALU.subtract).then_inc(acts_done, 1)
                            for d in range(NCH):
                                dve.wait_ge(outs_done, g * NCH + (d + 1))
                                for k, part, h, at_ in PARTS:
                                    last = nc.vector.scalar_tensor_tensor(
                                        xT[:, d, part], in0=outs[d % 2][h][:, at_], scalar=mods[:, G2 * NCH + d, k:k + 1],
                                        in1=xT[:, d, part], op0=ALU.mult, op1=ALU.add)
                                last.then_inc(outs_free, 1)

        def ssd_mixer():
            with ExitStack() as ph:
                Y = sb("Y", [P, TILES, SSM_INNER], into=ph)
                with ExitStack() as h_life:
                    hT = sb("hT", [P, NCH, TOK], into=h_life)
                    norm_modulate("m1", hT, scale_of(scale_mix), shift_of(SH1))
                    ssd_scan(Y, hT)
                    gate_by_z(Y, hT)
                yT = sb("yT", [P, SSM_INNER // P, TOK], into=ph)
                norm_y(Y, yT)
                project("ssd_out", N_SSD_OUT, yT, add_gated(G1), dve_evac=True, chunks=2 * NCH)

        def ssd_scan(Y, hT):
            first = take(N_SSD)
            with ExitStack() as ph:
                W64 = 2 * HEADS
                DT_N = 96
                wdt_s = sb("wdt_s", [P, NCH + 1, W64], into=ph)
                dt = sb("dt", [P, TILES, W64], into=ph)
                dA = sb("dA", [P, TILES, W64], into=ph)
                t1 = sb("dt_t1", [P, TILES, W64], into=ph)
                t2 = sb("dt_t2", [P, TILES, W64], into=ph)
                t3 = sb("dt_t3", [P, TILES, W64], into=ph)
                negA = sb("negA", [P, W64], into=ph)
                decay = sb("decay", [P, TILES, 6 * HEADS], into=ph)
                IN_F, OUT_F, IN_B, OUT_B, ALL_F, ALL_B = (HEADS * k for k in range(6))
                state_w = sb("state_w", [P, TILES, W64], into=ph)
                with ExitStack() as pp:
                    pdt = pb("pdt", into=pp)
                    pdec = [pb(f"pdec{j}", into=pp) for j in range(6)]
                    tiles_of = lambda at_: pdec[at_ // HEADS][:, 0:TILES * HEADS].rearrange("p (t h) -> p t h", t=TILES)
                    wdt_loaded, pad_ready, dt_done, dt_act, dA_done, dec_done, dec_exp = (
                        sem(n) for n in ("wdt_loaded", "pad_ready", "dt_done", "dt_act", "dA_done", "dec_done", "dec_exp"))
                    with nc.Block() as block:
                        @block.sync
                        def _(sp):
                            sp.dma_start(wdt_s[:, 0:NCH, :], wdt).then_inc(wdt_loaded, 16)

                        @block.tensor
                        def _(pe):
                            pe.wait_ge(wdt_loaded, 16)
                            pe.wait_ge(pad_ready, 1)
                            wdt_row = wdt_s[:, :, :].rearrange("p c h -> p (c h)")
                            for t in range(TILES):
                                for c in range(NCH):
                                    last = nc.tensor.matmul(pdt[:, t * W64:t * W64 + DT_N], lhsT=hT[:, c, t * P:(t + 1) * P],
                                                            rhs=wdt_row[:, c * W64:c * W64 + DT_N], start=c == 0, stop=c == NCH - 1)
                            last.then_inc(dt_done, 1)
                            pe.wait_ge(dA_done, 1)
                            f, b = dA[:, :, 0:HEADS], dA[:, :, HEADS:W64]
                            for at_, m, rhs in ((IN_F, LE, f), (OUT_F, GT, f), (IN_B, GE, b), (OUT_B, LT, b),
                                                (ALL_F, ONES, f), (ALL_B, ONES, b)):
                                last = nc.tensor.matmul(tiles_of(at_), lhsT=masks[:, m, :], rhs=rhs, start=True, stop=True)
                            last.then_inc(dec_done, 1)

                        @block.scalar
                        def _(act):
                            nc.scalar.activation(negA[:, :], row("a_log"), ACT.Exp).then_inc(dt_act, 1)
                            act.wait_ge(dt_act, 2)
                            nc.scalar.activation(t2[:, :, :], t2[:, :, :], ACT.Exp).then_inc(dt_act, 1)
                            act.wait_ge(dt_act, 4)
                            nc.scalar.activation(t3[:, :, :], t1[:, :, :], ACT.Ln).then_inc(dt_act, 1)
                            act.wait_ge(dec_done, 1)
                            for at_ in (IN_F, OUT_F, IN_B, OUT_B, ALL_F, ALL_B):
                                nc.scalar.activation(decay[:, :, at_:at_ + HEADS], tiles_of(at_), ACT.Exp).then_inc(dec_exp, 1)

                        @block.vector
                        def _(dve):
                            v = nc.vector

                            def step(ins):
                                dve_steps.did(ins)
                                dve_steps.settle(dve)

                            v.memset(wdt_s[:, NCH, :], 0.0).then_inc(pad_ready, 1)
                            dve.wait_ge(dt_done, 1)
                            step(v.tensor_tensor(dt[:, :, :], pdt[:, 0:TILES * W64].rearrange("p (t h) -> p t h", t=TILES),
                                                 bcast(row("dt_bias"), 1, TILES), ALU.add))
                            dve.wait_ge(dt_act, 1)
                            v.scalar_tensor_tensor(t2[:, :, :], in0=dt[:, :, :], scalar=-1.0, in1=dt[:, :, :],
                                                   op0=ALU.mult, op1=ALU.min).then_inc(dt_act, 1)
                            step(v.tensor_scalar(dt[:, :, :], dt[:, :, :], 0.0, None, ALU.max))
                            dve.wait_ge(dt_act, 3)
                            v.tensor_scalar(t1[:, :, :], t2[:, :, :], 1.0, None, ALU.add).then_inc(dt_act, 1)
                            dve.wait_ge(dt_act, 5)
                            step(v.tensor_scalar(dA[:, :, :], t1[:, :, :], 1.0, None, ALU.is_equal))
                            step(v.scalar_tensor_tensor(t1[:, :, :], in0=t1[:, :, :], scalar=-1.0, in1=dA[:, :, :],
                                                        op0=ALU.add, op1=ALU.add))
                            step(v.tensor_tensor(t3[:, :, :], t3[:, :, :], dA[:, :, :], ALU.add))
                            step(v.reciprocal(t1[:, :, :], t1[:, :, :]))
                            step(v.tensor_tensor(t3[:, :, :], t3[:, :, :], t2[:, :, :], ALU.mult))
                            step(v.tensor_tensor(t3[:, :, :], t3[:, :, :], t1[:, :, :], ALU.mult))
                            step(v.tensor_tensor(dt[:, :, :], dt[:, :, :], t3[:, :, :], ALU.add))
                            v.scalar_tensor_tensor(dA[:, :, :], in0=dt[:, :, :], scalar=-1.0,
                                                   in1=bcast(negA[:, :], 1, TILES), op0=ALU.mult, op1=ALU.mult).then_inc(dA_done, 1)
                            dve.wait_ge(dec_exp, 6)
                            v.tensor_tensor(state_w[:, :, 0:HEADS], dt[:, :, 0:HEADS], decay[:, :, OUT_F:OUT_F + HEADS], ALU.mult)
                            v.tensor_tensor(state_w[:, :, HEADS:W64], dt[:, :, HEADS:W64], decay[:, :, OUT_B:OUT_B + HEADS], ALU.mult)
                scan_groups(Y, hT, first, dt, dA, decay, state_w)

        def scan_groups(Y, hT, first, dt, dA, decay, state_w):
            IN_F, OUT_F, IN_B, OUT_B, ALL_F, ALL_B = (HEADS * k for k in range(6))
            LAST = SAMPLE_TILES - 1
            OWN = [(3, 1), (2, 1), (1, 1), (0, 0), (1, 0), (2, 0), (SAMPLE_TILES, 0), (SAMPLE_TILES, 1)]
            NST = len(OWN)
            GROUPS_ = SSM_GROUPS
            YN = 96
            with ExitStack() as ph:
                PADDED = 8 * (GRID_W + 2) + PROMPT + 2
                upad = sb("su", [P, 2, PADDED], into=ph)
                conv = sb("sv", [P, 2, PADDED], into=ph)
                xch = sb("xch", [P, 2, TOK], into=ph)
                bc = sb("bc", [P, 2, 2, TOK], into=ph)
                tokm = sb("tokm", [P, TILES, 3 * P], into=ph)
                xdt = sb("xdt", [P, 2, 2, GW + YN - HEADDIM], into=ph)
                xw = sb("xw", [P, 4, GW], into=ph)
                xD = sb("xD", [P, GW], into=ph)
                spans = sb("spans", [P, 2, HPG, P], into=ph)
                E = sb("E", [P, HPG, P], into=ph)
                CBm = sb("CBm", [P, 2, P], into=ph)
                mix = sb("mix", [P, 2, 2, HPG, P], into=ph)
                off = sb("off", [P, 2, GW], into=ph)
                SF = sb("SF", [P, SAMPLE_TILES, GW], into=ph)
                SB = sb("SB", [P, SAMPLE_TILES, GW], into=ph)
                last_s = sb("last_s", [P, 2, GW], into=ph)
                ps = [pb(f"gs{h}", into=ph) for h in range(2)]
                p_t = pb("p_t", into=ph)
                p_seg = pb("p_seg", into=ph)
                p_cb = pb("p_cb", into=ph)
                p_y = pb("p_y", into=ph)
                p_off = pb("p_off", into=ph)
                p_st = pb("p_st", into=ph)
                turn_bank = [p_t, p_y]
                st_bank = [p_st, p_off, p_y, p_cb]
                S = {n: sem("scan_" + n) for n in (
                    "init_in", "proj", "copied", "conved", "silued", "turned", "turned_out", "weighted", "spanned",
                    "seg", "exped", "cb", "cb_used", "mixed", "y", "y_used", "off", "st", "st_used", "states",
                    "final", "final_out", "last_free", "dma_turns")}

                def groups(eng, body):
                    with eng.Fori(0, GROUPS_ // 2 - 1) as r:
                        for j in range(2):
                            body(lambda per, k: r * (2 * per) + (j * per + k), j, False)
                    for j in range(2):
                        body(lambda per, k: (GROUPS_ - 2 + j) * per + k, j, j == 1)

                def channel_block(n, b, ahead):
                    return n(2, 2 * ahead + b) if b < 2 else n(1, ahead + (16 if b == 2 else 24))

                with nc.Block() as block:
                    @block.sync
                    def _(sp):
                        feed(sp, first, N_SSD)

                    @block.gpsimd
                    def _(pool):
                        p = nc.gpsimd
                        pool.sem_inc(S["last_free"], 1)
                        pool.sem_inc(S["exped"], 1)
                        with pool.Fori(0, SSM_GROUPS) as g:
                            pool.wait_ge(S["y_used"], g * TILES + 1)
                            pool.sem_inc(S["dma_turns"], 1)
                            pool.dma_start(SF[:, 0, :], state_in[g][:, 0, :]).then_inc(S["init_in"], 16)
                            pool.dma_start(SB[:, LAST, :], state_in[g][:, 1, :]).then_inc(S["init_in"], 16)
                            for t in range(TILES):
                                pool.wait_ge(S["seg"], g * TILES + (t + 1))
                                for d, m in ((0, GT), (1, LT)):
                                    last = p.tensor_tensor(
                                        spans[:, d, :, :], bcast(masks[:, m, :], 1, HPG),
                                        bcast(dA[:, t, bass.ds(g * HPG + d * HEADS, HPG)], 2, P), ALU.mult)
                                last.then_inc(S["spanned"], 1)
                                if t == 0:
                                    pool.wait_ge(S["final"], g + 1)
                                    pool.sem_inc(S["dma_turns"], 1)
                                    pool.dma_start(state_out[g], last_s[:, :, :]).then_inc(S["final_out"], 16)
                            pool.wait_ge(S["final_out"], g * 16 + 16)
                            pool.sem_inc(S["last_free"], 1)

                    @block.tensor
                    def _(pe):
                        mm = nc.tensor.matmul
                        pe.sem_inc(S["seg"], 1)
                        pe.sem_inc(S["copied"], 1)

                        def project_block(n, half, b, of_next):
                            k = b + (4 if of_next else 0)
                            if b == 0:
                                pe.wait_ge(half_loaded[half], n(8, (8 if of_next else 0) + 16 * (first // SLOTS) + 16 - 8 * half))
                            pe.wait_ge(S["copied"], n(4, k + 1))
                            for c in range(NCH):
                                for h in range(2):
                                    last = mm(ps[h][:, 0:HALF_TOK], lhsT=ring[:, HALF_RING * half + b, c * P:(c + 1) * P],
                                              rhs=hT[:, c, HALVES[h]], start=c == 0, stop=c == NCH - 1)
                            last.then_inc(blocks_used, 1)

                        def cb_and_seg(n, j, t):
                            tok = slice(t * P, (t + 1) * P)
                            pe.wait_ge(S["cb_used"], n(TILES, t + 1))
                            mm(p_cb[:, 0:P], lhsT=bc[:, j, 0, tok], rhs=bc[:, j, 1, tok], start=True,
                               stop=True).then_inc(S["cb"], 1)
                            pe.wait_ge(S["spanned"], n(TILES, t + 1))
                            pe.wait_ge(S["exped"], n(TILES, t + 1))
                            for h in range(HPG):
                                mm(p_seg[:, h * P:(h + 1) * P], lhsT=spans[:, 0, h, :], rhs=masks[:, LE, :],
                                   start=True, stop=False)
                                last = mm(p_seg[:, h * P:(h + 1) * P], lhsT=spans[:, 1, h, :],
                                          rhs=masks[:, GE, :], start=False, stop=True)
                            last.then_inc(S["seg"], 1)

                        def body(n, j, last_group):
                            def next_block(b):
                                if not last_group:
                                    project_block(n, 1 - j, b, True)

                            pe.wait_ge(S["silued"], n(4, 3))
                            pe.wait_ge(S["y_used"], n(TILES, 1))
                            for t in range(TILES):
                                pe.wait_ge(S["turned_out"], n(TILES, t + 1))
                                for b in range(3):
                                    src = bc[:, j, 0, :] if b == 2 else xch[:, b, :]
                                    last = nc.tensor.transpose(turn_bank[t % 2][:, b * P:(b + 1) * P], src[:, t * P:(t + 1) * P],
                                                               masks[:, IDENT, :])
                                last.then_inc(S["turned"], 1)
                            pe.wait_ge(S["turned_out"], n(TILES, TILES + 2))
                            for k, (t, d) in enumerate(OWN):
                                if k == 4:
                                    next_block(0)
                                pe.wait_ge(S["weighted"], n(NST, k + 1))
                                pe.wait_ge(S["st_used"], n(NST, k + 1))
                                mm(st_bank[k % 4][:, 0:GW], lhsT=tokm[:, t, 2 * P:3 * P], rhs=xw[:, k % 4, :],
                                   start=True, stop=True).then_inc(S["st"], 1)
                            next_block(1)
                            pe.wait_ge(S["silued"], n(4, 4))
                            pe.wait_ge(S["states"], n(1, 1))
                            cb_and_seg(n, j, 0)
                            next_block(2)
                            for t in range(TILES):
                                if t + 1 < TILES:
                                    cb_and_seg(n, j, t + 1)
                                if t == 1:
                                    next_block(3)
                                tok = slice(t * P, (t + 1) * P)
                                pe.wait_ge(S["y_used"], n(TILES, t + 1))
                                if t < SAMPLE_TILES:
                                    mm(p_off[:, 0:GW], lhsT=bc[:, j, 1, tok], rhs=SF[:, t, :], start=True, stop=True)
                                    mm(p_off[:, GW:2 * GW], lhsT=bc[:, j, 1, tok], rhs=SB[:, t, :], start=True,
                                       stop=True).then_inc(S["off"], 1)
                                pe.wait_ge(S["mixed"], n(TILES, t + 2))
                                for h in range(HPG):
                                    out = p_y[:, h * HEADDIM:h * HEADDIM + YN]
                                    for d in range(2):
                                        last = mm(out, lhsT=mix[:, t % 2, d, h, :], rhs=xdt[:, t % 2, d, h * HEADDIM:h * HEADDIM + YN],
                                                  start=d == 0, stop=d == 1)
                                last.then_inc(S["y"], 1)

                        for b in range(4):
                            project_block(lambda per, k: k, 0, b, False)
                        groups(pe, body)

                    @block.scalar
                    def _(act):
                        a = nc.scalar.activation
                        act.sem_inc(S["turned_out"], 2)

                        def copy_block(n, b, ahead):
                            k = b + 4 * ahead
                            act.wait_ge(blocks_used, n(4, first + k + 1))
                            act.wait_ge(S["conved"], n(4, k + 1))
                            u = upad[:, b % 2, :]
                            rows_a = HALF_TOK // GRID_W
                            for h, at_, dst in ((0, slice(0, HALF_TOK), grid(u)[:, 0:rows_a, :]),
                                                (1, slice(0, SAMPLE - HALF_TOK), grid(u)[:, rows_a:8, :])):
                                a(dst, ps[h][:, at_].rearrange("p (r w) -> p r w", w=GRID_W), ACT.Copy)
                            a(row_p(u), ps[1][:, SAMPLE - HALF_TOK:HALF_TOK], ACT.Copy).then_inc(S["copied"], 1)

                        def silu_block(n, j, b, ahead, ch):
                            act.wait_ge(S["conved"], n(4, b + 4 * ahead + 3))
                            bias = cols[:, bass.ds(ch + COL_AT["ssd_conv_b"][0], 1)]
                            v = conv[:, b % 2, :]
                            dst = xch[:, b, :] if b < 2 else bc[:, j, b - 2, :]
                            a(dst[:, 0:SAMPLE].rearrange("p (r w) -> p r w", w=GRID_W), grid(v), ACT.Silu, bias=bias)
                            a(dst[:, SAMPLE:TOK], row_p(v), ACT.Silu, bias=bias).then_inc(S["silued"], 1)

                        def body(n, j, last_group):
                            def next_copy(b):
                                if not last_group:
                                    copy_block(n, b, 1)

                            def next_silu(b):
                                if not last_group:
                                    silu_block(n, 1 - j, b, 1, channel_block(n, b, 1))

                            act.wait_ge(S["y_used"], n(TILES, 1))
                            for t in range(TILES):
                                act.wait_ge(S["turned"], n(TILES, t + 1))
                                a(tokm[:, t, :], turn_bank[t % 2][:, 0:3 * P], ACT.Copy).then_inc(S["turned_out"], 1)
                            silu_block(n, j, 3, 0, channel_block(n, 3, 0))
                            for b in range(2):
                                next_copy(b)
                                next_silu(b)

                            def exp(t):
                                act.wait_ge(S["seg"], n(TILES, t + 2))
                                act.wait_ge(S["mixed"], n(TILES, t + 1))
                                a(E[:, :, :].rearrange("p h l -> p (h l)"), p_seg[:, :], ACT.Exp).then_inc(S["exped"], 1)

                            exp(0)
                            next_copy(2)
                            exp(1)
                            next_silu(2)
                            exp(2)
                            next_copy(3)
                            exp(3)
                            exp(4)

                        for b in range(4):
                            copy_block(lambda per, k: k, b, 0)
                            if b < 3:
                                silu_block(lambda per, k: k, 0, b, 0, channel_block(lambda per, k: k, b, 0))
                        groups(act, body)

                    @block.vector
                    def _(dve):
                        v = nc.vector
                        D = dve_steps
                        heads = lambda ap: ap.rearrange("p (h q) -> p h q", h=HPG)
                        D.did(v.memset(upad[:, :, :], 0.0))
                        D.did(v.memset(xdt[:, :, :, :], 0.0))
                        D.settle(dve)
                        for name, k in (("conved", 2), ("st_used", 4), ("cb_used", 1), ("mixed", 1), ("y_used", 1)):
                            dve.sem_inc(S[name], k)

                        def conv_block(n, b, ahead):
                            k = b + 4 * ahead
                            dve.wait_ge(S["copied"], n(4, k + 2))
                            if k >= 2:
                                dve.wait_ge(S["silued"], n(4, k - 1))
                            ch = channel_block(n, b, ahead)
                            w = lambda m: cols[:, bass.ds(ch * 3 + (COL_AT["ssd_conv_w"][0] + m), 1)]
                            conv3(dve, conv[:, b % 2, :], upad[:, b % 2, :], w)
                            dve.sem_inc(S["conved"], 1)

                        def body(n, j, last_group):
                            hd = lambda ap3, t, at_: bcast(ap3[:, t, bass.ds(n(HPG, at_), HPG)], 2, HEADDIM)

                            def next_block(b):
                                if not last_group:
                                    conv_block(n, b, 1)

                            def weigh(k):
                                t, d = OWN[k]
                                dve.wait_ge(S["turned_out"], n(TILES, t + 3))
                                v.tensor_tensor(heads(xw[:, k % 4, :]), heads(tokm[:, t, 0:GW]),
                                                hd(state_w, t, d * HEADS), ALU.mult).then_inc(S["weighted"], 1)

                            def carry(k):
                                t, d = OWN[k]
                                own = st_bank[k % 4][:, 0:GW]
                                dve.wait_ge(S["st"], n(NST, k + 1))
                                if t == SAMPLE_TILES:
                                    if d == 0:
                                        dve.wait_ge(S["last_free"], n(1, 1))
                                    D.did(v.tensor_copy(last_s[:, d, :], own))
                                    D.settle(dve)
                                    dve.sem_inc(S["st_used"], 1)
                                    return
                                src, dst = (SF[:, t, :], SF[:, t + 1, :]) if d == 0 else (SB[:, t, :], SB[:, t - 1, :])
                                D.did(v.tensor_tensor(heads(dst), heads(src), hd(decay, t, ALL_B if d else ALL_F), ALU.mult))
                                D.settle(dve)
                                D.did(v.tensor_tensor(dst, dst, own, ALU.add))
                                D.settle(dve)
                                dve.sem_inc(S["st_used"], 1)

                            conv_block(n, 3, 0)
                            for k in range(4):
                                weigh(k)
                            dve.wait_ge(S["init_in"], n(32, 32))
                            for k in range(4):
                                carry(k)
                            for k in range(4, NST):
                                weigh(k)
                            next_block(0)
                            for k in range(4, NST):
                                carry(k)
                            dve.sem_inc(S["states"], 1)
                            dve.sem_inc(S["final"], 1)
                            next_block(1)

                            def weights(t):
                                for d in range(2):
                                    D.did(v.tensor_tensor(heads(xdt[:, t % 2, d, 0:GW]), heads(tokm[:, t, 0:GW]),
                                                          hd(dt, t, d * HEADS), ALU.mult))
                                dve.wait_ge(S["cb"], n(TILES, t + 1))
                                dve.wait_ge(S["mixed"], n(TILES, t + 1))
                                D.did(v.tensor_tensor(CBm[:, 0, :], p_cb[:, 0:P], masks[:, LE, :], ALU.mult))
                                D.did(v.tensor_tensor(CBm[:, 1, :], p_cb[:, 0:P], masks[:, GE, :], ALU.mult))
                                D.settle(dve)
                                dve.sem_inc(S["cb_used"], 1)
                                dve.wait_ge(S["exped"], n(TILES, t + 2))
                                for d in range(2):
                                    last = v.tensor_tensor(mix[:, t % 2, d, :, :], E[:, :, :], bcast(CBm[:, d, :], 1, HPG),
                                                           ALU.mult)
                                last.then_inc(S["mixed"], 1)

                            weights(0)
                            for t in range(TILES):
                                if t + 1 < TILES:
                                    weights(t + 1)
                                if t == 0:
                                    next_block(2)
                                dve.wait_ge(S["y_used"], n(TILES, t + 1))
                                D.did(v.tensor_tensor(heads(xD[:, :]), heads(tokm[:, t, 0:GW]),
                                                      bcast(rows[:, bass.ds(n(HPG, ROW_AT["d"][0]), HPG)], 2, HEADDIM), ALU.mult))
                                y_out_t = Y[:, t, bass.ds(n(GW, 0), GW)]
                                if t < SAMPLE_TILES:
                                    dve.wait_ge(S["off"], n(SAMPLE_TILES, t + 1))
                                    D.did(v.tensor_tensor(heads(off[:, 0, :]), heads(p_off[:, 0:GW]), hd(decay, t, IN_F), ALU.mult))
                                    D.did(v.tensor_tensor(heads(off[:, 1, :]), heads(p_off[:, GW:2 * GW]), hd(decay, t, IN_B), ALU.mult))
                                    D.settle(dve)
                                    D.did(v.tensor_tensor(off[:, 0, :], off[:, 0, :], off[:, 1, :], ALU.add))
                                    D.settle(dve)
                                    D.did(v.tensor_tensor(xD[:, :], xD[:, :], off[:, 0, :], ALU.add))
                                dve.wait_ge(S["y"], n(TILES, t + 1))
                                D.settle(dve)
                                v.tensor_tensor(y_out_t, p_y[:, 0:GW], xD[:, :], ALU.add).then_inc(S["y_used"], 1)

                        CONV = 4 * 3
                        GROUP = 6 * 2 + 2 + TILES * 5 + SAMPLE_TILES * 4
                        for b in range(3):
                            conv_block(lambda per, k: k, b, 0)
                        with D.loop(dve, GROUPS_ // 2 - 1, 2 * (GROUP + CONV)) as r:
                            for j in range(2):
                                body(lambda per, k, j=j: r * (2 * per) + (j * per + k), j, False)
                        for j in range(2):
                            body(lambda per, k, j=j: (GROUPS_ - 2 + j) * per + k, j, j == 1)

        def gate_by_z(Y, hT):
            first = take(N_Z)
            with ExitStack() as ph:
                h2 = sb("h_z", [P, NCH, 2, TOK], F32R, into=ph)
                split_into(h2, hT, NCH)
                wide = sb("wide_z", [P, 2, 2, 1024], F32R, into=ph)
                zs = sb("zs", [P, 2, 512], into=ph)
                ps = [pb(f"pz{t}", into=ph) for t in range(TILES)]
                his_done, wide_used, z_done, z_out, gated = (
                    sem("z_" + n) for n in ("his_done", "wide_used", "done", "out", "gated"))
                with nc.Block() as block:
                    @block.sync
                    def _(sp):
                        feed(sp, first, N_Z)

                    @block.tensor
                    def _(pe):
                        pe.sem_inc(z_out, TILES)
                        with pe.Fori(0, N_Z // SLOTS) as r:
                            for s in range(SLOTS):
                                j, begin, end = s // 4, s % 4 == 0, s % 4 == 3
                                pe.wait_ge(blocks_used, r * SLOTS + (first + s + 1))
                                for c in (0, 1):
                                    for t in range(TILES):
                                        if begin and c == 0:
                                            pe.wait_ge(z_out, r * (2 * TILES) + (j * TILES + t + 1))
                                        for h_part, w_part in ((0, 0), (1, 0), (0, 1)):
                                            last = nc.tensor.matmul(
                                                ps[t][:, :], lhsT=h2[:, (s % 4) * 2 + c, h_part, t * P:(t + 1) * P],
                                                rhs=wide[:, s % 2, w_part, c * 512:(c + 1) * 512],
                                                start=begin and c == 0 and h_part + w_part == 0,
                                                stop=end and c == 1 and w_part == 1)
                                        if end and c == 1:
                                            last.then_inc(z_done, 1)
                                if end:
                                    pe.wait_ge(z_done, r * (2 * TILES) + ((j + 1) * TILES))
                                    pe.sem_inc(wide_used, 1)
                                else:
                                    last.then_inc(wide_used, 1)

                    @block.scalar
                    def _(act):
                        act.sem_inc(wide_used, 2)

                        def hi(r, s):
                            act.wait_ge(half_loaded[s // HALF_RING], (r + (first // SLOTS + 1)) * 16)
                            act.wait_ge(wide_used, r * SLOTS + (s + 1))
                            nc.scalar.activation(wide[:, s % 2, 0, :], ring[:, s, :], ACT.Copy).then_inc(his_done, 1)

                        def silus(r, j):
                            for t in range(TILES):
                                k = j * TILES + t
                                act.wait_ge(z_done, r * (2 * TILES) + (k + 1))
                                act.wait_ge(gated, r * (2 * TILES) + (k + 1))
                                nc.scalar.activation(zs[:, k % 2, :], ps[t][:, :], ACT.Silu).then_inc(z_out, 1)

                        def round_(r, last):
                            for j in range(2):
                                for s in ((2, 3, 4), (5, 6, 7))[j]:
                                    hi(r, s)
                                silus(r, j)
                            if not last:
                                for s in range(2):
                                    hi(r + 1, s)

                        for s in range(2):
                            hi(0, s)
                        with act.Fori(0, N_Z // SLOTS - 1) as r:
                            round_(r, False)
                        round_(N_Z // SLOTS - 1, True)

                    @block.gpsimd
                    def _(pool):
                        with pool.Fori(0, N_Z // SLOTS) as r:
                            for s in range(SLOTS):
                                pool.wait_ge(his_done, r * SLOTS + (s + 1))
                                nc.gpsimd.tensor_tensor(wide[:, s % 2, 1, :], ring[:, s, :], wide[:, s % 2, 0, :].bitcast(F32),
                                                        ALU.subtract).then_inc(blocks_used, 1)

                    @block.vector
                    def _(dve):
                        dve.sem_inc(gated, 2)
                        with dve.Fori(0, 2) as r:
                            for k in range(2 * TILES):
                                dve.wait_ge(z_out, r * (2 * TILES) + (k + 1 + TILES))
                                y = Y[:, k % TILES, bass.ds(r * 1024 + (k // TILES) * 512, 512)]
                                nc.vector.tensor_tensor(y, y, zs[:, k % 2, :], ALU.mult).then_inc(gated, 1)

        def norm_y(Y, yT):
            with ExitStack() as ph:
                junk = sb("junk", [P, SSM_INNER], into=ph)
                ss = sb("ss", [P, TILES], into=ph)
                ps = [pb(f"pyt{j}", into=ph) for j in range(2)]
                summed, rooted, scaled, turned, out = (sem(n) for n in ("y_summed", "y_rooted", "y_scaled", "y_turned", "y_out"))
                with nc.Block() as block:
                    @block.vector
                    def _(dve):
                        v = nc.vector
                        for t in range(TILES):
                            dve_steps.did(v.tensor_tensor_reduce(out=junk[:, :], in0=Y[:, t, :], in1=Y[:, t, :], scale=1.0,
                                                                 scalar=0.0, op0=ALU.mult, op1=ALU.add,
                                                                 accum_out=ss[:, t:t + 1]))
                            dve_steps.settle(dve)
                        dve.sem_inc(summed, 1)
                        dve.wait_ge(rooted, 1)
                        dve_steps.did(v.reciprocal(ss[:, :], ss[:, :]))
                        dve_steps.settle(dve)
                        for t in range(TILES):
                            v.tensor_scalar(Y[:, t, :], Y[:, t, :], ss[:, t:t + 1], None, ALU.mult).then_inc(scaled, 1)
                            for b in range(4):
                                k = 4 * t + b
                                dve.wait_ge(turned, k + 1)
                                v.tensor_tensor(yT[:, 4 * b:4 * b + 4, t * P:(t + 1) * P],
                                                ps[k % 2][:, :].rearrange("p (b t) -> p b t", b=4),
                                                bcast(col("ssd_norm_w", 4 * b, 4 * b + 4), 2, P), ALU.mult).then_inc(out, 1)

                    @block.scalar
                    def _(act):
                        act.wait_ge(summed, 1)
                        nc.scalar.activation(ss[:, :], ss[:, :], ACT.Sqrt, bias=eps[:, :], scale=1.0 / SSM_INNER).then_inc(rooted, 1)

                    @block.tensor
                    def _(pe):
                        for t in range(TILES):
                            pe.wait_ge(scaled, t + 1)
                            for b in range(4):
                                k = 4 * t + b
                                if k >= 2:
                                    pe.wait_ge(out, k - 1)
                                for q in range(4):
                                    last = nc.tensor.transpose(ps[k % 2][:, q * P:(q + 1) * P],
                                                               Y[:, t, (4 * b + q) * P:(4 * b + q + 1) * P], masks[:, IDENT, :])
                                last.then_inc(turned, 1)

        def scale_of(t):
            return lambda c, k: t[:, c, k:k + 1]

        def shift_of(comp):
            return lambda c, k: mods[:, comp * NCH + c, k:k + 1]

        stages = []
        for layer in range(DEPTH):
            stages += [
                lambda layer=layer: adaln(layer),
                ssd_mixer if layer % 2 else even_mixer,
                lambda layer=layer: peer(layer),
            ]
        for stage in stages:
            stage()
        yT_out = sb("yT_out", [P, NCH, TOK])
        norm_modulate("last", yT_out, lambda c, k: col("norm_final", c, c + 1), None)
        stored = sem("stored")
        with nc.Block() as block:
            @block.sync
            def _(sp):
                sp.dma_start(y_out, yT_out[:, :, :]).then_inc(stored, 16)
                sp.wait_ge(stored, 16)


def kernel(**inputs):
    import numpy as np
    import concourse.bacc as bacc
    from concourse.bass_utils import run_bass_kernel_spmd

    a = {k: np.asarray(v) for k, v in inputs.items()}

    def chunks(v):
        return v.reshape(-1, P).T

    def out_blocks(w):
        k, n = w.shape
        return w.reshape(k // P, P, n // P, P).transpose(2, 1, 0, 3).reshape(n // P, P, k)

    w_ssd = a["ssd_w_in"][0]
    w_z, w_xbc, w_dt = w_ssd[:, :SSM_INNER], w_ssd[:, SSM_INNER:SSM_INNER + 4096], w_ssd[:, SSM_INNER + 4096:]
    xbc = out_blocks(w_xbc)
    order = [b for g in range(SSM_GROUPS) for b in (2 * g, 2 * g + 1, 16 + g, 24 + g)]
    z = w_z.reshape(4, 2, P, 4, 512).transpose(3, 0, 2, 1, 4).reshape(16, P, 1024)
    ssd_out = a["ssd_w_out"][0].reshape(2, NCH, P, NCH, P).transpose(3, 0, 2, 1, 4).reshape(16, P, 1024)

    def experts_of(layer):
        G, B = EXPERT_BLOCKS // BLOCKS_PER_GROUP, BLOCKS_PER_GROUP
        u = a["peer_u"][layer].reshape(G, B, KEYS, NCH, P).transpose(0, 1, 4, 3, 2).reshape(G, B, P, 1024)
        v = a["peer_v"][layer].reshape(G, B, P, 1024)
        E = EARLY // B
        return np.concatenate([u[:E].reshape(EARLY, P, 1024), v[:E].reshape(EARLY, P, 1024),
                               np.concatenate([u[E:], v[E:]], axis=1).reshape(N_LATE, P, 1024)])

    stream = np.concatenate([
        out_blocks(a["adaln_w"][0]), out_blocks(a["even_w_in"][0]), out_blocks(a["even_w_out"][0]),
        out_blocks(a["peer_w_q"][0]), experts_of(0),
        out_blocks(a["adaln_w"][1]), xbc[order], z, ssd_out, out_blocks(a["peer_w_q"][1]), experts_of(1)])
    keys = a["peer_keys"].transpose(0, 4, 1, 2, 3).reshape(DEPTH, P, 2 * PEER_HEADS * KEYS)
    wdt = w_dt.reshape(NCH, P, 64).transpose(1, 0, 2)
    xin = np.concatenate([a["x_sample"][0], a["x_prompt"][0]]).T.reshape(NCH, P, TOK).transpose(1, 0, 2)
    cond = np.stack([a["c"][0], a["c_ctx"]], axis=1).reshape(NCH, P, 2).transpose(1, 0, 2).reshape(P, 2 * NCH)
    cols = np.concatenate([
        cond, chunks(a["adaln_b"].reshape(-1)), chunks(a["norm_mix"].reshape(-1)), chunks(a["norm_ffn"].reshape(-1)),
        chunks(a["norm_final"]), a["even_conv_w"][0].reshape(3, 4, P).transpose(2, 1, 0).reshape(P, 12),
        a["ssd_conv_w"][0].reshape(3, 32, P).transpose(2, 1, 0).reshape(P, 96), chunks(a["ssd_conv_b"][0]),
        chunks(a["ssd_norm_w"][0])], axis=1)
    f32 = np.float32
    rows = np.concatenate([
        a["ssd_dt_bias"][0].reshape(-1), a["ssd_a_log"][0].reshape(-1), a["ssd_d"][0], np.arange(P, dtype=f32),
        np.arange(TOPK, dtype=f32), np.array(PAIR_AT, f32), np.array([0] + PAIRS_OF[:-1], f32)])
    rows = np.broadcast_to(rows[None, :], (P, NROWS))
    k, l = np.arange(P)[:, None], np.arange(P)[None, :]
    masks = np.stack([k <= l, k < l, k >= l, k > l, k >= 0 * l, k == l], axis=1).astype(f32)

    def angles(n):
        return 2 * np.pi * (np.outer(np.arange(n), np.arange(n)) % n) / n

    at, ac = angles(SAMPLE), angles(P)
    scale_s, scale_p = (SAMPLE * P) ** -0.5, 1.0 / P
    tiles = lambda m: m.reshape(SAMPLE_TILES, P, SAMPLE).transpose(1, 0, 2).reshape(P, -1)
    dft = np.concatenate([tiles(np.cos(at) * scale_s), tiles(-np.sin(at) * scale_s), np.cos(ac), np.sin(ac),
                          np.cos(ac) * scale_p, -np.sin(ac) * scale_p], axis=1).astype(f32)

    def states(s):
        return s[0, 0].reshape(SSM_GROUPS, GW, P).transpose(0, 2, 1)

    state_in = np.stack([states(a["state_ssd_fwd"]), states(a["state_ssd_bwd"])], axis=2)

    nc = bacc.Bacc("TRN2", target_bir_lowering=False, num_devices=1)
    arrays = dict(stream=stream, keys=keys, wdt=wdt, xin=xin, cols=cols, rows=rows, masks=masks, dft=dft,
                  state_in=state_in)
    arrays = {n: np.ascontiguousarray(v) for n, v in arrays.items()}
    aps = [nc.dram_tensor(f"in_{n}", v.shape, F32, kind="ExternalInput").ap() for n, v in arrays.items()]
    y = nc.dram_tensor("y", (P, NCH, TOK), F32, kind="ExternalOutput").ap()
    state_out = nc.dram_tensor("state_out", (SSM_GROUPS, P, 2, GW), F32, kind="ExternalOutput").ap()
    gates = nc.dram_tensor("gates", (TOK // SCATTER_TOK, P, KEYS, SCATTER_TOK), F32, kind="Internal").ap()
    hidden = nc.dram_tensor("hidden", (EARLY, P, TOK), F32, kind="Internal").ap()
    hybrid_trunk(nc, *aps, y, state_out, gates, hidden)
    r = run_bass_kernel_spmd(nc, [{f"in_{n}": v for n, v in arrays.items()}], core_ids=[0]).results[0]
    y = r["y"].transpose(1, 0, 2).reshape(D_MODEL, TOK).T
    st = r["state_out"].transpose(2, 0, 3, 1).reshape(2, 1, 1, HEADS, HEADDIM, P)
    return (np.ascontiguousarray(y[None, SAMPLE:]), np.ascontiguousarray(y[None, :SAMPLE]),
            np.ascontiguousarray(st[0]), np.ascontiguousarray(st[1]))
```
